# Optimizing a Trainium2 kernel written in Bass

```python
import math
import jax, jax.numpy as jnp
from jax import lax
import numpy as np

D_MODEL = 1024
BATCH = 1
SEQ = 1024
DEPTH = 1
DEC_BATCH = 1
DEC_SEQ = 512
PAST_LEN = 128

HEAD_DIM = 64
HEADS_PER_GROUP = 4
GROUPS = ((128, 1), (512, 4), (2048, 16))
N_GROUPS = len(GROUPS)
N_ATT_HEADS = N_GROUPS * HEADS_PER_GROUP
ATT_W = N_ATT_HEADS * HEAD_DIM
ATT_OUT = HEADS_PER_GROUP * HEAD_DIM
F_GROUPS = 6
F_CH = 128
F_W = F_GROUPS * F_CH
IN_W = 3 * ATT_W + F_W
NUM_BUCKETS = 32
MAX_DISTANCE = 1024
N_EXPERTS = 16
CAPACITY_FACTOR = 2
D_FF = 2048
N_BRANCH = 2
EPS = 1e-6
NEG = -1e30

kernel_name = "hybrid_dilated_fnet_ec_encoder"

def rmsnorm(x, g):
    xf = x.astype(jnp.float32)
    y = xf * lax.rsqrt(jnp.mean(xf * xf, axis=-1, keepdims=True) + EPS) * g.astype(jnp.float32)
    return y.astype(x.dtype)

def t5_bucket(rel):
    nb = NUM_BUCKETS // 2
    max_exact = nb // 2
    ret = (rel > 0).astype(np.int32) * nb
    n = np.abs(rel)
    large = max_exact + (np.log(np.maximum(n, max_exact) / max_exact)
                         / np.log(MAX_DISTANCE / max_exact) * (nb - max_exact)).astype(np.int32)
    large = np.minimum(large, nb - 1)
    return (ret + np.where(n < max_exact, n, large)).astype(np.int32)

def dilated_group(q, k, v, bias_tab, dil, half_keys):
    B, S, H, Dh = q.shape
    blk = half_keys
    L = S // dil
    nb = -(-L // blk)
    Lp = nb * blk

    def to_blocks(t):
        t = t.reshape(B, L, dil, H, Dh)
        t = jnp.pad(t, ((0, 0), (0, Lp - L), (0, 0), (0, 0), (0, 0)))
        return t.reshape(B, nb, blk, dil, H, Dh)

    def windows(t):
        tp = jnp.pad(t, ((0, 0), (1, 1), (0, 0), (0, 0), (0, 0), (0, 0)))
        return jnp.concatenate([tp[:, :-2], tp[:, 1:-1], tp[:, 2:]], axis=2)

    qb = to_blocks(q * (1.0 / math.sqrt(Dh)))
    kw = windows(to_blocks(k))
    vw = windows(to_blocks(v))

    qi = np.arange(blk)[:, None]
    kj = np.arange(3 * blk)[None, :]
    delta = kj - blk - qi
    band = np.abs(delta) <= half_keys
    kglob = np.arange(nb)[:, None] * blk + np.arange(3 * blk)[None, :] - blk
    valid = (kglob >= 0) & (kglob < L)
    mask = band[None, :, :] & valid[:, None, :]
    bucket = t5_bucket(dil * delta)
    bias = jnp.transpose(bias_tab[bucket], (0, 2, 1)).astype(jnp.float32)

    s = jnp.einsum('bnqrhe,bnkrhe->bnqrhk', qb, kw, preferred_element_type=jnp.float32)
    s = s + bias[None, None, :, None, :, :]
    s = jnp.where(jnp.asarray(mask)[None, :, :, None, None, :], s, NEG)
    m = jnp.max(s, axis=-1, keepdims=True)
    p = jnp.exp(s - m)
    den = jnp.sum(p, axis=-1)
    o = jnp.einsum('bnqrhk,bnkrhe->bnqrhe', p, vw.astype(jnp.float32)) / den[..., None]
    lse = m[..., 0] + jnp.log(den)
    o = o.reshape(B, Lp, dil, H, Dh)[:, :L].reshape(B, S, H, Dh)
    lse = lse.reshape(B, Lp, dil, H)[:, :L].reshape(B, S, H)
    return o, lse

def fourier_mix(u):
    B, S, _ = u.shape
    uf = u.astype(jnp.float32).reshape(B, S, F_GROUPS, F_CH)
    y = jnp.fft.fftn(uf, axes=(1, 3), norm="ortho").real
    return y.reshape(B, S, F_W).astype(u.dtype)

def expert_choice(xn, w_router, w_eg, w_eu, w_ed):
    B, S, D = xn.shape
    T = B * S
    C = CAPACITY_FACTOR * T // N_EXPERTS
    xt = xn.reshape(T, D)
    aff = jax.nn.softmax((xt @ w_router).astype(jnp.float32), axis=-1)
    gate, idx = lax.top_k(aff.T, C)
    xe = xt[idx]
    h = jax.nn.silu(jnp.einsum('ecd,edf->ecf', xe, w_eg)) * jnp.einsum('ecd,edf->ecf', xe, w_eu)
    ye = jnp.einsum('ecf,efd->ecd', h, w_ed) * gate[..., None].astype(xn.dtype)
    out = jnp.zeros((T, D), xn.dtype).at[idx.reshape(-1)].add(ye.reshape(-1, D))
    return out.reshape(B, S, D)

def encoder(x, rel_bias, norm1_g, w_in, w_attn_br, w_four_br, w_gate, b_gate, w_out,
            norm2_g, w_router, w_exp_gate, w_exp_up, w_exp_down, final_g):
    B, S, D = x.shape
    for l in range(DEPTH):
        xn = rmsnorm(x, norm1_g[l])
        proj = xn @ w_in[l]
        q = proj[..., :ATT_W].reshape(B, S, N_GROUPS, HEADS_PER_GROUP, HEAD_DIM)
        k = proj[..., ATT_W:2 * ATT_W].reshape(B, S, N_GROUPS, HEADS_PER_GROUP, HEAD_DIM)
        v = proj[..., 2 * ATT_W:3 * ATT_W].reshape(B, S, N_GROUPS, HEADS_PER_GROUP, HEAD_DIM)
        u = proj[..., 3 * ATT_W:]

        outs, lses = [], []
        for g, (win, dil) in enumerate(GROUPS):
            o, lse = dilated_group(q[:, :, g], k[:, :, g], v[:, :, g],
                                   rel_bias[:, g * HEADS_PER_GROUP:(g + 1) * HEADS_PER_GROUP],
                                   dil, (win // 2) // dil)
            outs.append(o)
            lses.append(lse)
        wts = jax.nn.softmax(jnp.stack(lses, axis=0), axis=0)
        att = jnp.sum(wts[..., None] * jnp.stack(outs, axis=0), axis=0)
        att = att.reshape(B, S, ATT_OUT).astype(x.dtype)

        four = fourier_mix(u)

        gates = jax.nn.sigmoid((xn @ w_gate[l] + b_gate[l]).astype(jnp.float32))
        gates = gates.astype(x.dtype).reshape(B, S, N_BRANCH, D)
        mix = gates[:, :, 0] * (att @ w_attn_br[l]) + gates[:, :, 1] * (four @ w_four_br[l])
        x = x + mix @ w_out[l]

        x = x + expert_choice(rmsnorm(x, norm2_g[l]), w_router[l], w_exp_gate[l],
                              w_exp_up[l], w_exp_down[l])
    return rmsnorm(x, final_g)

def setup_inputs(seed: int = 0) -> dict:
    key = jax.random.key(seed)
    ks = jax.random.split(key, 16)
    f32 = jnp.float32

    def nrm(k, shape, scale):
        return jax.random.normal(k, shape, f32) * scale

    return {
        "x_prompt": nrm(ks[0], (BATCH, SEQ, D_MODEL), 1.0),
        "x_sample": nrm(ks[1], (DEC_BATCH, DEC_SEQ, D_MODEL), 1.0),
        "rel_bias": nrm(ks[2], (NUM_BUCKETS, N_ATT_HEADS), 0.5),
        "norm1_g": 1.0 + nrm(ks[3], (DEPTH, D_MODEL), 0.02),
        "w_in": nrm(ks[4], (DEPTH, D_MODEL, IN_W), D_MODEL ** -0.5),
        "w_attn_br": nrm(ks[5], (DEPTH, ATT_OUT, D_MODEL), ATT_OUT ** -0.5),
        "w_four_br": nrm(ks[6], (DEPTH, F_W, D_MODEL), F_W ** -0.5),
        "w_gate": nrm(ks[7], (DEPTH, D_MODEL, N_BRANCH * D_MODEL), D_MODEL ** -0.5),
        "b_gate": nrm(ks[8], (DEPTH, N_BRANCH * D_MODEL), 0.02),
        "w_out": nrm(ks[9], (DEPTH, D_MODEL, D_MODEL), D_MODEL ** -0.5),
        "norm2_g": 1.0 + nrm(ks[10], (DEPTH, D_MODEL), 0.02),
        "w_router": nrm(ks[11], (DEPTH, D_MODEL, N_EXPERTS), D_MODEL ** -0.5),
        "w_exp_gate": nrm(ks[12], (DEPTH, N_EXPERTS, D_MODEL, D_FF), D_MODEL ** -0.5),
        "w_exp_up": nrm(ks[13], (DEPTH, N_EXPERTS, D_MODEL, D_FF), D_MODEL ** -0.5),
        "w_exp_down": nrm(ks[14], (DEPTH, N_EXPERTS, D_FF, D_MODEL), D_FF ** -0.5),
        "final_g": 1.0 + nrm(ks[15], (D_MODEL,), 0.02),
    }

def reference(x_prompt, x_sample, rel_bias, norm1_g, w_in, w_attn_br, w_four_br, w_gate,
              b_gate, w_out, norm2_g, w_router, w_exp_gate, w_exp_up, w_exp_down, final_g):
    y_prompt = encoder(x_prompt, rel_bias, norm1_g, w_in, w_attn_br, w_four_br, w_gate, b_gate,
                       w_out, norm2_g, w_router, w_exp_gate, w_exp_up, w_exp_down, final_g)
    y_sample = encoder(x_sample, rel_bias, norm1_g, w_in, w_attn_br, w_four_br, w_gate, b_gate,
                       w_out, norm2_g, w_router, w_exp_gate, w_exp_up, w_exp_down, final_g)
    return (y_prompt, y_sample)


_drawn_inputs = setup_inputs


def setup_inputs(seed=0):
    import zlib

    import numpy as np

    out = dict(_drawn_inputs(seed))
    spreads = {}
    factors = {'norm1_g': 4.477, 'b_gate': 8.0, 'norm2_g': 3.521, 'final_g': 2.858}
    for name, (base, spread) in spreads.items():
        noise = np.random.default_rng([zlib.crc32(name.encode()), seed]).standard_normal(out[name].shape)
        drawn = base * np.exp(spread * noise) if base else spread * noise
        out[name] = __import__('jax').numpy.asarray(drawn.astype(out[name].dtype))
    for name, factor in factors.items():
        out[name] = (out[name] * factor).astype(out[name].dtype)
    return out
```

```python
from collections import namedtuple
from contextlib import ExitStack

import concourse.bass as bass
import numpy as np
from concourse import mybir

F32 = mybir.dt.float32
U32 = mybir.dt.uint32
ALU = mybir.AluOpType
ACT = mybir.ActivationFunctionType
AX = mybir.AxisListType

P = 128
D = 1024
KT = D // P
SEQS = ((0, 1024), (1024, 512))
TOKENS = 1536
NT = TOKENS // P
CH = 512
NCH = TOKENS // CH
HD = 64
HEADS = 4
GROUPS = ((128, 1), (512, 4), (2048, 16))
NG = len(GROUPS)
HALF = 64
GW = HEADS * HD
ATT_W = NG * GW
F_GROUPS = 6
F_W = F_GROUPS * P
BUCKETS = 32
MAX_DISTANCE = 1024
E = 16
CAPS = tuple(2 * n // E for _, n in SEQS)
CAP = sum(CAPS)
FF = 2048
FT = FF // P
EPS = 1e-6
NEG = -1e30
WB = 256
AROW = GW + 2 * HEADS
TOEP = 384
KB = 1024


TABLES = ((0, 1), (1, 1)) + tuple((2, P * GROUPS[2][1] // n) for _, n in SEQS)



def bucket_of(rel):
    nb = BUCKETS // 2
    exact = nb // 2
    n = np.abs(rel)
    large = exact + (np.log(np.maximum(n, exact) / exact) / np.log(MAX_DISTANCE / exact) * (nb - exact)).astype(np.int32)
    return (rel > 0).astype(np.int32) * nb + np.where(n < exact, n, np.minimum(large, nb - 1))


def bucket_one_hot():
    table = np.zeros((BUCKETS + 1, len(TABLES), TOEP), np.float32)
    place = np.arange(TOEP) - 191
    for i, (g, classes) in enumerate(TABLES):
        dil = GROUPS[g][1]
        seen = (place % classes == 0) & (np.abs(place) <= HALF * classes)
        row = np.where(seen, bucket_of(dil // classes * place), BUCKETS)
        table[row, i, np.arange(TOEP)] = 1.0
    return table.reshape(BUCKETS + 1, len(TABLES) * TOEP)


def position_table(n):
    t = np.concatenate([np.arange(0, n, 2), np.arange(1, n, 2)])
    angle = 2 * np.pi * ((t[:, None] * np.arange(n // 2)[None, :]) % n) / n
    both = np.stack([np.cos(angle), np.sin(angle)], 1) / np.sqrt(n * P)
    return both.astype(np.float32)


def channel_table():
    c = np.arange(P)
    angle = 2 * np.pi * ((c[:, None] * c[None, :]) % P) / P
    return np.stack([np.cos(angle), -np.sin(angle)], 1).astype(np.float32)



QueryTile = namedtuple("QueryTile", "s r classes q0 k0 keys bias")


def attention_plan(g):
    dil = GROUPS[g][1]
    tiles, values = [], []
    for s, (base, n) in enumerate(SEQS):
        length = n // dil
        if length > P:
            cuts = [0] + list(range(HALF, length, P)) + [length]
            for r in range(dil):
                first = len(values)
                for a, b in zip(cuts, cuts[1:]):
                    values.append((s, r, 1, a, b - a))
                for i in range(length // P):
                    keys = [(first + i + c, cuts[i + c + 1] - cuts[i + c]) for c in range(2)]
                    tiles.append(QueryTile(s=s, r=r, classes=1, q0=i * P, k0=cuts[i], keys=keys,
                                                 bias=cuts[i] - i * P + HALF))
        else:
            classes = P // length
            for r in range(dil // classes):
                values.append((s, r, classes, 0, P))
                tiles.append(QueryTile(s=s, r=r, classes=classes, q0=0, k0=0, keys=[(len(values) - 1, P)], bias=HALF))
    return tiles, values


PLANS = [attention_plan(g) for g in range(NG)]
MAXV = max(len(v) for _, v in PLANS)


def of_class(view, s, g, r, classes, a, n):
    base, size = SEQS[s]
    return view[:, base:base + size].rearrange("p (n r) -> p r n", r=GROUPS[g][1] // classes)[:, r, a:a + n]


def encoder(nc, x, rel_bias, norm1_g, w_in, w_attn_br, w_four_br, w_gate, b_gate, w_out, norm2_g,
            w_router, w_eg, w_eu, w_ed, final_g, identity, one_hot, pos_prompt, pos_sample, chan, y):
    ctx = ExitStack()
    with ctx:
        ARENA = 17 * KB

        def at(name, kb, shape, dt=F32):
            return nc.alloc_sbuf_tensor_at(name, list(shape), dt, offset=int(ARENA + kb * KB))

        def sem(name):
            return ctx.enter_context(nc.semaphore(name))

        def sems(name, n):
            return [sem(f"{name}{i}") for i in range(n)]

        xnT = at("xnT", 0, [P, KT, TOKENS])
        attT = at("attT", 48, [P, GW // P, TOKENS])
        fourT = at("fourT", 60, [P, F_GROUPS, TOKENS])
        wblk = at("wblk", 96, [P, 4, KT, WB])
        xin = at("xin", 128, [P, 4, D])
        xs = at("xs", 144, [P, 2, D])
        g1 = at("g1", 152, [P, D])
        junk = at("junk", 156, [P, D])
        hot = at("hot", 160, [BUCKETS + 1, len(TABLES) * TOEP])
        relx = at("relx", 167, [BUCKETS + 1, len(TABLES) * HEADS, P])
        toep_sb = at("toep_sb", 176, [P, len(TABLES) * HEADS, TOEP])
        qT = at("qT", 128, [P, 2, TOKENS])
        kT = at("kT", 140, [P, 2, TOKENS])
        V = at("V", 152, [P, MAXV, GW])
        band = at("band", 168, [P, 2 * HEADS, 2 * P])
        same = at("same", 176, [P, 2, HEADS, P])
        sc = at("sc", 180, [P, 2, HEADS, 2 * P])
        pT = at("pT", 188, [P, 2, HEADS, 2, P])
        orow = at("orow", 196, [P, 3, AROW])
        u = at("u", 128, [P, NT, WB])
        tabP = at("tabP", 140, [P, 8, 2, 512])
        tabS = at("tabS", 172, [P, 4, 2, 256])
        eo = at("eo", 180, [P, 4, 512])
        fe = at("fe", 188, [P, 2, 512])
        comb = at("comb", 192, [P, 2, NG, AROW])
        attk = at("attk", 198.25, [P, 2, GW])
        cw = at("cw", 200.25, [P, 64])
        chan_sb = at("chan_sb", 200.5, [P, 2, P])
        mixT = at("mixT", 128, [P, KT, TOKENS])
        sig = at("sig", 176, [P, 2, 2, CH])
        gated = at("gated", 184, [P, 2, 2, CH])
        xres = at("xres", 48, [P, 2, D])
        xn2 = at("xn2", 56, [P, 2, D])
        xn2T = at("xn2T", 64, [P, 2, KT, P])
        g2 = at("g2", 72, [P, D])
        aff = [at("affP", 76, [E, 1024]), at("affS", 80, [E, 512])]
        junk2 = at("junk2", 84, [P, D])
        vals = [at("valsP", 88, [E, CAPS[0]]), at("valsS", 88.5, [E, CAPS[1]])]
        idxr = [at("idxrP", 89, [E, CAPS[0]], U32), at("idxrS", 89.5, [E, CAPS[1]], U32)]
        idxf = [at("idxfP", 90, [E, CAPS[0]]), at("idxfS", 90.5, [E, CAPS[1]])]
        atok = at("atok", 91, [P, 2, E])
        ring = at("ring", 0, [P, 6, 16, WB])
        xg = [at("xgP", 96, [CAPS[0], D]), at("xgS", 100, [CAPS[1], D])]
        xeT = at("xeT", 104, [P, KT, CAP])
        hT = at("hT", 110, [P, FT, CAP])
        ytok = [at("ytokP", 122, [CAPS[0], D]), at("ytokS", 126, [CAPS[1], D])]
        yT = at("yT", 130, [P, 2, CAP])
        sg = at("sg", 132, [P, 4, CAP])
        sgg = at("sgg", 135, [P, 4, CAP])
        fin = at("fin", 128, [P, 4, D])
        fout = at("fout", 144, [P, 4, D])
        gF = at("gF", 160, [P, D])
        ident = at("ident", 202, [P, P])
        bg = at("bg", 202.5, [P, 2 * KT])
        relb = at("relb", 202.75, [BUCKETS + 1, NG * HEADS])
        wr = at("wr", 203, [P, KT, E])
        stat = at("stat", 203.5, [P, 64])
        negm = at("negm", 203.75, [P, 2, HEADS])
        gate = [at("gateP", 204, [CAPS[0], E]), at("gateS", 204.125, [CAPS[1], E])]
        idx = [at("idxP", 204.25, [CAPS[0], E], U32), at("idxS", 204.375, [CAPS[1], E], U32)]
        idx_in = [at("idx_inP", 204.5, [CAPS[0], 1], U32), at("idx_inS", 204.53125, [CAPS[1], 1], U32)]
        idx_out = [at("idx_outP", 204.5625, [CAPS[0], 1], U32), at("idx_outS", 204.59375, [CAPS[1], 1], U32)]

        ps = ctx.enter_context(nc.psum_tensor("ps", [P, 8, 512], F32))

        toep = nc.dram_tensor("toep", [P, len(TABLES) * HEADS, TOEP], F32, kind="Internal").ap()
        attrows = nc.dram_tensor("attrows", [NG, TOKENS, AROW], F32, kind="Internal").ap()
        resid = nc.dram_tensor("resid", [TOKENS, D], F32, kind="Internal").ap()
        normed = nc.dram_tensor("normed", [TOKENS, D], F32, kind="Internal").ap()

        w_loaded = sems("w_loaded", 4)
        G0, R0 = 12, 24

        def in_block(n):
            return (n % 3) * ATT_W + (n // 3) * WB if n < 9 else 3 * ATT_W + (n - 9) * WB

        def load_in_block(sp, n):
            c = in_block(n)
            sp.dma_start(wblk[:, n % 3, :, :], w_in[0, :, c:c + WB].rearrange("(k p) n -> p k n", p=P)) \
              .then_inc(w_loaded[n % 3], 16)

        def gate_cols(w, first, j):
            return w[0, :, bass.ds(j * WB + first, WB)].rearrange("(k p) n -> p k n", p=P)

        def load_gate_block(sp, b, j):
            if b < 2:
                sp.dma_start(wblk[:, b, :, :], gate_cols(w_gate, b * D, j)).then_inc(w_loaded[b], 16)
            else:
                sp.dma_start(wblk[:, 2, 0:2, :], gate_cols(w_attn_br, 0, j)).then_inc(w_loaded[2], 16)
                sp.dma_start(wblk[:, 2, 2:8, :], gate_cols(w_four_br, 0, j)).then_inc(w_loaded[2], 16)

        def gate_block_at(b, j):
            return (j + 1) * 16 + 64 if b < 2 else (j + 1) * 32 + 64

        c_loaded, x_in_ld = sem("c_loaded"), sems("x_in_ld", 4)
        n_ssq, n_var, n_std, n_rstd, n_xs = (sem(n) for n in ("n_ssq", "n_var", "n_std", "n_rstd", "n_xs"))
        n_T, n_evA, n_evD = sem("n_T"), sem("n_evA"), sem("n_evD")
        t_masked, t_mm, t_sb, t_sbD, t_out, t_tab, t_rel = (sem(n) for n in ("t_masked", "t_mm", "t_sb", "t_sbD", "t_out", "t_tab", "t_rel"))
        CONSTS = 6

        with nc.Block() as block:
            @block.sync
            def _(sp):
                sp.dma_start(ident[:, :], identity).then_inc(c_loaded, 16)
                sp.dma_start(g1[:, :], norm1_g.partition_broadcast(P)).then_inc(c_loaded, 16)
                for s in range(4):
                    sp.dma_start(xin[:, s, :], x[s * P:(s + 1) * P, :]).then_inc(x_in_ld[s], 16)
                sp.dma_start(hot[:, :], one_hot).then_inc(c_loaded, 16)
                sp.dma_start(relb[0:BUCKETS, :], rel_bias).then_inc(c_loaded, 16)
                sp.dma_start(bg[:, :], b_gate).then_inc(c_loaded, 16)
                sp.dma_start(wr[:, :, :], w_router[0].rearrange("(k p) e -> p k e", p=P)).then_inc(c_loaded, 16)
                for n in range(3):
                    load_in_block(sp, n)
                with sp.Fori(1, NT // 4) as i:
                    for s in range(4):
                        sp.wait_ge(n_xs, i * 4 + (s - 3))
                        sp.dma_start(xin[:, s, :], x[bass.ds(i * 4 * P + s * P, P), :]).then_inc(x_in_ld[s], 16)
                sp.wait_ge(t_sb, len(TABLES) * HEADS // 2)
                sp.wait_ge(t_sbD, len(TABLES) * HEADS // 2)
                sp.dma_start(toep, toep_sb[:, :, :]).then_inc(t_out, 16)

            @block.gpsimd
            def _(pool):
                pool.memset(relb[BUCKETS:BUCKETS + 1, :], NEG).then_inc(t_masked, 1)

            @block.scalar
            def _(act):
                def square(i, s):
                    act.wait_ge(x_in_ld[s], (i + 1) * 16)
                    if s or not isinstance(i, int) or i:
                        act.wait_ge(n_ssq, i * 4 + s)
                    act.activation(junk[:, :], xin[:, s, :], ACT.Square, accum_out=stat[:, s:s + 1]).then_inc(n_ssq, 1)

                def root(i, s):
                    act.wait_ge(n_var, i * 4 + s + 1)
                    act.activation(stat[:, 8 + s:9 + s], stat[:, 4 + s:5 + s], ACT.Sqrt).then_inc(n_std, 1)

                def evict(i, s):
                    act.wait_ge(n_T, (i * 4 + s) * 2 + 1)
                    act.activation(xnT[:, 0:4, bass.ds((i * 4 + s) * P, P)], ps[:, 2 * (s % 2), :].rearrange("p (k t) -> p k t", k=4),
                                   ACT.Copy).then_inc(n_evA, 1)

                def body(i):
                    for s in range(4):
                        square(i, s)
                        root(i, s)
                        evict(i, s)
                body(0)
                with act.Fori(1, NT // 4) as i:
                    body(i)
                for r in range(0, len(TABLES) * HEADS, 2):
                    act.wait_ge(t_mm, r + 1)
                    act.activation(toep_sb[:, r, :], ps[:, 4 + r % 4, 0:TOEP], ACT.Copy).then_inc(t_sb, 1)

            @block.vector
            def _(dve):
                dve.wait_ge(c_loaded, 16 * CONSTS)

                def body(i):
                    for s in range(4):
                        n = i * 4 + s
                        dve.wait_ge(n_ssq, n + 1)
                        dve.tensor_scalar(stat[:, 4 + s:5 + s], stat[:, s:s + 1], 1.0 / D, EPS, ALU.mult, ALU.add).then_inc(n_var, 1)
                        dve.wait_ge(n_std, n + 1)
                        dve.reciprocal(stat[:, 12 + s:13 + s], stat[:, 8 + s:9 + s]).then_inc(n_rstd, 1)
                        dve.wait_ge(n_rstd, n + 1)
                        if s >= 2 or not isinstance(i, int) or i:
                            dve.wait_ge(n_T, (n - 1) * 2)
                        dve.scalar_tensor_tensor(out=xs[:, s % 2, :], in0=xin[:, s, :], scalar=stat[:, 12 + s:13 + s],
                                                 in1=g1[:, :], op0=ALU.mult, op1=ALU.mult).then_inc(n_xs, 1)
                        dve.wait_ge(n_T, n * 2 + 2)
                        dve.tensor_copy(xnT[:, 4:8, bass.ds(n * P, P)],
                                        ps[:, 2 * (s % 2) + 1, :].rearrange("p (k t) -> p k t", k=4)).then_inc(n_evD, 1)
                body(0)
                with dve.Fori(1, NT // 4) as i:
                    body(i)
                dve.wait_ge(t_masked, 1)
                for i, (g, _) in enumerate(TABLES):
                    dve.tensor_copy(relx[:, i * HEADS:(i + 1) * HEADS, :],
                                    relb[:, g * HEADS:(g + 1) * HEADS].rearrange("b (h o) -> b h o", o=1)
                                    .broadcast_to([BUCKETS + 1, HEADS, P])).then_inc(t_rel, 1)
                for r in range(1, len(TABLES) * HEADS, 2):
                    dve.wait_ge(t_mm, r + 1)
                    dve.tensor_copy(toep_sb[:, r, :], ps[:, 4 + r % 4, 0:TOEP]).then_inc(t_sbD, 1)

            @block.tensor
            def _(pe):
                pe.wait_ge(c_loaded, 16 * CONSTS)
                def body(i):
                    for s in range(4):
                        n = i * 4 + s
                        pe.wait_ge(n_xs, n + 1)
                        if s >= 2 or not isinstance(i, int) or i:
                            pe.wait_ge(n_evA, n - 1)
                            pe.wait_ge(n_evD, n - 1)
                        for k in range(KT):
                            mm = pe.transpose(ps[:, 2 * (s % 2) + k // 4, (k % 4) * P:(k % 4 + 1) * P],
                                              xs[:, s % 2, k * P:(k + 1) * P], ident[:, :])
                            if k % 4 == 3:
                                mm.then_inc(n_T, 1)
                body(0)
                with pe.Fori(1, NT // 4) as i:
                    body(i)
                pe.wait_ge(t_rel, len(TABLES))
                for r in range(len(TABLES) * HEADS):
                    if r >= 4:
                        pe.wait_ge(t_sb if r % 2 == 0 else t_sbD, (r - 4) // 2 + 1)
                    i = r // HEADS
                    pe.matmul(ps[:, 4 + r % 4, 0:TOEP], relx[:, r, :], hot[:, i * TOEP:(i + 1) * TOEP],
                              start=True, stop=True).then_inc(t_mm, 1)

        p_mm, q_ev, kv_ev = sem("p_mm"), sem("q_ev"), sem("kv_ev")
        s_mm, s_max, s_neg, s_exp = sem("s_mm"), sem("s_max"), sem("s_neg"), sem("s_exp")
        pt_T, pt_evA, pt_evD, o_mm, o_ev = sem("pt_T"), sem("pt_evA"), sem("pt_evD"), sem("o_mm"), sem("o_ev")
        o_st = sems("o_st", 3)
        PB = [sum(12 + len(PLANS[h][1]) for h in range(g)) for g in range(NG + 1)]
        KVB = [sum(6 + len(PLANS[h][1]) for h in range(g)) for g in range(NG + 1)]
        units = [(g, i, t) for g in range(NG) for i, t in enumerate(PLANS[g][0])]
        first_unit = [next(n for n, v in enumerate(units) if v[0] == g) for g in range(NG)] + [len(units)]
        NU = len(units)

        def bias_of(g, t, h):
            if t.classes > 1:
                return same[:, t.s, h, :]
            return band[:, g * HEADS + h, t.bias:t.bias + sum(w for _, w in t.keys)]

        def bank_rows(bank, h, w):
            return ps[:, bank, (h // 2) * 256:(h // 2) * 256 + w]

        def copy_turned(copy, n, t, half, done):
            widths = [w for _, w in t.keys]
            src = ps[:, 4 + half, :].rearrange("p (h c q) -> p h c q", h=2, c=2)
            if len(widths) == 2 and widths[0] == widths[1]:
                ins = copy(pT[:, n % 2, 2 * half:2 * half + 2, :, :], src)
            else:
                for c, w in enumerate(widths):
                    ins = copy(pT[0:w, n % 2, 2 * half:2 * half + 2, c, :], src[0:w, :, c, :])
            ins.then_inc(done, 1)

        with nc.Block() as block:
            @block.sync
            def _(sp):
                sp.wait_ge(t_out, 16)
                rows = len(TABLES) * HEADS
                sp.dma_start(band[:, :, :], bass.AP(tensor=toep.tensor, offset=191 - HALF,
                                                    ap=[[rows * TOEP - 1, P], [TOEP, 2 * HEADS], [1, 2 * P]])).then_inc(t_tab, 16)
                for s in range(2):
                    sp.dma_start(same[:, s, :, :], bass.AP(tensor=toep.tensor, offset=(2 + s) * HEADS * TOEP + 191,
                                                           ap=[[rows * TOEP - 1, P], [TOEP, HEADS], [1, P]])).then_inc(t_tab, 16)

                def store(n):
                    g, i, t = units[n]
                    sp.wait_ge(o_ev, n + 1)
                    sp.wait_ge(s_exp, 4 * (n + 1))
                    base, size = SEQS[t.s]
                    rows = attrows[g, base:base + size, :].rearrange("(n r) f -> r n f", r=GROUPS[g][1] // t.classes)
                    sp.dma_start(rows[t.r, t.q0:t.q0 + P, :], orow[:, n % 3, :]).then_inc(o_st[n % 3], 16)
                for g in range(NG):
                    for b, done in enumerate((6, 12, 12 + len(PLANS[g][1]))):
                        sp.wait_ge(p_mm, PB[g] + done)
                        load_in_block(sp, 3 * g + b + 3)
                    for n in range(first_unit[g], first_unit[g + 1]):
                        store(n)
                for b in range(3):
                    sp.wait_ge(o_st[b], 16 * (NU // 3))

            @block.tensor
            def _(pe):
                def bank_free(g, p):
                    if p < 2:
                        if g:
                            pe.wait_ge(o_ev, first_unit[g])
                        return
                    if p - 2 < 6:
                        pe.wait_ge(q_ev, 6 * g + p - 1)
                    else:
                        pe.wait_ge(kv_ev, KVB[g] + p - 7)

                def project(g):
                    p = 0
                    for b in range(2):
                        n = 3 * g + b
                        pe.wait_ge(w_loaded[b], 16 * (g + 1))
                        for hp in range(2):
                            for c in range(NCH):
                                bank_free(g, p)
                                for k in range(KT):
                                    mm = pe.matmul(ps[:, 6 + p % 2, :], wblk[:, b, k, hp * P:(hp + 1) * P],
                                                   xnT[:, k, c * CH:(c + 1) * CH], start=k == 0, stop=k == KT - 1)
                                mm.then_inc(p_mm, 1)
                                p += 1
                    pe.wait_ge(w_loaded[2], 16 * (g + 1))
                    for s, r, classes, a, w in PLANS[g][1]:
                        bank_free(g, p)
                        for k in range(KT):
                            mm = pe.matmul(ps[0:w, 6 + p % 2, 0:GW], of_class(xnT[:, k, :], s, g, r, classes, a, w),
                                           wblk[:, 2, k, :], start=k == 0, stop=k == KT - 1)
                        mm.then_inc(p_mm, 1)
                        p += 1
                    pe.wait_ge(q_ev, 6 * (g + 1))
                    pe.wait_ge(kv_ev, KVB[g + 1])

                def scores(n):
                    g, i, t = units[n]
                    if n >= 2:
                        pe.wait_ge(s_max, 4 * (n - 1))
                    w = sum(w for _, w in t.keys)
                    for h in range(HEADS):
                        rows = slice(64 * (h % 2), 64 * (h % 2) + 64)
                        mm = pe.matmul(bank_rows(2 * (n % 2) + h % 2, h, w),
                                       of_class(qT[rows, h // 2, :], t.s, g, t.r, t.classes, t.q0, P),
                                       of_class(kT[rows, h // 2, :], t.s, g, t.r, t.classes, t.k0, w),
                                       start=True, stop=True)
                        if h >= 2:
                            mm.then_inc(s_mm, 1)

                def turn(n):
                    g, i, t = units[n]
                    pe.wait_ge(s_exp, 4 * (n + 1))
                    if n:
                        pe.wait_ge(pt_evA, n)
                        pe.wait_ge(pt_evD, n)
                    for h in range(HEADS):
                        at_key = 0
                        for c, (_, w) in enumerate(t.keys):
                            mm = pe.transpose(ps[0:w, 4 + h // 2, ((h % 2) * 2 + c) * P:((h % 2) * 2 + c + 1) * P],
                                              sc[:, n % 2, h, at_key:at_key + w], ident[:, :])
                            at_key += w
                        if h % 2:
                            mm.then_inc(pt_T, 1)

                def outputs(n):
                    g, i, t = units[n]
                    pe.wait_ge(pt_evA, n + 1)
                    pe.wait_ge(pt_evD, n + 1)
                    if n >= 2:
                        pe.wait_ge(o_ev, n - 1)
                    for h in range(HEADS):
                        for c, (v, w) in enumerate(t.keys):
                            mm = pe.matmul(ps[:, 6 + n % 2, h * HD:(h + 1) * HD], pT[0:w, n % 2, h, c, :],
                                           V[0:w, v, h * HD:(h + 1) * HD], start=c == 0, stop=c == len(t.keys) - 1)
                    mm.then_inc(o_mm, 1)

                for g in range(NG):
                    project(g)
                    a, b = first_unit[g], first_unit[g + 1]
                    for n in range(a, b + 2):
                        if n < b:
                            scores(n)
                        if a <= n - 1 < b:
                            turn(n - 1)
                        if a <= n - 2 < b:
                            outputs(n - 2)

            @block.scalar
            def _(act):
                def exps(n):
                    g, i, t = units[n]
                    act.wait_ge(s_neg, n + 1)
                    w = sum(w for _, w in t.keys)
                    for h in range(HEADS):
                        act.activation(sc[:, n % 2, h, 0:w], sc[:, n % 2, h, 0:w], ACT.Exp, bias=negm[:, n % 2, h:h + 1],
                                       accum_out=orow[:, n % 3, GW + HEADS + h:GW + HEADS + h + 1]).then_inc(s_exp, 1)

                def turned(n):
                    g, i, t = units[n]
                    act.wait_ge(pt_T, 2 * n + 1)
                    copy_turned(lambda o, x: act.activation(o, x, ACT.Copy), n, t, 0, pt_evA)

                for g in range(NG):
                    for hp in range(2):
                        for c in range(NCH):
                            p = hp * NCH + c
                            act.wait_ge(p_mm, PB[g] + p + 1)
                            act.activation(qT[:, hp, c * CH:(c + 1) * CH], ps[:, 6 + p % 2, :], ACT.Copy,
                                           scale=HD ** -0.5).then_inc(q_ev, 1)
                    a, b = first_unit[g], first_unit[g + 1]
                    for n in range(a, b + 1):
                        if n < b:
                            exps(n)
                        if n - 1 >= a:
                            turned(n - 1)

            @block.vector
            def _(dve):
                def biased(n):
                    g, i, t = units[n]
                    w = sum(w for _, w in t.keys)
                    if n >= 3:
                        dve.wait_ge(o_st[n % 3], 16 * (n // 3))
                    if n >= 2:
                        dve.wait_ge(pt_T, 2 * (n - 1))
                    for h in (0, 2, 1, 3):
                        dve.wait_ge(s_mm, 2 * n + 1 + h % 2)
                        dve.tensor_tensor_reduce(sc[:, n % 2, h, 0:w], bank_rows(2 * (n % 2) + h % 2, h, w), bias_of(g, t, h),
                                                 1.0, -3.0e38, ALU.add, ALU.max,
                                                 orow[:, n % 3, GW + h:GW + h + 1]).then_inc(s_max, 1)
                    dve.wait_ge(s_max, 4 * (n + 1))
                    if n >= 2:
                        dve.wait_ge(s_exp, 4 * (n - 1))
                    dve.tensor_scalar(negm[:, n % 2, :], orow[:, n % 3, GW:GW + HEADS], -1.0, None, ALU.mult).then_inc(s_neg, 1)

                def turned(n):
                    g, i, t = units[n]
                    dve.wait_ge(pt_T, 2 * n + 2)
                    copy_turned(dve.tensor_copy, n, t, 1, pt_evD)

                def outputs(n):
                    dve.wait_ge(o_mm, n + 1)
                    dve.tensor_copy(orow[:, n % 3, 0:GW], ps[:, 6 + n % 2, 0:GW]).then_inc(o_ev, 1)

                for g in range(NG):
                    for hp in range(2):
                        for c in range(NCH):
                            p = 6 + hp * NCH + c
                            dve.wait_ge(p_mm, PB[g] + p + 1)
                            dve.tensor_copy(kT[:, hp, c * CH:(c + 1) * CH], ps[:, 6 + p % 2, :]).then_inc(kv_ev, 1)
                    for v, (s, r, classes, _, w) in enumerate(PLANS[g][1]):
                        p = 12 + v
                        dve.wait_ge(p_mm, PB[g] + p + 1)
                        dve.tensor_copy(V[0:w, v, :], ps[0:w, 6 + p % 2, 0:GW]).then_inc(kv_ev, 1)
                    a, b = first_unit[g], first_unit[g + 1]
                    if g == 0:
                        dve.wait_ge(t_tab, 16 * 3)
                    for n in range(a, b + 2):
                        if n < b:
                            biased(n)
                        if a <= n - 1 < b:
                            turned(n - 1)
                        if a <= n - 2 < b:
                            outputs(n - 2)

        f_tab, f_u, f_uev, f_e, f_eev, f_f, f_fe, f_fo = (sem(n) for n in ("f_tab", "f_u", "f_uev", "f_e", "f_eev", "f_f", "f_fe", "f_fo"))
        a_ld = sems("a_ld", 2)
        a_max, a_w, a_exp, a_at, a_T, a_ev = (sem(n) for n in ("a_max", "a_w", "a_exp", "a_at", "a_T", "a_ev"))
        items = [(c, s) for c in range(F_GROUPS) for s in range(2)]
        u_tiles = [(s, par, j) for s, (_, n) in enumerate(SEQS) for par in range(2) for j in range(n // 2 // P)]
        tabs = (tabP, tabS)

        with nc.Block() as block:
            @block.sync
            def _(sp):
                sp.dma_start(chan_sb[:, :, :], chan).then_inc(f_tab, 16)
                sp.dma_start(tabP[:, :, :, :], pos_prompt.rearrange("(t p) c k -> p t c k", p=P)).then_inc(f_tab, 16)
                sp.dma_start(tabS[:, :, :, :], pos_sample.rearrange("(t p) c k -> p t c k", p=P)).then_inc(f_tab, 16)
                for t in range(NT):
                    if t >= 2:
                        sp.wait_ge(a_at, 3 * (t - 1))
                    sp.dma_start(comb[:, t % 2, :, :], attrows[:, t * P:(t + 1) * P, :].rearrange("g p f -> p g f")) \
                      .then_inc(a_ld[t % 2], 16)
                for b in range(3):
                    sp.wait_ge(f_u, NT * (b + 1))
                    load_gate_block(sp, b, 0)

            @block.tensor
            def _(pe):
                def channels(pair):
                    pe.wait_ge(w_loaded[pair], 16 * 4)
                    for i, (s, par, j) in enumerate(u_tiles):
                        n = pair * NT + i
                        if n >= 2:
                            pe.wait_ge(f_uev, n - 1)
                        base, size = SEQS[s]
                        for k in range(KT):
                            toks = xnT[:, k, base:base + size].rearrange("p (n r) -> p r n", r=2)[:, par, j * P:(j + 1) * P]
                            mm = pe.matmul(ps[:, 4 + n % 2, 0:WB], toks, wblk[:, pair, k, :], start=k == 0, stop=k == KT - 1)
                        mm.then_inc(f_u, 1)

                def positions(i, par):
                    c, s = items[i]
                    half = SEQS[s][1] // 2
                    nt = half // P
                    first = (0 if s == 0 else 8) + par * nt
                    for part in range(2):
                        n = 4 * i + 2 * par + part
                        if n >= 2:
                            pe.wait_ge(f_eev, n - 1)
                        for j in range(nt):
                            mm = pe.matmul(ps[:, part, 0:half], u[:, first + j, (c % 2) * P:(c % 2 + 1) * P],
                                           tabs[s][:, par * nt + j, part, :], start=j == 0, stop=j == nt - 1)
                        mm.then_inc(f_e, 1)

                def over_channels(i, par):
                    c, s = items[i]
                    half = SEQS[s][1] // 2
                    pe.wait_ge(f_eev, 4 * i + 2 * par + 2)
                    if i:
                        pe.wait_ge(f_fe if par == 0 else f_fo, i if par == 0 else 2 * i)
                    for part in range(2):
                        mm = pe.matmul(ps[:, 2 + par, 0:half], chan_sb[:, part, :], eo[:, 2 * par + part, 0:half],
                                       start=part == 0, stop=part == 1)
                    mm.then_inc(f_f, 1)

                def merged(t):
                    pe.wait_ge(a_at, 3 * (t + 1))
                    if t:
                        pe.wait_ge(a_ev, t)
                    for h in range(2):
                        mm = pe.transpose(ps[:, 6, h * P:(h + 1) * P], attk[:, t % 2, h * P:(h + 1) * P], ident[:, :])
                    mm.then_inc(a_T, 1)

                for i in range(len(items)):
                    if i % 4 == 0:
                        if i:
                            over_channels(i - 1, 1)
                        channels(i // 4)
                        pe.wait_ge(f_uev, NT * (i // 4 + 1))
                        if i == 0:
                            pe.wait_ge(f_tab, 48)
                    positions(i, 0)
                    if i % 4:
                        over_channels(i - 1, 1)
                    positions(i, 1)
                    over_channels(i, 0)
                    merged(i)
                over_channels(len(items) - 1, 1)

            @block.scalar
            def _(act):
                for i in range(len(items)):
                    c, s = items[i]
                    base, size = SEQS[s]
                    half = size // 2
                    if i % 4 == 0:
                        for m in range(NT):
                            n = (i // 4) * NT + m
                            act.wait_ge(f_u, n + 1)
                            act.activation(u[:, m, :], ps[:, 4 + n % 2, 0:WB], ACT.Copy).then_inc(f_uev, 1)
                    for par in range(2):
                        for part in range(2):
                            n = 4 * i + 2 * par + part
                            act.wait_ge(f_e, n + 1)
                            act.activation(eo[:, 2 * par + part, 0:half], ps[:, part, 0:half], ACT.Copy).then_inc(f_eev, 1)
                    act.wait_ge(f_f, 2 * i + 1)
                    if i >= 2:
                        act.wait_ge(f_fo, 2 * (i - 1))
                    act.activation(fe[:, i % 2, 0:half], ps[:, 2, 0:half], ACT.Copy).then_inc(f_fe, 1)
                    act.wait_ge(a_max, 2 * (i + 1))
                    act.activation(cw[:, 16 + 0:16 + 12], cw[:, 4:16], ACT.Exp).then_inc(a_exp, 1)
                    act.wait_ge(a_T, i + 1)
                    act.activation(attT[:, :, i * P:(i + 1) * P], ps[:, 6, 0:2 * P].rearrange("p (h t) -> p h t", h=2),
                                   ACT.Copy).then_inc(a_ev, 1)

            @block.vector
            def _(dve):
                def weights(t):
                    b = comb[:, t % 2, :, :]
                    m = lambda g: b[:, g, GW:GW + HEADS]
                    dve.wait_ge(a_ld[t % 2], 16 * (t // 2 + 1))
                    if t:
                        dve.wait_ge(a_exp, t)
                    dve.tensor_tensor(cw[:, 0:4], m(0), m(1), ALU.max).then_inc(a_w, 1)
                    dve.wait_ge(a_w, 6 * t + 1)
                    dve.tensor_tensor(cw[:, 0:4], cw[:, 0:4], m(2), ALU.max).then_inc(a_max, 1)
                    dve.wait_ge(a_max, 2 * t + 1)
                    dve.tensor_tensor(cw[:, 4:16].rearrange("p (g h) -> p g h", g=NG), b[:, :, GW:GW + HEADS],
                                      cw[:, 0:4].rearrange("p (o h) -> p o h", o=1).broadcast_to([P, NG, HEADS]),
                                      ALU.subtract).then_inc(a_max, 1)

                def merge(t):
                    b = comb[:, t % 2, :, :]
                    dve.wait_ge(a_exp, t + 1)
                    dve.tensor_tensor(cw[:, 28:40].rearrange("p (g h) -> p g h", g=NG), b[:, :, GW + HEADS:AROW],
                                      cw[:, 16:28].rearrange("p (g h) -> p g h", g=NG), ALU.mult).then_inc(a_w, 1)
                    dve.wait_ge(a_w, 6 * t + 2)
                    dve.tensor_tensor(cw[:, 40:44], cw[:, 28:32], cw[:, 32:36], ALU.add).then_inc(a_w, 1)
                    dve.wait_ge(a_w, 6 * t + 3)
                    dve.tensor_tensor(cw[:, 40:44], cw[:, 40:44], cw[:, 36:40], ALU.add).then_inc(a_w, 1)
                    dve.wait_ge(a_w, 6 * t + 4)
                    dve.reciprocal(cw[:, 44:48], cw[:, 40:44]).then_inc(a_w, 1)
                    dve.wait_ge(a_w, 6 * t + 5)
                    dve.tensor_tensor(cw[:, 48:60].rearrange("p (g h) -> p g h", g=NG), cw[:, 16:28].rearrange("p (g h) -> p g h", g=NG),
                                      cw[:, 44:48].rearrange("p (o h) -> p o h", o=1).broadcast_to([P, NG, HEADS]),
                                      ALU.mult).then_inc(a_w, 1)
                    dve.wait_ge(a_w, 6 * t + 6)
                    for g in range(NG):
                        o = b[:, g, 0:GW].rearrange("p (h e) -> p h e", h=HEADS)
                        ins = dve.tensor_tensor(o, o, cw[:, 48 + 4 * g:52 + 4 * g].rearrange("p (h o) -> p h o", o=1)
                                                .broadcast_to([P, HEADS, HD]), ALU.mult)
                    ins.then_inc(a_at, 1)
                    dve.wait_ge(a_at, 3 * t + 1)
                    dve.tensor_tensor(b[:, 0, 0:GW], b[:, 0, 0:GW], b[:, 1, 0:GW], ALU.add).then_inc(a_at, 1)
                    dve.wait_ge(a_at, 3 * t + 2)
                    if t >= 2:
                        dve.wait_ge(a_T, t - 1)
                    dve.tensor_tensor(attk[:, t % 2, :], b[:, 0, 0:GW], b[:, 2, 0:GW], ALU.add).then_inc(a_at, 1)

                def butterfly(i):
                    c, s = items[i]
                    base, size = SEQS[s]
                    half = size // 2
                    dve.wait_ge(f_fe, i + 1)
                    dve.wait_ge(f_f, 2 * i + 2)
                    dve.tensor_tensor(fourT[:, c, base:base + half], fe[:, i % 2, 0:half], ps[:, 3, 0:half], ALU.add).then_inc(f_fo, 1)
                    dve.tensor_tensor(fourT[:, c, base + half:base + size], fe[:, i % 2, 0:half], ps[:, 3, 0:half],
                                      ALU.subtract).then_inc(f_fo, 1)

                for i in range(len(items)):
                    if i:
                        butterfly(i - 1)
                    weights(i)
                    merge(i)
                butterfly(len(items) - 1)

        m_mm, m_sig, m_gat, m_mix = (sem(n) for n in ("m_mm", "m_sig", "m_gat", "m_mix"))
        SUB = 2 * NCH

        with nc.Block() as block:
            @block.sync
            def _(sp):
                with sp.Fori(0, KT // 2 - 1) as j:
                    sp.wait_ge(m_mm, (j + 1) * (4 * SUB))
                    for b in range(3):
                        load_gate_block(sp, b, j + 1)
                sp.dma_start(wblk[:, 3, :, :], gate_cols(w_out, 3 * WB, 0)).then_inc(w_loaded[3], 16)
                sp.wait_ge(m_mm, (KT // 2) * 4 * SUB)
                for b in range(3):
                    sp.dma_start(wblk[:, b, :, :], gate_cols(w_out, b * WB, 0)).then_inc(w_loaded[b], 16)

            @block.tensor
            def _(pe):
                def pair(j, first=False):
                    for b in range(3):
                        pe.wait_ge(w_loaded[b], gate_block_at(b, j))
                    for dt in range(2):
                        for c in range(NCH):
                            s = dt * NCH + c
                            if s >= 2 or not first:
                                pe.wait_ge(m_gat, (j * SUB + s - 1) * 2)
                            toks = slice(c * CH, (c + 1) * CH)
                            cols = slice(dt * P, (dt + 1) * P)
                            for q, (b, ks, src) in enumerate(((0, range(8), xnT), (1, range(8), xnT), (2, range(2), attT),
                                                              (2, range(2, 8), fourT))):
                                for k in ks:
                                    mm = pe.matmul(ps[:, 4 * (s % 2) + q, :], wblk[:, b, k, cols], src[:, k - ks[0], toks],
                                                   start=k == ks[0], stop=k == ks[-1])
                                mm.then_inc(m_mm, 1)
                pair(0, True)
                with pe.Fori(1, KT // 2) as j:
                    pair(j)

            @block.scalar
            def _(act):
                def pair(j, first=False):
                    for s in range(SUB):
                        for q in range(2):
                            act.wait_ge(m_mm, (j * SUB + s) * 4 + q + 1)
                            if q == 0 and (s >= 2 or not first):
                                act.wait_ge(m_gat, (j * SUB + s - 1) * 2)
                            act.nop(nofuse=True)
                            act.activation(sig[:, s % 2, q, :], ps[:, 4 * (s % 2) + q, :], ACT.Sigmoid,
                                           bias=bg[:, bass.ds(j * 2 + (q * KT + s // NCH), 1)]).then_inc(m_sig, 1)
                pair(0, True)
                with act.Fori(1, KT // 2) as j:
                    pair(j)

            @block.vector
            def _(dve):
                def pair(j, first=False):
                    for s in range(SUB):
                        n = j * SUB + s
                        for q in range(2):
                            dve.wait_ge(m_sig, n * 2 + q + 1)
                            dve.wait_ge(m_mm, n * 4 + q + 3)
                            if q == 0 and (s >= 2 or not first):
                                dve.wait_ge(m_mix, n - 1)
                            dve.tensor_tensor(gated[:, s % 2, q, :], ps[:, 4 * (s % 2) + 2 + q, :], sig[:, s % 2, q, :],
                                              ALU.mult).then_inc(m_gat, 1)
                        dve.wait_ge(m_gat, n * 2 + 2)
                        c = s % NCH
                        dve.tensor_tensor(mixT[:, bass.ds(j * 2 + s // NCH, 1), c * CH:(c + 1) * CH].rearrange("p o t -> p (o t)"),
                                          gated[:, s % 2, 0, :], gated[:, s % 2, 1, :], ALU.add).then_inc(m_mix, 1)
                pair(0, True)
                with dve.Fori(1, KT // 2) as j:
                    pair(j)

        ring_ld = sems("ring_ld", 6)
        r_g2, r_x, r_st = sem("r_g2"), sems("r_x", 2), sems("r_st", 2)
        r_y, r_x2, r_ssq, r_var, r_std, r_rstd, r_xn = (sem(n) for n in ("r_y", "r_x2", "r_ssq", "r_var", "r_std", "r_rstd", "r_xn"))
        r_T, r_TevA, r_TevD, r_lg, r_sm, r_exp, r_af, r_aT, r_aev = (sem(n) for n in (
            "r_T", "r_TevA", "r_TevD", "r_lg", "r_sm", "r_exp", "r_af", "r_aT", "r_aev"))
        r_top, r_idf, r_iT, r_fin = (sem(n) for n in ("r_top", "r_idf", "r_iT", "r_fin"))

        def chunk_parts(e, j):
            if j < 8:
                return [w[0, bass.ds(e, 1), :, j * WB:(j + 1) * WB].rearrange("o (k p) n -> p (o k) n", p=P) for w in (w_eg, w_eu)]
            c = (j - 8) * WB
            return [w_ed[0, bass.ds(e, 1), h * D:(h + 1) * D, c:c + WB].rearrange("o (k p) n -> p (o k) n", p=P) for h in range(2)]

        def load_chunk(sp, e, j):
            for h, part in enumerate(chunk_parts(e, j)):
                sp.dma_start(ring[:, j % 6, 8 * h:8 * h + 8, :], part).then_inc(ring_ld[j % 6], 16)

        with nc.Block() as block:
            @block.sync
            def _(sp):
                sp.dma_start(g2[:, :], norm2_g.partition_broadcast(P)).then_inc(r_g2, 16)
                for t in range(2):
                    sp.dma_start(xres[:, t, :], x[t * P:(t + 1) * P, :]).then_inc(r_x[t], 16)
                for j in range(3):
                    load_chunk(sp, 0, j)
                for t in range(NT):
                    rows = slice(t * P, (t + 1) * P)
                    sp.wait_ge(r_xn, t + 1)
                    sp.dma_start(resid[rows, :], xres[:, t % 2, :]).then_inc(r_st[t % 2], 16)
                    sp.dma_start(normed[rows, :], xn2[:, t % 2, :]).then_inc(r_st[t % 2], 16)
                    if t + 2 < NT:
                        sp.wait_ge(r_st[t % 2], 32 * (t // 2 + 1))
                        sp.dma_start(xres[:, t % 2, :], x[(t + 2) * P:(t + 3) * P, :]).then_inc(r_x[t % 2], 16)
                for b in range(2):
                    sp.wait_ge(r_st[b], 32 * (NT // 2))

            @block.tensor
            def _(pe):
                def out(t):
                    if t == 0:
                        for b in range(3):
                            pe.wait_ge(w_loaded[b], gate_block_at(b, 3) + 16)
                        pe.wait_ge(w_loaded[3], 16)
                    if t:
                        pe.wait_ge(r_x2, 2 * t)
                    for nb in range(4):
                        for k in range(KT):
                            mm = pe.matmul(ps[:, nb // 2, (nb % 2) * WB:(nb % 2 + 1) * WB], mixT[:, k, t * P:(t + 1) * P],
                                           wblk[:, nb, k, :], start=k == 0, stop=k == KT - 1)
                        if nb % 2:
                            mm.then_inc(r_y, 1)

                def turn(t):
                    pe.wait_ge(r_xn, t + 1)
                    if t:
                        pe.wait_ge(r_TevA, t)
                        pe.wait_ge(r_TevD, t)
                    for k in range(KT):
                        mm = pe.transpose(ps[:, 2 + k // 4, (k % 4) * P:(k % 4 + 1) * P], xn2[:, t % 2, k * P:(k + 1) * P], ident[:, :])
                        if k % 4 == 3:
                            mm.then_inc(r_T, 1)

                def logits(t):
                    pe.wait_ge(r_TevA, t + 1)
                    pe.wait_ge(r_TevD, t + 1)
                    if t:
                        pe.wait_ge(r_exp, t)
                    for k in range(KT):
                        mm = pe.matmul(ps[:, 4, 0:E], xn2T[:, t % 2, k, :], wr[:, k, :], start=k == 0, stop=k == KT - 1)
                    mm.then_inc(r_lg, 1)

                def turn_aff(t):
                    pe.wait_ge(r_af, 2 * (t + 1))
                    if t:
                        pe.wait_ge(r_aev, t)
                    pe.transpose(ps[0:E, 5, 0:P], atok[:, t % 2, :], ident[:, :]).then_inc(r_aT, 1)

                for t in range(NT + 3):
                    if t < NT:
                        out(t)
                    if 0 <= t - 1 < NT:
                        turn(t - 1)
                    if 0 <= t - 2 < NT:
                        logits(t - 2)
                    if 0 <= t - 3 < NT:
                        turn_aff(t - 3)
                for s in range(2):
                    pe.wait_ge(r_idf, s + 1)
                    cap = CAPS[s]
                    pe.transpose(ps[0:cap, 6 + s, 0:E], vals[s][:, :], ident[0:E, 0:E])
                    pe.transpose(ps[0:cap, 6 + s, E:2 * E], idxf[s][:, :], ident[0:E, 0:E]).then_inc(r_iT, 1)

            @block.scalar
            def _(act):
                def norm(t):
                    act.wait_ge(r_x2, 2 * (t + 1))
                    if t:
                        act.wait_ge(r_ssq, t)
                    act.activation(junk2[:, :], xres[:, t % 2, :], ACT.Square, accum_out=stat[:, 0:1]).then_inc(r_ssq, 1)
                    act.wait_ge(r_var, t + 1)
                    act.activation(stat[:, 2:3], stat[:, 1:2], ACT.Sqrt).then_inc(r_std, 1)

                def turned(t):
                    act.wait_ge(r_T, 2 * t + 1)
                    if t >= 2:
                        act.wait_ge(r_lg, t - 1)
                    act.activation(xn2T[:, t % 2, 0:4, :], ps[:, 2, :].rearrange("p (k t) -> p k t", k=4), ACT.Copy).then_inc(r_TevA, 1)

                def softmax(t):
                    act.wait_ge(r_sm, t + 1)
                    act.activation(stat[:, 32 + 16 * (t % 2):48 + 16 * (t % 2)], ps[:, 4, 0:E], ACT.Exp, bias=stat[:, 5:6],
                                   accum_out=stat[:, 6:7]).then_inc(r_exp, 1)

                for t in range(NT + 2):
                    if t < NT:
                        norm(t)
                    if 0 <= t - 1 < NT:
                        turned(t - 1)
                    if 0 <= t - 2 < NT:
                        softmax(t - 2)

            @block.vector
            def _(dve):
                dve.wait_ge(r_g2, 16)

                def norm(t):
                    dve.wait_ge(r_x[t % 2], 16 * (t // 2 + 1))
                    for h in range(2):
                        dve.wait_ge(r_y, 2 * t + h + 1)
                        half = xres[:, t % 2, h * CH:(h + 1) * CH]
                        dve.tensor_tensor(half, half, ps[:, h, :], ALU.add).then_inc(r_x2, 1)
                    dve.wait_ge(r_ssq, t + 1)
                    dve.tensor_scalar(stat[:, 1:2], stat[:, 0:1], 1.0 / D, EPS, ALU.mult, ALU.add).then_inc(r_var, 1)
                    dve.wait_ge(r_std, t + 1)
                    dve.reciprocal(stat[:, 3:4], stat[:, 2:3]).then_inc(r_rstd, 1)
                    dve.wait_ge(r_rstd, t + 1)
                    if t >= 2:
                        dve.wait_ge(r_T, 2 * (t - 1))
                        dve.wait_ge(r_st[t % 2], 32 * (t // 2))
                    dve.scalar_tensor_tensor(out=xn2[:, t % 2, :], in0=xres[:, t % 2, :], scalar=stat[:, 3:4], in1=g2[:, :],
                                             op0=ALU.mult, op1=ALU.mult).then_inc(r_xn, 1)

                def turned(t):
                    dve.wait_ge(r_T, 2 * t + 2)
                    if t >= 2:
                        dve.wait_ge(r_lg, t - 1)
                    dve.tensor_copy(xn2T[:, t % 2, 4:8, :], ps[:, 3, :].rearrange("p (k t) -> p k t", k=4)).then_inc(r_TevD, 1)

                def softmax(t):
                    dve.wait_ge(r_lg, t + 1)
                    dve.tensor_reduce(stat[:, 5:6], ps[:, 4, 0:E], AX.X, ALU.max, negate=True).then_inc(r_sm, 1)
                    dve.wait_ge(r_exp, t + 1)
                    dve.reciprocal(stat[:, 7:8], stat[:, 6:7]).then_inc(r_af, 1)
                    dve.wait_ge(r_af, 2 * t + 1)
                    if t >= 2:
                        dve.wait_ge(r_aT, t - 1)
                    dve.tensor_scalar(atok[:, t % 2, :], stat[:, 32 + 16 * (t % 2):48 + 16 * (t % 2)], stat[:, 7:8], None,
                                      ALU.mult).then_inc(r_af, 1)

                def keep(t):
                    s, tile = (0, t) if t < 8 else (1, t - 8)
                    dve.wait_ge(r_aT, t + 1)
                    dve.tensor_copy(aff[s][:, tile * P:(tile + 1) * P], ps[0:E, 5, 0:P]).then_inc(r_aev, 1)

                tops = [0]

                def top(s, r):
                    v = vals[s][:, 8 * r:8 * r + 8]
                    if tops[0] or True:
                        dve.wait_ge(r_top, tops[0])
                    dve.max(v, aff[s][:, :]).then_inc(r_top, 1)
                    dve.wait_ge(r_top, tops[0] + 1)
                    dve.max_index(idxr[s][:, 8 * r:8 * r + 8], v, aff[s][:, :]).then_inc(r_top, 1)
                    dve.wait_ge(r_top, tops[0] + 2)
                    dve.match_replace(aff[s][:, :], v, aff[s][:, :], -1.0).then_inc(r_top, 1)
                    tops[0] += 3

                def as_float(s):
                    dve.wait_ge(r_top, tops[0])
                    dve.tensor_scalar(idxf[s][:, :], idxr[s][:, :], float(SEQS[s][0]), None, ALU.add).then_inc(r_idf, 1)

                rounds = list(range(CAPS[0] // 8))
                for t in range(NT + 3):
                    if t < NT:
                        norm(t)
                    if 0 <= t - 1 < NT:
                        turned(t - 1)
                    if 0 <= t - 2 < NT:
                        softmax(t - 2)
                    if 0 <= t - 3 < NT:
                        keep(t - 3)
                    if t >= 11 or t == 10 and False:
                        if t == 11:
                            dve.wait_ge(r_aev, 8)
                        for _ in range(4):
                            if rounds:
                                top(0, rounds.pop(0))
                while rounds:
                    top(0, rounds.pop(0))
                as_float(0)
                dve.wait_ge(r_aev, NT)
                for r in range(CAPS[1] // 8):
                    top(1, r)
                as_float(1)
                for s in range(2):
                    cap = CAPS[s]
                    dve.wait_ge(r_iT, s + 1)
                    dve.tensor_copy(gate[s][:, :], ps[0:cap, 6 + s, 0:E])
                    dve.tensor_copy(idx[s][:, :], ps[0:cap, 6 + s, E:2 * E]).then_inc(r_fin, 1)
                dve.wait_ge(r_fin, 2)

        x_idx, x_in, x_T, x_ev = (sem(n) for n in ("x_idx", "x_in", "x_T", "x_ev"))
        gu_mm, gu_sig, gu_g, h_done = (sem(n) for n in ("gu_mm", "gu_sig", "gu_g", "h_done"))
        y_mm, y_ev, yt_T, yt_ev, sc_idx, scat = (sem(n) for n in ("y_mm", "y_ev", "yt_T", "yt_ev", "sc_idx", "scat"))
        GU_BANKS, Y_BANKS = 4, 2

        with nc.Block() as block:
            @block.sync
            def _(sp):
                for j in range(3, 6):
                    load_chunk(sp, 0, j)
                def late(e):
                    for j in range(6, 12):
                        sp.wait_ge(gu_mm, e * FT + 2 * (j - 5))
                        sp.nop(nofuse=True)
                        load_chunk(sp, e, j)
                with sp.Fori(0, E - 1) as e:
                    late(e)
                    for j in range(6):
                        if j + 6 < 8:
                            sp.wait_ge(gu_mm, e * FT + 2 * (j + 7))
                        else:
                            sp.wait_ge(y_mm, e * KT + 2 * (j - 1))
                        sp.nop(nofuse=True)
                        load_chunk(sp, e + 1, j)
                late(E - 1)

            @block.gpsimd
            def _(pool):
                def pick(dst, e, done, n):
                    for s in range(2):
                        ins = pool.tensor_copy(dst[s][:, :], idx[s][:, bass.ds(e, 1)])
                        ins.then_inc(done, 1)
                    pool.wait_ge(done, n)
                    pool.nop(nofuse=True)

                def gather(e, n):
                    pick(idx_in, e, x_idx, n)
                    for s in range(2):
                        pool.indirect_dma_start(xg[s][:, :], None, normed, bass.IndirectOffsetOnAxis(ap=idx_in[s][:, 0:1], axis=0)) \
                            .then_inc(x_in, 16)

                def scatter(e, n, before):
                    pool.wait_ge(yt_ev, n * KT + Y_BANKS)
                    if before is not None:
                        pool.wait_ge(scat, before)
                    pick(idx_out, e, sc_idx, n * 2)
                    for s in range(2):
                        pool.indirect_dma_start(resid, bass.IndirectOffsetOnAxis(ap=idx_out[s][:, 0:1], axis=0), ytok[s][:, :], None,
                                                compute_op=ALU.add).then_inc(scat, 16)
                gather(0, 2)
                with pool.Fori(0, E - 1) as e:
                    pool.wait_ge(x_T, (e + 1) * 4)
                    gather(e + 1, (e + 2) * 2)
                    scatter(e, e + 1, e * 32)
                scatter(E - 1, E, (E - 1) * 32)
                pool.wait_ge(scat, E * 32)

            @block.tensor
            def _(pe):
                def turn_tokens(n):
                    pe.wait_ge(x_in, (n + 1) * 32)
                    for b in range(4):
                        for k in (2 * b, 2 * b + 1):
                            at_col = (k % 2) * CAP
                            pe.transpose(ps[:, b, at_col:at_col + CAPS[0]], xg[0][:, k * P:(k + 1) * P], ident[:, :])
                            mm = pe.transpose(ps[:, b, at_col + CAPS[0]:at_col + CAP], xg[1][:, k * P:(k + 1) * P],
                                              ident[0:CAPS[1], 0:CAPS[1]])
                        mm.then_inc(x_T, 1)

                def chunk_there(e, j):
                    pe.wait_ge(ring_ld[j % 6], (e * 2 + (j // 6 + 1)) * 32)

                def gate_up(e):
                    pe.wait_ge(x_ev, (e + 1) * 4)
                    for j in range(8):
                        chunk_there(e, j)
                        for ft in range(2):
                            q = 2 * j + ft
                            pe.wait_ge(h_done, e * FT + (q + 1))
                            for part in range(2):
                                for k in range(KT):
                                    mm = pe.matmul(ps[:, q % 4, part * CAP:(part + 1) * CAP],
                                                   ring[:, j % 6, 8 * part + k, ft * P:(ft + 1) * P], xeT[:, k, :],
                                                   start=k == 0, stop=k == KT - 1)
                            mm.then_inc(gu_mm, 1)

                def turn_y(e, dt):
                    pe.wait_ge(y_ev, e * KT + (dt + 1 + Y_BANKS))
                    pe.wait_ge(yt_ev, e * KT + (dt + 1))
                    pe.transpose(ps[:, 6 + dt % 2, 0:P], yT[:, dt % 2, 0:CAPS[0]], ident[:, :])
                    pe.transpose(ps[0:CAPS[1], 6 + dt % 2, P:2 * P], yT[:, dt % 2, CAPS[0]:CAP], ident[:, :]).then_inc(yt_T, 1)

                def down(e, last):
                    pe.wait_ge(h_done, (e + 1) * FT + GU_BANKS)
                    for dt in range(KT):
                        j = 8 + dt // 2
                        chunk_there(e, j)
                        pe.wait_ge(y_ev, e * KT + (dt + 1))
                        for k in range(FT):
                            mm = pe.matmul(ps[:, 4 + dt % 2, 0:CAP], ring[:, j % 6, k, (dt % 2) * P:(dt % 2 + 1) * P], hT[:, k, :],
                                           start=k == 0, stop=k == FT - 1)
                        mm.then_inc(y_mm, 1)
                        if dt:
                            turn_y(e, dt - 1)
                    if not last:
                        turn_tokens(e + 1)
                    turn_y(e, KT - 1)

                turn_tokens(0)
                with pe.Fori(0, E - 1) as e:
                    gate_up(e)
                    down(e, False)
                gate_up(E - 1)
                down(E - 1, True)

            @block.scalar
            def _(act):
                act.sem_inc(y_ev, Y_BANKS)

                def tokens(n):
                    for b in range(4):
                        act.wait_ge(x_T, n * 4 + (b + 1))
                        act.activation(xeT[:, 2 * b:2 * b + 2, :], ps[:, b, 0:2 * CAP].rearrange("p (k t) -> p k t", k=2),
                                       ACT.Copy).then_inc(x_ev, 1)

                def expert(e, last):
                    for q in range(FT):
                        act.wait_ge(gu_mm, e * FT + (q + 1))
                        act.activation(sg[:, q % 4, :], ps[:, q % 4, 0:CAP], ACT.Sigmoid).then_inc(gu_sig, 1)
                    for dt in range(KT):
                        act.wait_ge(y_mm, e * KT + (dt + 1))
                        act.activation(yT[:, dt % 2, :], ps[:, 4 + dt % 2, 0:CAP], ACT.Copy).then_inc(y_ev, 1)
                    if not last:
                        tokens(e + 1)
                tokens(0)
                with act.Fori(0, E - 1) as e:
                    expert(e, False)
                expert(E - 1, True)

            @block.vector
            def _(dve):
                dve.sem_inc(h_done, GU_BANKS)
                dve.sem_inc(yt_ev, Y_BANKS)

                def expert(e):
                    for q in range(FT):
                        dve.wait_ge(gu_sig, e * FT + (q + 1))
                        dve.tensor_tensor(sgg[:, q % 4, :], ps[:, q % 4, 0:CAP], sg[:, q % 4, :], ALU.mult).then_inc(gu_g, 1)
                        dve.wait_ge(gu_g, e * FT + (q + 1))
                        dve.tensor_tensor(hT[:, q, :], ps[:, q % 4, CAP:2 * CAP], sgg[:, q % 4, :], ALU.mult).then_inc(h_done, 1)
                    dve.wait_ge(scat, e * 32)
                    for dt in range(KT):
                        dve.wait_ge(yt_T, e * KT + (dt + 1))
                        cols = slice(dt * P, (dt + 1) * P)
                        dve.tensor_scalar(ytok[0][:, cols], ps[:, 6 + dt % 2, 0:P], gate[0][:, bass.ds(e, 1)], None, ALU.mult)
                        dve.tensor_scalar(ytok[1][:, cols], ps[0:CAPS[1], 6 + dt % 2, P:2 * P], gate[1][:, bass.ds(e, 1)], None,
                                          ALU.mult).then_inc(yt_ev, 1)
                with dve.Fori(0, E) as e:
                    expert(e)

        l_g, l_ld, l_st = sem("l_g"), sems("l_ld", 4), sems("l_st", 4)
        l_ssq, l_var, l_std, l_rstd, l_y = (sem(n) for n in ("l_ssq", "l_var", "l_std", "l_rstd", "l_y"))
        LT = NT // 4

        with nc.Block() as block:
            @block.sync
            def _(sp):
                sp.dma_start(gF[:, :], final_g.rearrange("(o d) -> o d", o=1).partition_broadcast(P)).then_inc(l_g, 16)
                for s in range(4):
                    sp.dma_start(fin[:, s, :], resid[s * P:(s + 1) * P, :]).then_inc(l_ld[s], 16)
                with sp.Fori(1, LT) as i:
                    for s in range(4):
                        sp.wait_ge(l_y, i * 4 + (s - 3))
                        sp.dma_start(fin[:, s, :], resid[bass.ds(i * 4 * P + s * P, P), :]).then_inc(l_ld[s], 16)

            @block.scalar
            def _(act):
                def squares(i):
                    for s in range(4):
                        act.wait_ge(l_ld[s], (i + 1) * 16)
                        act.activation(fout[:, s, :], fin[:, s, :], ACT.Square, accum_out=stat[:, s:s + 1]).then_inc(l_ssq, 1)

                def roots(i):
                    for s in range(4):
                        act.wait_ge(l_var, i * 4 + (s + 1))
                        act.activation(stat[:, 8 + s:9 + s], stat[:, 4 + s:5 + s], ACT.Sqrt).then_inc(l_std, 1)

                def rows(i):
                    for s in range(4):
                        act.wait_ge(l_y, i * 4 + (s + 1))
                        act.dma_start(y[bass.ds(i * 4 * P + s * P, P), :], fout[:, s, :]).then_inc(l_st[s], 16)
                squares(0)
                roots(0)
                rows(0)
                with act.Fori(1, LT) as i:
                    for s in range(4):
                        act.wait_ge(l_st[s], i * 16)
                    squares(i)
                    roots(i)
                    rows(i)
                for s in range(4):
                    act.wait_ge(l_st[s], LT * 16)

            @block.vector
            def _(dve):
                dve.wait_ge(l_g, 16)
                with dve.Fori(0, LT) as i:
                    for s in range(4):
                        dve.wait_ge(l_ssq, i * 4 + (s + 1))
                        dve.tensor_scalar(stat[:, 4 + s:5 + s], stat[:, s:s + 1], 1.0 / D, EPS, ALU.mult, ALU.add).then_inc(l_var, 1)
                    for s in range(4):
                        dve.wait_ge(l_std, i * 4 + (s + 1))
                        dve.reciprocal(stat[:, 12 + s:13 + s], stat[:, 8 + s:9 + s]).then_inc(l_rstd, 1)
                        dve.wait_ge(l_rstd, i * 4 + (s + 1))
                        dve.scalar_tensor_tensor(out=fout[:, s, :], in0=fin[:, s, :], scalar=stat[:, 12 + s:13 + s], in1=gF[:, :],
                                                 op0=ALU.mult, op1=ALU.mult).then_inc(l_y, 1)


_INS = ['rel_bias', 'norm1_g', 'w_in', 'w_attn_br', 'w_four_br', 'w_gate', 'b_gate', 'w_out', 'norm2_g', 'w_router',
        'w_exp_gate', 'w_exp_up', 'w_exp_down', 'final_g']


def kernel(**inputs):
    import numpy as _np
    import concourse.bacc as _bacc
    from concourse import mybir as _mybir
    from concourse.bass_utils import run_bass_kernel_spmd as _run

    nc = _bacc.Bacc("TRN2", target_bir_lowering=False, num_devices=1)
    arrays, args = {}, []

    def add(name, a):
        a = _np.ascontiguousarray(a)
        arrays[name] = a
        args.append(nc.dram_tensor(name, a.shape, _mybir.dt.from_np(a.dtype), kind="ExternalInput").ap())

    xp, xs = _np.asarray(inputs["x_prompt"]), _np.asarray(inputs["x_sample"])
    add("in_x_dram", _np.concatenate([xp.reshape(-1, D), xs.reshape(-1, D)], 0))
    for name in _INS:
        a = _np.asarray(inputs[name])
        add(f"in_{name}_dram", a.reshape(-1, P).T if name == "b_gate" else a)
    add("c_identity_dram", _np.eye(P, dtype=_np.float32))
    add("c_one_hot_dram", bucket_one_hot())
    add("c_pos_prompt_dram", position_table(SEQS[0][1]))
    add("c_pos_sample_dram", position_table(SEQS[1][1]))
    add("c_chan_dram", channel_table())
    out = nc.dram_tensor("out_y_dram", (TOKENS, D), _mybir.dt.float32, kind="ExternalOutput").ap()
    encoder(nc, *args, out)
    r = _run(nc, [arrays], core_ids=[0])
    got = r.results[0]["out_y_dram"]
    n = SEQS[0][1]
    return got[:n].reshape(xp.shape), got[n:].reshape(xs.shape)
```

```python
from collections import namedtuple
from contextlib import ExitStack

import concourse.bass as bass
import numpy as np
from concourse import mybir

F32 = mybir.dt.float32
F32R = mybir.dt.float32r
U32 = mybir.dt.uint32
ALU = mybir.AluOpType
ACT = mybir.ActivationFunctionType
AX = mybir.AxisListType

P = 128
D = 1024
KT = D // P
SEQS = ((0, 1024), (1024, 512))
TOKENS = 1536
NT = TOKENS // P
CH = 512
NCH = TOKENS // CH
HD = 64
HEADS = 4
GROUPS = ((128, 1), (512, 4), (2048, 16))
NG = len(GROUPS)
HALF = 64
GW = HEADS * HD
ATT_W = NG * GW
F_GROUPS = 6
F_W = F_GROUPS * P
BUCKETS = 32
MAX_DISTANCE = 1024
E = 16
CAPS = tuple(2 * n // E for _, n in SEQS)
CAP = sum(CAPS)
FF = 2048
FT = FF // P
EPS = 1e-6
NEG = -1e30
WB = 256
AROW = GW + 2 * HEADS
TOEP = 384
KB = 1024


TABLES = ((0, 1), (1, 1)) + tuple((2, P * GROUPS[2][1] // n) for _, n in SEQS)



def bucket_of(rel):
    nb = BUCKETS // 2
    exact = nb // 2
    n = np.abs(rel)
    large = exact + (np.log(np.maximum(n, exact) / exact) / np.log(MAX_DISTANCE / exact) * (nb - exact)).astype(np.int32)
    return (rel > 0).astype(np.int32) * nb + np.where(n < exact, n, np.minimum(large, nb - 1))


def bucket_one_hot():
    table = np.zeros((BUCKETS + 1, len(TABLES), TOEP), np.float32)
    place = np.arange(TOEP) - 191
    for i, (g, classes) in enumerate(TABLES):
        dil = GROUPS[g][1]
        seen = (place % classes == 0) & (np.abs(place) <= HALF * classes)
        row = np.where(seen, bucket_of(dil // classes * place), BUCKETS)
        table[row, i, np.arange(TOEP)] = 1.0
    return table.reshape(BUCKETS + 1, len(TABLES) * TOEP)


def position_table(n):
    t = np.concatenate([np.arange(0, n, 2), np.arange(1, n, 2)])
    angle = 2 * np.pi * ((t[:, None] * np.arange(n // 2)[None, :]) % n) / n
    both = np.stack([np.cos(angle), np.sin(angle)], 1) / np.sqrt(n * P)
    return both.astype(np.float32)


def channel_table():
    c = np.arange(P)
    angle = 2 * np.pi * ((c[:, None] * c[None, :]) % P) / P
    return np.stack([np.cos(angle), -np.sin(angle)], 1).astype(np.float32)



QueryTile = namedtuple("QueryTile", "s r classes q0 k0 keys bias")


def attention_plan(g):
    dil = GROUPS[g][1]
    tiles, values = [], []
    for s, (base, n) in enumerate(SEQS):
        length = n // dil
        if length > P:
            cuts = [0] + list(range(HALF, length, P)) + [length]
            for r in range(dil):
                first = len(values)
                for a, b in zip(cuts, cuts[1:]):
                    values.append((s, r, 1, a, b - a))
                for i in range(length // P):
                    keys = [(first + i + c, cuts[i + c + 1] - cuts[i + c]) for c in range(2)]
                    tiles.append(QueryTile(s=s, r=r, classes=1, q0=i * P, k0=cuts[i], keys=keys,
                                                 bias=cuts[i] - i * P + HALF))
        else:
            classes = P // length
            for r in range(dil // classes):
                values.append((s, r, classes, 0, P))
                tiles.append(QueryTile(s=s, r=r, classes=classes, q0=0, k0=0, keys=[(len(values) - 1, P)], bias=HALF))
    return tiles, values


PLANS = [attention_plan(g) for g in range(NG)]
MAXV = max(len(v) for _, v in PLANS)


def of_class(view, s, g, r, classes, a, n):
    base, size = SEQS[s]
    return view[:, base:base + size].rearrange("p (n r) -> p r n", r=GROUPS[g][1] // classes)[:, r, a:a + n]


def encoder(nc, x, rel_bias, norm1_g, w_in, w_attn_br, w_four_br, w_gate, b_gate, w_out, norm2_g,
            w_router, w_eg, w_eu, w_ed, final_g, identity, one_hot, pos_prompt, pos_sample, chan, y):
    ctx = ExitStack()
    with ctx:
        ARENA = 17 * KB

        def at(name, kb, shape, dt=F32):
            return nc.alloc_sbuf_tensor_at(name, list(shape), dt, offset=int(ARENA + kb * KB))

        def sem(name):
            return ctx.enter_context(nc.semaphore(name))

        def sems(name, n):
            return [sem(f"{name}{i}") for i in range(n)]

        xnT = at("xnT", 0, [P, KT, TOKENS])
        attT = at("attT", 48, [P, GW // P, TOKENS])
        fourT = at("fourT", 60, [P, F_GROUPS, TOKENS])
        wblk = at("wblk", 96, [P, 4, KT, WB])
        xin = at("xin", 128, [P, 4, D])
        xs = at("xs", 144, [P, 2, D])
        g1 = at("g1", 152, [P, D])
        junk = at("junk", 156, [P, D])
        hot = at("hot", 160, [BUCKETS + 1, len(TABLES) * TOEP])
        relx = at("relx", 167, [BUCKETS + 1, len(TABLES) * HEADS, P])
        toep_sb = at("toep_sb", 176, [P, len(TABLES) * HEADS, TOEP])
        qT = at("qT", 128, [P, 2, TOKENS])
        kT = at("kT", 140, [P, 2, TOKENS])
        V = at("V", 152, [P, MAXV, GW])
        band = at("band", 168, [P, 2 * HEADS, 2 * P])
        same = at("same", 176, [P, 2, HEADS, P])
        sc = at("sc", 180, [P, 2, HEADS, 2 * P])
        pT = at("pT", 188, [P, 2, HEADS, 2, P])
        orow = at("orow", 196, [P, 3, AROW])
        u = at("u", 128, [P, NT, WB])
        tabP = at("tabP", 140, [P, 8, 2, 512])
        tabS = at("tabS", 172, [P, 4, 2, 256])
        eo = at("eo", 180, [P, 4, 512])
        fe = at("fe", 188, [P, 2, 512])
        comb = at("comb", 192, [P, 2, NG, AROW])
        attk = at("attk", 198.25, [P, 2, GW])
        cw = at("cw", 200.25, [P, 64])
        chan_sb = at("chan_sb", 200.5, [P, 2, P])
        mixT = at("mixT", 128, [P, KT, TOKENS])
        sig = at("sig", 176, [P, 2, 2, CH])
        gated = at("gated", 184, [P, 2, 2, CH])
        xres = at("xres", 48, [P, 2, D])
        xn2 = at("xn2", 56, [P, 2, D])
        xn2T = at("xn2T", 64, [P, 2, KT, P])
        g2 = at("g2", 72, [P, D])
        aff = [at("affP", 76, [E, 1024]), at("affS", 80, [E, 512])]
        junk2 = at("junk2", 84, [P, D])
        vals = [at("valsP", 88, [E, CAPS[0]]), at("valsS", 88.5, [E, CAPS[1]])]
        idxr = [at("idxrP", 89, [E, CAPS[0]], U32), at("idxrS", 89.5, [E, CAPS[1]], U32)]
        idxf = [at("idxfP", 90, [E, CAPS[0]]), at("idxfS", 90.5, [E, CAPS[1]])]
        atok = at("atok", 91, [P, 2, E])
        raw = at("raw", 0, [P, 4, 16, WB])
        wh = at("wh", 64, [P, 4, 16 * P], F32R)
        wl = at("wl", 96, [P, 4, 16 * P], F32R)
        xsplit = at("xsplit", 128, [P, KT, 2, CAP], F32R)
        hsplit = at("hsplit", 140, [P, FT, 2 * CAP], F32R)
        xg = [at("xgP", 164, [CAPS[0], D]), at("xgS", 168, [CAPS[1], D])]
        ytok = [at("ytokP", 172, [CAPS[0], D]), at("ytokS", 176, [CAPS[1], D])]
        low = at("low", 180, [P, 2, 2, CAP])
        gu = at("gu", 183, [P, 2, 2, CAP])
        sg = at("sg", 186, [P, 2, CAP])
        sgg = at("sgg", 187.5, [P, 2, CAP])
        h = at("h", 189, [P, 4, CAP])
        ylow = at("ylow", 192, [CAPS[1], 2, CH])
        ysum = at("ysum", 196, [CAPS[1], 2, CH])
        fin = at("fin", 128, [P, 4, D])
        fout = at("fout", 144, [P, 4, D])
        gF = at("gF", 160, [P, D])
        ident = at("ident", 202, [P, P])
        bg = at("bg", 202.5, [P, 2 * KT])
        relb = at("relb", 202.75, [BUCKETS + 1, NG * HEADS])
        wr = at("wr", 203, [P, KT, E])
        stat = at("stat", 203.5, [P, 64])
        negm = at("negm", 203.75, [P, 2, HEADS])
        gate = [at("gateP", 204, [CAPS[0], E]), at("gateS", 204.125, [CAPS[1], E])]
        idx = [at("idxP", 204.25, [CAPS[0], E], U32), at("idxS", 204.375, [CAPS[1], E], U32)]
        idx_in = [at("idx_inP", 204.5, [CAPS[0], 1], U32), at("idx_inS", 204.53125, [CAPS[1], 1], U32)]
        idx_out = [at("idx_outP", 204.5625, [CAPS[0], 1], U32), at("idx_outS", 204.59375, [CAPS[1], 1], U32)]

        ps = ctx.enter_context(nc.psum_tensor("ps", [P, 8, 512], F32))

        toep = nc.dram_tensor("toep", [P, len(TABLES) * HEADS, TOEP], F32, kind="Internal").ap()
        attrows = nc.dram_tensor("attrows", [NG, TOKENS, AROW], F32, kind="Internal").ap()
        resid = nc.dram_tensor("resid", [TOKENS, D], F32, kind="Internal").ap()
        normed = nc.dram_tensor("normed", [TOKENS, D], F32, kind="Internal").ap()

        w_loaded = sems("w_loaded", 4)
        G0, R0 = 12, 24

        def in_block(n):
            return (n % 3) * ATT_W + (n // 3) * WB if n < 9 else 3 * ATT_W + (n - 9) * WB

        def load_in_block(sp, n):
            c = in_block(n)
            sp.dma_start(wblk[:, n % 3, :, :], w_in[0, :, c:c + WB].rearrange("(k p) n -> p k n", p=P)) \
              .then_inc(w_loaded[n % 3], 16)

        def gate_cols(w, first, j):
            return w[0, :, bass.ds(j * WB + first, WB)].rearrange("(k p) n -> p k n", p=P)

        def load_gate_block(sp, b, j):
            if b < 2:
                sp.dma_start(wblk[:, b, :, :], gate_cols(w_gate, b * D, j)).then_inc(w_loaded[b], 16)
            else:
                sp.dma_start(wblk[:, 2, 0:2, :], gate_cols(w_attn_br, 0, j)).then_inc(w_loaded[2], 16)
                sp.dma_start(wblk[:, 2, 2:8, :], gate_cols(w_four_br, 0, j)).then_inc(w_loaded[2], 16)

        def gate_block_at(b, j):
            return (j + 1) * 16 + 64 if b < 2 else (j + 1) * 32 + 64

        c_loaded, x_in_ld = sem("c_loaded"), sems("x_in_ld", 4)
        n_ssq, n_var, n_std, n_rstd, n_xs = (sem(n) for n in ("n_ssq", "n_var", "n_std", "n_rstd", "n_xs"))
        n_T, n_evA, n_evD = sem("n_T"), sem("n_evA"), sem("n_evD")
        t_masked, t_mm, t_sb, t_sbD, t_out, t_tab, t_rel = (sem(n) for n in ("t_masked", "t_mm", "t_sb", "t_sbD", "t_out", "t_tab", "t_rel"))
        CONSTS = 6

        with nc.Block() as block:
            @block.sync
            def _(sp):
                sp.dma_start(ident[:, :], identity).then_inc(c_loaded, 16)
                sp.dma_start(g1[:, :], norm1_g.partition_broadcast(P)).then_inc(c_loaded, 16)
                for s in range(4):
                    sp.dma_start(xin[:, s, :], x[s * P:(s + 1) * P, :]).then_inc(x_in_ld[s], 16)
                sp.dma_start(hot[:, :], one_hot).then_inc(c_loaded, 16)
                sp.dma_start(relb[0:BUCKETS, :], rel_bias).then_inc(c_loaded, 16)
                sp.dma_start(bg[:, :], b_gate).then_inc(c_loaded, 16)
                sp.dma_start(wr[:, :, :], w_router[0].rearrange("(k p) e -> p k e", p=P)).then_inc(c_loaded, 16)
                for n in range(3):
                    load_in_block(sp, n)
                with sp.Fori(1, NT // 4) as i:
                    for s in range(4):
                        sp.wait_ge(n_xs, i * 4 + (s - 3))
                        sp.dma_start(xin[:, s, :], x[bass.ds(i * 4 * P + s * P, P), :]).then_inc(x_in_ld[s], 16)
                sp.wait_ge(t_sb, len(TABLES) * HEADS // 2)
                sp.wait_ge(t_sbD, len(TABLES) * HEADS // 2)
                sp.dma_start(toep, toep_sb[:, :, :]).then_inc(t_out, 16)

            @block.gpsimd
            def _(pool):
                pool.memset(relb[BUCKETS:BUCKETS + 1, :], NEG).then_inc(t_masked, 1)

            @block.scalar
            def _(act):
                def square(i, s):
                    act.wait_ge(x_in_ld[s], (i + 1) * 16)
                    if s or not isinstance(i, int) or i:
                        act.wait_ge(n_ssq, i * 4 + s)
                    act.activation(junk[:, :], xin[:, s, :], ACT.Square, accum_out=stat[:, s:s + 1]).then_inc(n_ssq, 1)

                def root(i, s):
                    act.wait_ge(n_var, i * 4 + s + 1)
                    act.activation(stat[:, 8 + s:9 + s], stat[:, 4 + s:5 + s], ACT.Sqrt).then_inc(n_std, 1)

                def evict(i, s):
                    act.wait_ge(n_T, (i * 4 + s) * 2 + 1)
                    act.activation(xnT[:, 0:4, bass.ds((i * 4 + s) * P, P)], ps[:, 2 * (s % 2), :].rearrange("p (k t) -> p k t", k=4),
                                   ACT.Copy).then_inc(n_evA, 1)

                def body(i):
                    for s in range(4):
                        square(i, s)
                        root(i, s)
                        evict(i, s)
                body(0)
                with act.Fori(1, NT // 4) as i:
                    body(i)
                for r in range(0, len(TABLES) * HEADS, 2):
                    act.wait_ge(t_mm, r + 1)
                    act.activation(toep_sb[:, r, :], ps[:, 4 + r % 4, 0:TOEP], ACT.Copy).then_inc(t_sb, 1)

            @block.vector
            def _(dve):
                dve.wait_ge(c_loaded, 16 * CONSTS)

                def body(i):
                    for s in range(4):
                        n = i * 4 + s
                        dve.wait_ge(n_ssq, n + 1)
                        dve.tensor_scalar(stat[:, 4 + s:5 + s], stat[:, s:s + 1], 1.0 / D, EPS, ALU.mult, ALU.add).then_inc(n_var, 1)
                        dve.wait_ge(n_std, n + 1)
                        dve.reciprocal(stat[:, 12 + s:13 + s], stat[:, 8 + s:9 + s]).then_inc(n_rstd, 1)
                        dve.wait_ge(n_rstd, n + 1)
                        if s >= 2 or not isinstance(i, int) or i:
                            dve.wait_ge(n_T, (n - 1) * 2)
                        dve.scalar_tensor_tensor(out=xs[:, s % 2, :], in0=xin[:, s, :], scalar=stat[:, 12 + s:13 + s],
                                                 in1=g1[:, :], op0=ALU.mult, op1=ALU.mult).then_inc(n_xs, 1)
                        dve.wait_ge(n_T, n * 2 + 2)
                        dve.tensor_copy(xnT[:, 4:8, bass.ds(n * P, P)],
                                        ps[:, 2 * (s % 2) + 1, :].rearrange("p (k t) -> p k t", k=4)).then_inc(n_evD, 1)
                body(0)
                with dve.Fori(1, NT // 4) as i:
                    body(i)
                dve.wait_ge(t_masked, 1)
                for i, (g, _) in enumerate(TABLES):
                    dve.tensor_copy(relx[:, i * HEADS:(i + 1) * HEADS, :],
                                    relb[:, g * HEADS:(g + 1) * HEADS].rearrange("b (h o) -> b h o", o=1)
                                    .broadcast_to([BUCKETS + 1, HEADS, P])).then_inc(t_rel, 1)
                for r in range(1, len(TABLES) * HEADS, 2):
                    dve.wait_ge(t_mm, r + 1)
                    dve.tensor_copy(toep_sb[:, r, :], ps[:, 4 + r % 4, 0:TOEP]).then_inc(t_sbD, 1)

            @block.tensor
            def _(pe):
                pe.wait_ge(c_loaded, 16 * CONSTS)
                def body(i):
                    for s in range(4):
                        n = i * 4 + s
                        pe.wait_ge(n_xs, n + 1)
                        if s >= 2 or not isinstance(i, int) or i:
                            pe.wait_ge(n_evA, n - 1)
                            pe.wait_ge(n_evD, n - 1)
                        for k in range(KT):
                            mm = pe.transpose(ps[:, 2 * (s % 2) + k // 4, (k % 4) * P:(k % 4 + 1) * P],
                                              xs[:, s % 2, k * P:(k + 1) * P], ident[:, :])
                            if k % 4 == 3:
                                mm.then_inc(n_T, 1)
                body(0)
                with pe.Fori(1, NT // 4) as i:
                    body(i)
                pe.wait_ge(t_rel, len(TABLES))
                for r in range(len(TABLES) * HEADS):
                    if r >= 4:
                        pe.wait_ge(t_sb if r % 2 == 0 else t_sbD, (r - 4) // 2 + 1)
                    i = r // HEADS
                    pe.matmul(ps[:, 4 + r % 4, 0:TOEP], relx[:, r, :], hot[:, i * TOEP:(i + 1) * TOEP],
                              start=True, stop=True).then_inc(t_mm, 1)

        p_mm, q_ev, kv_ev = sem("p_mm"), sem("q_ev"), sem("kv_ev")
        s_mm, s_max, s_neg, s_exp = sem("s_mm"), sem("s_max"), sem("s_neg"), sem("s_exp")
        pt_T, pt_evA, pt_evD, o_mm, o_ev = sem("pt_T"), sem("pt_evA"), sem("pt_evD"), sem("o_mm"), sem("o_ev")
        o_st = sems("o_st", 3)
        PB = [sum(12 + len(PLANS[h][1]) for h in range(g)) for g in range(NG + 1)]
        KVB = [sum(6 + len(PLANS[h][1]) for h in range(g)) for g in range(NG + 1)]
        units = [(g, i, t) for g in range(NG) for i, t in enumerate(PLANS[g][0])]
        first_unit = [next(n for n, v in enumerate(units) if v[0] == g) for g in range(NG)] + [len(units)]
        NU = len(units)

        def bias_of(g, t, h):
            if t.classes > 1:
                return same[:, t.s, h, :]
            return band[:, g * HEADS + h, t.bias:t.bias + sum(w for _, w in t.keys)]

        def bank_rows(bank, h, w):
            return ps[:, bank, (h // 2) * 256:(h // 2) * 256 + w]

        def copy_turned(copy, n, t, half, done):
            widths = [w for _, w in t.keys]
            src = ps[:, 4 + half, :].rearrange("p (h c q) -> p h c q", h=2, c=2)
            if len(widths) == 2 and widths[0] == widths[1]:
                ins = copy(pT[:, n % 2, 2 * half:2 * half + 2, :, :], src)
            else:
                for c, w in enumerate(widths):
                    ins = copy(pT[0:w, n % 2, 2 * half:2 * half + 2, c, :], src[0:w, :, c, :])
            ins.then_inc(done, 1)

        with nc.Block() as block:
            @block.sync
            def _(sp):
                sp.wait_ge(t_out, 16)
                rows = len(TABLES) * HEADS
                sp.dma_start(band[:, :, :], bass.AP(tensor=toep.tensor, offset=191 - HALF,
                                                    ap=[[rows * TOEP - 1, P], [TOEP, 2 * HEADS], [1, 2 * P]])).then_inc(t_tab, 16)
                for s in range(2):
                    sp.dma_start(same[:, s, :, :], bass.AP(tensor=toep.tensor, offset=(2 + s) * HEADS * TOEP + 191,
                                                           ap=[[rows * TOEP - 1, P], [TOEP, HEADS], [1, P]])).then_inc(t_tab, 16)

                def store(n):
                    g, i, t = units[n]
                    sp.wait_ge(o_ev, n + 1)
                    sp.wait_ge(s_exp, 4 * (n + 1))
                    base, size = SEQS[t.s]
                    rows = attrows[g, base:base + size, :].rearrange("(n r) f -> r n f", r=GROUPS[g][1] // t.classes)
                    sp.dma_start(rows[t.r, t.q0:t.q0 + P, :], orow[:, n % 3, :]).then_inc(o_st[n % 3], 16)
                for g in range(NG):
                    for b, done in enumerate((6, 12, 12 + len(PLANS[g][1]))):
                        sp.wait_ge(p_mm, PB[g] + done)
                        load_in_block(sp, 3 * g + b + 3)
                    for n in range(first_unit[g], first_unit[g + 1]):
                        store(n)
                for b in range(3):
                    sp.wait_ge(o_st[b], 16 * (NU // 3))

            @block.tensor
            def _(pe):
                def bank_free(g, p):
                    if p < 2:
                        if g:
                            pe.wait_ge(o_ev, first_unit[g])
                        return
                    if p - 2 < 6:
                        pe.wait_ge(q_ev, 6 * g + p - 1)
                    else:
                        pe.wait_ge(kv_ev, KVB[g] + p - 7)

                def project(g):
                    p = 0
                    for b in range(2):
                        n = 3 * g + b
                        pe.wait_ge(w_loaded[b], 16 * (g + 1))
                        for hp in range(2):
                            for c in range(NCH):
                                bank_free(g, p)
                                for k in range(KT):
                                    mm = pe.matmul(ps[:, 6 + p % 2, :], wblk[:, b, k, hp * P:(hp + 1) * P],
                                                   xnT[:, k, c * CH:(c + 1) * CH], start=k == 0, stop=k == KT - 1)
                                mm.then_inc(p_mm, 1)
                                p += 1
                    pe.wait_ge(w_loaded[2], 16 * (g + 1))
                    for s, r, classes, a, w in PLANS[g][1]:
                        bank_free(g, p)
                        for k in range(KT):
                            mm = pe.matmul(ps[0:w, 6 + p % 2, 0:GW], of_class(xnT[:, k, :], s, g, r, classes, a, w),
                                           wblk[:, 2, k, :], start=k == 0, stop=k == KT - 1)
                        mm.then_inc(p_mm, 1)
                        p += 1
                    pe.wait_ge(q_ev, 6 * (g + 1))
                    pe.wait_ge(kv_ev, KVB[g + 1])

                def scores(n):
                    g, i, t = units[n]
                    if n >= 2:
                        pe.wait_ge(s_max, 4 * (n - 1))
                    w = sum(w for _, w in t.keys)
                    for h in range(HEADS):
                        rows = slice(64 * (h % 2), 64 * (h % 2) + 64)
                        mm = pe.matmul(bank_rows(2 * (n % 2) + h % 2, h, w),
                                       of_class(qT[rows, h // 2, :], t.s, g, t.r, t.classes, t.q0, P),
                                       of_class(kT[rows, h // 2, :], t.s, g, t.r, t.classes, t.k0, w),
                                       start=True, stop=True)
                        if h >= 2:
                            mm.then_inc(s_mm, 1)

                def turn(n):
                    g, i, t = units[n]
                    pe.wait_ge(s_exp, 4 * (n + 1))
                    if n:
                        pe.wait_ge(pt_evA, n)
                        pe.wait_ge(pt_evD, n)
                    for h in range(HEADS):
                        at_key = 0
                        for c, (_, w) in enumerate(t.keys):
                            mm = pe.transpose(ps[0:w, 4 + h // 2, ((h % 2) * 2 + c) * P:((h % 2) * 2 + c + 1) * P],
                                              sc[:, n % 2, h, at_key:at_key + w], ident[:, :])
                            at_key += w
                        if h % 2:
                            mm.then_inc(pt_T, 1)

                def outputs(n):
                    g, i, t = units[n]
                    pe.wait_ge(pt_evA, n + 1)
                    pe.wait_ge(pt_evD, n + 1)
                    if n >= 2:
                        pe.wait_ge(o_ev, n - 1)
                    for h in range(HEADS):
                        for c, (v, w) in enumerate(t.keys):
                            mm = pe.matmul(ps[:, 6 + n % 2, h * HD:(h + 1) * HD], pT[0:w, n % 2, h, c, :],
                                           V[0:w, v, h * HD:(h + 1) * HD], start=c == 0, stop=c == len(t.keys) - 1)
                    mm.then_inc(o_mm, 1)

                for g in range(NG):
                    project(g)
                    a, b = first_unit[g], first_unit[g + 1]
                    for n in range(a, b + 2):
                        if n < b:
                            scores(n)
                        if a <= n - 1 < b:
                            turn(n - 1)
                        if a <= n - 2 < b:
                            outputs(n - 2)

            @block.scalar
            def _(act):
                def exps(n):
                    g, i, t = units[n]
                    act.wait_ge(s_neg, n + 1)
                    w = sum(w for _, w in t.keys)
                    for h in range(HEADS):
                        act.activation(sc[:, n % 2, h, 0:w], sc[:, n % 2, h, 0:w], ACT.Exp, bias=negm[:, n % 2, h:h + 1],
                                       accum_out=orow[:, n % 3, GW + HEADS + h:GW + HEADS + h + 1]).then_inc(s_exp, 1)

                def turned(n):
                    g, i, t = units[n]
                    act.wait_ge(pt_T, 2 * n + 1)
                    copy_turned(lambda o, x: act.activation(o, x, ACT.Copy), n, t, 0, pt_evA)

                for g in range(NG):
                    for hp in range(2):
                        for c in range(NCH):
                            p = hp * NCH + c
                            act.wait_ge(p_mm, PB[g] + p + 1)
                            act.activation(qT[:, hp, c * CH:(c + 1) * CH], ps[:, 6 + p % 2, :], ACT.Copy,
                                           scale=HD ** -0.5).then_inc(q_ev, 1)
                    a, b = first_unit[g], first_unit[g + 1]
                    for n in range(a, b + 1):
                        if n < b:
                            exps(n)
                        if n - 1 >= a:
                            turned(n - 1)

            @block.vector
            def _(dve):
                def biased(n):
                    g, i, t = units[n]
                    w = sum(w for _, w in t.keys)
                    if n >= 3:
                        dve.wait_ge(o_st[n % 3], 16 * (n // 3))
                    if n >= 2:
                        dve.wait_ge(pt_T, 2 * (n - 1))
                    for h in (0, 2, 1, 3):
                        dve.wait_ge(s_mm, 2 * n + 1 + h % 2)
                        dve.tensor_tensor_reduce(sc[:, n % 2, h, 0:w], bank_rows(2 * (n % 2) + h % 2, h, w), bias_of(g, t, h),
                                                 1.0, -3.0e38, ALU.add, ALU.max,
                                                 orow[:, n % 3, GW + h:GW + h + 1]).then_inc(s_max, 1)
                    dve.wait_ge(s_max, 4 * (n + 1))
                    if n >= 2:
                        dve.wait_ge(s_exp, 4 * (n - 1))
                    dve.tensor_scalar(negm[:, n % 2, :], orow[:, n % 3, GW:GW + HEADS], -1.0, None, ALU.mult).then_inc(s_neg, 1)

                def turned(n):
                    g, i, t = units[n]
                    dve.wait_ge(pt_T, 2 * n + 2)
                    copy_turned(dve.tensor_copy, n, t, 1, pt_evD)

                def outputs(n):
                    dve.wait_ge(o_mm, n + 1)
                    dve.tensor_copy(orow[:, n % 3, 0:GW], ps[:, 6 + n % 2, 0:GW]).then_inc(o_ev, 1)

                for g in range(NG):
                    for hp in range(2):
                        for c in range(NCH):
                            p = 6 + hp * NCH + c
                            dve.wait_ge(p_mm, PB[g] + p + 1)
                            dve.tensor_copy(kT[:, hp, c * CH:(c + 1) * CH], ps[:, 6 + p % 2, :]).then_inc(kv_ev, 1)
                    for v, (s, r, classes, _, w) in enumerate(PLANS[g][1]):
                        p = 12 + v
                        dve.wait_ge(p_mm, PB[g] + p + 1)
                        dve.tensor_copy(V[0:w, v, :], ps[0:w, 6 + p % 2, 0:GW]).then_inc(kv_ev, 1)
                    a, b = first_unit[g], first_unit[g + 1]
                    if g == 0:
                        dve.wait_ge(t_tab, 16 * 3)
                    for n in range(a, b + 2):
                        if n < b:
                            biased(n)
                        if a <= n - 1 < b:
                            turned(n - 1)
                        if a <= n - 2 < b:
                            outputs(n - 2)

        f_tab, f_u, f_uev, f_e, f_eev, f_f, f_fe, f_fo = (sem(n) for n in ("f_tab", "f_u", "f_uev", "f_e", "f_eev", "f_f", "f_fe", "f_fo"))
        a_ld = sems("a_ld", 2)
        a_max, a_w, a_exp, a_at, a_T, a_ev = (sem(n) for n in ("a_max", "a_w", "a_exp", "a_at", "a_T", "a_ev"))
        items = [(c, s) for c in range(F_GROUPS) for s in range(2)]
        u_tiles = [(s, par, j) for s, (_, n) in enumerate(SEQS) for par in range(2) for j in range(n // 2 // P)]
        tabs = (tabP, tabS)

        with nc.Block() as block:
            @block.sync
            def _(sp):
                sp.dma_start(chan_sb[:, :, :], chan).then_inc(f_tab, 16)
                sp.dma_start(tabP[:, :, :, :], pos_prompt.rearrange("(t p) c k -> p t c k", p=P)).then_inc(f_tab, 16)
                sp.dma_start(tabS[:, :, :, :], pos_sample.rearrange("(t p) c k -> p t c k", p=P)).then_inc(f_tab, 16)
                for t in range(NT):
                    if t >= 2:
                        sp.wait_ge(a_at, 3 * (t - 1))
                    sp.dma_start(comb[:, t % 2, :, :], attrows[:, t * P:(t + 1) * P, :].rearrange("g p f -> p g f")) \
                      .then_inc(a_ld[t % 2], 16)
                for b in range(3):
                    sp.wait_ge(f_u, NT * (b + 1))
                    load_gate_block(sp, b, 0)

            @block.tensor
            def _(pe):
                def channels(pair):
                    pe.wait_ge(w_loaded[pair], 16 * 4)
                    for i, (s, par, j) in enumerate(u_tiles):
                        n = pair * NT + i
                        if n >= 2:
                            pe.wait_ge(f_uev, n - 1)
                        base, size = SEQS[s]
                        for k in range(KT):
                            toks = xnT[:, k, base:base + size].rearrange("p (n r) -> p r n", r=2)[:, par, j * P:(j + 1) * P]
                            mm = pe.matmul(ps[:, 4 + n % 2, 0:WB], toks, wblk[:, pair, k, :], start=k == 0, stop=k == KT - 1)
                        mm.then_inc(f_u, 1)

                def positions(i, par):
                    c, s = items[i]
                    half = SEQS[s][1] // 2
                    nt = half // P
                    first = (0 if s == 0 else 8) + par * nt
                    for part in range(2):
                        n = 4 * i + 2 * par + part
                        if n >= 2:
                            pe.wait_ge(f_eev, n - 1)
                        for j in range(nt):
                            mm = pe.matmul(ps[:, part, 0:half], u[:, first + j, (c % 2) * P:(c % 2 + 1) * P],
                                           tabs[s][:, par * nt + j, part, :], start=j == 0, stop=j == nt - 1)
                        mm.then_inc(f_e, 1)

                def over_channels(i, par):
                    c, s = items[i]
                    half = SEQS[s][1] // 2
                    pe.wait_ge(f_eev, 4 * i + 2 * par + 2)
                    if i:
                        pe.wait_ge(f_fe if par == 0 else f_fo, i if par == 0 else 2 * i)
                    for part in range(2):
                        mm = pe.matmul(ps[:, 2 + par, 0:half], chan_sb[:, part, :], eo[:, 2 * par + part, 0:half],
                                       start=part == 0, stop=part == 1)
                    mm.then_inc(f_f, 1)

                def merged(t):
                    pe.wait_ge(a_at, 3 * (t + 1))
                    if t:
                        pe.wait_ge(a_ev, t)
                    for h in range(2):
                        mm = pe.transpose(ps[:, 6, h * P:(h + 1) * P], attk[:, t % 2, h * P:(h + 1) * P], ident[:, :])
                    mm.then_inc(a_T, 1)

                for i in range(len(items)):
                    if i % 4 == 0:
                        if i:
                            over_channels(i - 1, 1)
                        channels(i // 4)
                        pe.wait_ge(f_uev, NT * (i // 4 + 1))
                        if i == 0:
                            pe.wait_ge(f_tab, 48)
                    positions(i, 0)
                    if i % 4:
                        over_channels(i - 1, 1)
                    positions(i, 1)
                    over_channels(i, 0)
                    merged(i)
                over_channels(len(items) - 1, 1)

            @block.scalar
            def _(act):
                for i in range(len(items)):
                    c, s = items[i]
                    base, size = SEQS[s]
                    half = size // 2
                    if i % 4 == 0:
                        for m in range(NT):
                            n = (i // 4) * NT + m
                            act.wait_ge(f_u, n + 1)
                            act.activation(u[:, m, :], ps[:, 4 + n % 2, 0:WB], ACT.Copy).then_inc(f_uev, 1)
                    for par in range(2):
                        for part in range(2):
                            n = 4 * i + 2 * par + part
                            act.wait_ge(f_e, n + 1)
                            act.activation(eo[:, 2 * par + part, 0:half], ps[:, part, 0:half], ACT.Copy).then_inc(f_eev, 1)
                    act.wait_ge(f_f, 2 * i + 1)
                    if i >= 2:
                        act.wait_ge(f_fo, 2 * (i - 1))
                    act.activation(fe[:, i % 2, 0:half], ps[:, 2, 0:half], ACT.Copy).then_inc(f_fe, 1)
                    act.wait_ge(a_max, 2 * (i + 1))
                    act.activation(cw[:, 16 + 0:16 + 12], cw[:, 4:16], ACT.Exp).then_inc(a_exp, 1)
                    act.wait_ge(a_T, i + 1)
                    act.activation(attT[:, :, i * P:(i + 1) * P], ps[:, 6, 0:2 * P].rearrange("p (h t) -> p h t", h=2),
                                   ACT.Copy).then_inc(a_ev, 1)

            @block.vector
            def _(dve):
                def weights(t):
                    b = comb[:, t % 2, :, :]
                    m = lambda g: b[:, g, GW:GW + HEADS]
                    dve.wait_ge(a_ld[t % 2], 16 * (t // 2 + 1))
                    if t:
                        dve.wait_ge(a_exp, t)
                    dve.tensor_tensor(cw[:, 0:4], m(0), m(1), ALU.max).then_inc(a_w, 1)
                    dve.wait_ge(a_w, 6 * t + 1)
                    dve.tensor_tensor(cw[:, 0:4], cw[:, 0:4], m(2), ALU.max).then_inc(a_max, 1)
                    dve.wait_ge(a_max, 2 * t + 1)
                    dve.tensor_tensor(cw[:, 4:16].rearrange("p (g h) -> p g h", g=NG), b[:, :, GW:GW + HEADS],
                                      cw[:, 0:4].rearrange("p (o h) -> p o h", o=1).broadcast_to([P, NG, HEADS]),
                                      ALU.subtract).then_inc(a_max, 1)

                def merge(t):
                    b = comb[:, t % 2, :, :]
                    dve.wait_ge(a_exp, t + 1)
                    dve.tensor_tensor(cw[:, 28:40].rearrange("p (g h) -> p g h", g=NG), b[:, :, GW + HEADS:AROW],
                                      cw[:, 16:28].rearrange("p (g h) -> p g h", g=NG), ALU.mult).then_inc(a_w, 1)
                    dve.wait_ge(a_w, 6 * t + 2)
                    dve.tensor_tensor(cw[:, 40:44], cw[:, 28:32], cw[:, 32:36], ALU.add).then_inc(a_w, 1)
                    dve.wait_ge(a_w, 6 * t + 3)
                    dve.tensor_tensor(cw[:, 40:44], cw[:, 40:44], cw[:, 36:40], ALU.add).then_inc(a_w, 1)
                    dve.wait_ge(a_w, 6 * t + 4)
                    dve.reciprocal(cw[:, 44:48], cw[:, 40:44]).then_inc(a_w, 1)
                    dve.wait_ge(a_w, 6 * t + 5)
                    dve.tensor_tensor(cw[:, 48:60].rearrange("p (g h) -> p g h", g=NG), cw[:, 16:28].rearrange("p (g h) -> p g h", g=NG),
                                      cw[:, 44:48].rearrange("p (o h) -> p o h", o=1).broadcast_to([P, NG, HEADS]),
                                      ALU.mult).then_inc(a_w, 1)
                    dve.wait_ge(a_w, 6 * t + 6)
                    for g in range(NG):
                        o = b[:, g, 0:GW].rearrange("p (h e) -> p h e", h=HEADS)
                        ins = dve.tensor_tensor(o, o, cw[:, 48 + 4 * g:52 + 4 * g].rearrange("p (h o) -> p h o", o=1)
                                                .broadcast_to([P, HEADS, HD]), ALU.mult)
                    ins.then_inc(a_at, 1)
                    dve.wait_ge(a_at, 3 * t + 1)
                    dve.tensor_tensor(b[:, 0, 0:GW], b[:, 0, 0:GW], b[:, 1, 0:GW], ALU.add).then_inc(a_at, 1)
                    dve.wait_ge(a_at, 3 * t + 2)
                    if t >= 2:
                        dve.wait_ge(a_T, t - 1)
                    dve.tensor_tensor(attk[:, t % 2, :], b[:, 0, 0:GW], b[:, 2, 0:GW], ALU.add).then_inc(a_at, 1)

                def butterfly(i):
                    c, s = items[i]
                    base, size = SEQS[s]
                    half = size // 2
                    dve.wait_ge(f_fe, i + 1)
                    dve.wait_ge(f_f, 2 * i + 2)
                    dve.tensor_tensor(fourT[:, c, base:base + half], fe[:, i % 2, 0:half], ps[:, 3, 0:half], ALU.add).then_inc(f_fo, 1)
                    dve.tensor_tensor(fourT[:, c, base + half:base + size], fe[:, i % 2, 0:half], ps[:, 3, 0:half],
                                      ALU.subtract).then_inc(f_fo, 1)

                for i in range(len(items)):
                    if i:
                        butterfly(i - 1)
                    weights(i)
                    merge(i)
                butterfly(len(items) - 1)

        m_mm, m_sig, m_gat, m_mix = (sem(n) for n in ("m_mm", "m_sig", "m_gat", "m_mix"))
        SUB = 2 * NCH

        with nc.Block() as block:
            @block.sync
            def _(sp):
                with sp.Fori(0, KT // 2 - 1) as j:
                    sp.wait_ge(m_mm, (j + 1) * (4 * SUB))
                    for b in range(3):
                        load_gate_block(sp, b, j + 1)
                sp.dma_start(wblk[:, 3, :, :], gate_cols(w_out, 3 * WB, 0)).then_inc(w_loaded[3], 16)
                sp.wait_ge(m_mm, (KT // 2) * 4 * SUB)
                for b in range(3):
                    sp.dma_start(wblk[:, b, :, :], gate_cols(w_out, b * WB, 0)).then_inc(w_loaded[b], 16)

            @block.tensor
            def _(pe):
                def pair(j, first=False):
                    for b in range(3):
                        pe.wait_ge(w_loaded[b], gate_block_at(b, j))
                    for dt in range(2):
                        for c in range(NCH):
                            s = dt * NCH + c
                            if s >= 2 or not first:
                                pe.wait_ge(m_gat, (j * SUB + s - 1) * 2)
                            toks = slice(c * CH, (c + 1) * CH)
                            cols = slice(dt * P, (dt + 1) * P)
                            for q, (b, ks, src) in enumerate(((0, range(8), xnT), (1, range(8), xnT), (2, range(2), attT),
                                                              (2, range(2, 8), fourT))):
                                for k in ks:
                                    mm = pe.matmul(ps[:, 4 * (s % 2) + q, :], wblk[:, b, k, cols], src[:, k - ks[0], toks],
                                                   start=k == ks[0], stop=k == ks[-1])
                                mm.then_inc(m_mm, 1)
                pair(0, True)
                with pe.Fori(1, KT // 2) as j:
                    pair(j)

            @block.scalar
            def _(act):
                def pair(j, first=False):
                    for s in range(SUB):
                        for q in range(2):
                            act.wait_ge(m_mm, (j * SUB + s) * 4 + q + 1)
                            if q == 0 and (s >= 2 or not first):
                                act.wait_ge(m_gat, (j * SUB + s - 1) * 2)
                            act.nop(nofuse=True)
                            act.activation(sig[:, s % 2, q, :], ps[:, 4 * (s % 2) + q, :], ACT.Sigmoid,
                                           bias=bg[:, bass.ds(j * 2 + (q * KT + s // NCH), 1)]).then_inc(m_sig, 1)
                pair(0, True)
                with act.Fori(1, KT // 2) as j:
                    pair(j)

            @block.vector
            def _(dve):
                def pair(j, first=False):
                    for s in range(SUB):
                        n = j * SUB + s
                        for q in range(2):
                            dve.wait_ge(m_sig, n * 2 + q + 1)
                            dve.wait_ge(m_mm, n * 4 + q + 3)
                            if q == 0 and (s >= 2 or not first):
                                dve.wait_ge(m_mix, n - 1)
                            dve.tensor_tensor(gated[:, s % 2, q, :], ps[:, 4 * (s % 2) + 2 + q, :], sig[:, s % 2, q, :],
                                              ALU.mult).then_inc(m_gat, 1)
                        dve.wait_ge(m_gat, n * 2 + 2)
                        c = s % NCH
                        dve.tensor_tensor(mixT[:, bass.ds(j * 2 + s // NCH, 1), c * CH:(c + 1) * CH].rearrange("p o t -> p (o t)"),
                                          gated[:, s % 2, 0, :], gated[:, s % 2, 1, :], ALU.add).then_inc(m_mix, 1)
                pair(0, True)
                with dve.Fori(1, KT // 2) as j:
                    pair(j)

        raw_ld = sems("raw_ld", 4)
        r_g2, r_x, r_st = sem("r_g2"), sems("r_x", 2), sems("r_st", 2)
        r_y, r_x2, r_ssq, r_var, r_std, r_rstd, r_xn = (sem(n) for n in ("r_y", "r_x2", "r_ssq", "r_var", "r_std", "r_rstd", "r_xn"))
        r_T, r_TevA, r_TevD, r_lg, r_sm, r_exp, r_af, r_aT, r_aev = (sem(n) for n in (
            "r_T", "r_TevA", "r_TevD", "r_lg", "r_sm", "r_exp", "r_af", "r_aT", "r_aev"))
        r_top, r_idf, r_iT, r_fin = (sem(n) for n in ("r_top", "r_idf", "r_iT", "r_fin"))

        def load_unit(sp, e, j):
            for i in range(2):
                if j < 8:
                    dst = raw[:, j % 4, 8 * i:8 * i + 8, :]
                    src = (w_eg, w_eu)[i][0, bass.ds(e, 1), :, j * WB:(j + 1) * WB]
                else:
                    dst = raw[:, j % 4, 8 * i:8 * i + 8, :].rearrange("p a n -> p (a n)").rearrange("p (k n) -> p k n", k=4)
                    row, c = (j % 2) * D + i * CH, (j - 8) // 2 * CH
                    src = w_ed[0, bass.ds(e, 1), row:row + CH, c:c + CH]
                sp.dma_start(dst, src.rearrange("o (k p) n -> p (o k) n", p=P)).then_inc(raw_ld[j % 4], 16)

        with nc.Block() as block:
            @block.sync
            def _(sp):
                sp.dma_start(g2[:, :], norm2_g.partition_broadcast(P)).then_inc(r_g2, 16)
                for t in range(2):
                    sp.dma_start(xres[:, t, :], x[t * P:(t + 1) * P, :]).then_inc(r_x[t], 16)
                for j in range(3):
                    load_unit(sp, 0, j)
                for t in range(NT):
                    rows = slice(t * P, (t + 1) * P)
                    sp.wait_ge(r_xn, t + 1)
                    sp.dma_start(resid[rows, :], xres[:, t % 2, :]).then_inc(r_st[t % 2], 16)
                    sp.dma_start(normed[rows, :], xn2[:, t % 2, :]).then_inc(r_st[t % 2], 16)
                    if t + 2 < NT:
                        sp.wait_ge(r_st[t % 2], 32 * (t // 2 + 1))
                        sp.dma_start(xres[:, t % 2, :], x[(t + 2) * P:(t + 3) * P, :]).then_inc(r_x[t % 2], 16)
                for b in range(2):
                    sp.wait_ge(r_st[b], 32 * (NT // 2))

            @block.tensor
            def _(pe):
                def out(t):
                    if t == 0:
                        for b in range(3):
                            pe.wait_ge(w_loaded[b], gate_block_at(b, 3) + 16)
                        pe.wait_ge(w_loaded[3], 16)
                    if t:
                        pe.wait_ge(r_x2, 2 * t)
                    for nb in range(4):
                        for k in range(KT):
                            mm = pe.matmul(ps[:, nb // 2, (nb % 2) * WB:(nb % 2 + 1) * WB], mixT[:, k, t * P:(t + 1) * P],
                                           wblk[:, nb, k, :], start=k == 0, stop=k == KT - 1)
                        if nb % 2:
                            mm.then_inc(r_y, 1)

                def turn(t):
                    pe.wait_ge(r_xn, t + 1)
                    if t:
                        pe.wait_ge(r_TevA, t)
                        pe.wait_ge(r_TevD, t)
                    for k in range(KT):
                        mm = pe.transpose(ps[:, 2 + k // 4, (k % 4) * P:(k % 4 + 1) * P], xn2[:, t % 2, k * P:(k + 1) * P], ident[:, :])
                        if k % 4 == 3:
                            mm.then_inc(r_T, 1)

                def logits(t):
                    pe.wait_ge(r_TevA, t + 1)
                    pe.wait_ge(r_TevD, t + 1)
                    if t:
                        pe.wait_ge(r_exp, t)
                    for k in range(KT):
                        mm = pe.matmul(ps[:, 4, 0:E], xn2T[:, t % 2, k, :], wr[:, k, :], start=k == 0, stop=k == KT - 1)
                    mm.then_inc(r_lg, 1)

                def turn_aff(t):
                    pe.wait_ge(r_af, 2 * (t + 1))
                    if t:
                        pe.wait_ge(r_aev, t)
                    pe.transpose(ps[0:E, 5, 0:P], atok[:, t % 2, :], ident[:, :]).then_inc(r_aT, 1)

                for t in range(NT + 3):
                    if t < NT:
                        out(t)
                    if 0 <= t - 1 < NT:
                        turn(t - 1)
                    if 0 <= t - 2 < NT:
                        logits(t - 2)
                    if 0 <= t - 3 < NT:
                        turn_aff(t - 3)
                for s in range(2):
                    pe.wait_ge(r_idf, s + 1)
                    cap = CAPS[s]
                    pe.transpose(ps[0:cap, 6 + s, 0:E], vals[s][:, :], ident[0:E, 0:E])
                    pe.transpose(ps[0:cap, 6 + s, E:2 * E], idxf[s][:, :], ident[0:E, 0:E]).then_inc(r_iT, 1)

            @block.scalar
            def _(act):
                def norm(t):
                    act.wait_ge(r_x2, 2 * (t + 1))
                    if t:
                        act.wait_ge(r_ssq, t)
                    act.activation(junk2[:, :], xres[:, t % 2, :], ACT.Square, accum_out=stat[:, 0:1]).then_inc(r_ssq, 1)
                    act.wait_ge(r_var, t + 1)
                    act.activation(stat[:, 2:3], stat[:, 1:2], ACT.Sqrt).then_inc(r_std, 1)

                def turned(t):
                    act.wait_ge(r_T, 2 * t + 1)
                    if t >= 2:
                        act.wait_ge(r_lg, t - 1)
                    act.activation(xn2T[:, t % 2, 0:4, :], ps[:, 2, :].rearrange("p (k t) -> p k t", k=4), ACT.Copy).then_inc(r_TevA, 1)

                def softmax(t):
                    act.wait_ge(r_sm, t + 1)
                    act.activation(stat[:, 32 + 16 * (t % 2):48 + 16 * (t % 2)], ps[:, 4, 0:E], ACT.Exp, bias=stat[:, 5:6],
                                   accum_out=stat[:, 6:7]).then_inc(r_exp, 1)

                for t in range(NT + 2):
                    if t < NT:
                        norm(t)
                    if 0 <= t - 1 < NT:
                        turned(t - 1)
                    if 0 <= t - 2 < NT:
                        softmax(t - 2)

            @block.vector
            def _(dve):
                dve.wait_ge(r_g2, 16)

                def norm(t):
                    dve.wait_ge(r_x[t % 2], 16 * (t // 2 + 1))
                    for h in range(2):
                        dve.wait_ge(r_y, 2 * t + h + 1)
                        half = xres[:, t % 2, h * CH:(h + 1) * CH]
                        dve.tensor_tensor(half, half, ps[:, h, :], ALU.add).then_inc(r_x2, 1)
                    dve.wait_ge(r_ssq, t + 1)
                    dve.tensor_scalar(stat[:, 1:2], stat[:, 0:1], 1.0 / D, EPS, ALU.mult, ALU.add).then_inc(r_var, 1)
                    dve.wait_ge(r_std, t + 1)
                    dve.reciprocal(stat[:, 3:4], stat[:, 2:3]).then_inc(r_rstd, 1)
                    dve.wait_ge(r_rstd, t + 1)
                    if t >= 2:
                        dve.wait_ge(r_T, 2 * (t - 1))
                        dve.wait_ge(r_st[t % 2], 32 * (t // 2))
                    dve.scalar_tensor_tensor(out=xn2[:, t % 2, :], in0=xres[:, t % 2, :], scalar=stat[:, 3:4], in1=g2[:, :],
                                             op0=ALU.mult, op1=ALU.mult).then_inc(r_xn, 1)

                def turned(t):
                    dve.wait_ge(r_T, 2 * t + 2)
                    if t >= 2:
                        dve.wait_ge(r_lg, t - 1)
                    dve.tensor_copy(xn2T[:, t % 2, 4:8, :], ps[:, 3, :].rearrange("p (k t) -> p k t", k=4)).then_inc(r_TevD, 1)

                def softmax(t):
                    dve.wait_ge(r_lg, t + 1)
                    dve.tensor_reduce(stat[:, 5:6], ps[:, 4, 0:E], AX.X, ALU.max, negate=True).then_inc(r_sm, 1)
                    dve.wait_ge(r_exp, t + 1)
                    dve.reciprocal(stat[:, 7:8], stat[:, 6:7]).then_inc(r_af, 1)
                    dve.wait_ge(r_af, 2 * t + 1)
                    if t >= 2:
                        dve.wait_ge(r_aT, t - 1)
                    dve.tensor_scalar(atok[:, t % 2, :], stat[:, 32 + 16 * (t % 2):48 + 16 * (t % 2)], stat[:, 7:8], None,
                                      ALU.mult).then_inc(r_af, 1)

                def keep(t):
                    s, tile = (0, t) if t < 8 else (1, t - 8)
                    dve.wait_ge(r_aT, t + 1)
                    dve.tensor_copy(aff[s][:, tile * P:(tile + 1) * P], ps[0:E, 5, 0:P]).then_inc(r_aev, 1)

                tops = [0]

                def top(s, r):
                    v = vals[s][:, 8 * r:8 * r + 8]
                    if tops[0] or True:
                        dve.wait_ge(r_top, tops[0])
                    dve.max(v, aff[s][:, :]).then_inc(r_top, 1)
                    dve.wait_ge(r_top, tops[0] + 1)
                    dve.max_index(idxr[s][:, 8 * r:8 * r + 8], v, aff[s][:, :]).then_inc(r_top, 1)
                    dve.wait_ge(r_top, tops[0] + 2)
                    dve.match_replace(aff[s][:, :], v, aff[s][:, :], -1.0).then_inc(r_top, 1)
                    tops[0] += 3

                def as_float(s):
                    dve.wait_ge(r_top, tops[0])
                    dve.tensor_scalar(idxf[s][:, :], idxr[s][:, :], float(SEQS[s][0]), None, ALU.add).then_inc(r_idf, 1)

                rounds = list(range(CAPS[0] // 8))
                for t in range(NT + 3):
                    if t < NT:
                        norm(t)
                    if 0 <= t - 1 < NT:
                        turned(t - 1)
                    if 0 <= t - 2 < NT:
                        softmax(t - 2)
                    if 0 <= t - 3 < NT:
                        keep(t - 3)
                    if t >= 11 or t == 10 and False:
                        if t == 11:
                            dve.wait_ge(r_aev, 8)
                        for _ in range(4):
                            if rounds:
                                top(0, rounds.pop(0))
                while rounds:
                    top(0, rounds.pop(0))
                as_float(0)
                dve.wait_ge(r_aev, NT)
                for r in range(CAPS[1] // 8):
                    top(1, r)
                as_float(1)
                for s in range(2):
                    cap = CAPS[s]
                    dve.wait_ge(r_iT, s + 1)
                    dve.tensor_copy(gate[s][:, :], ps[0:cap, 6 + s, 0:E])
                    dve.tensor_copy(idx[s][:, :], ps[0:cap, 6 + s, E:2 * E]).then_inc(r_fin, 1)
                dve.wait_ge(r_fin, 2)

        SUBS = FT + 8
        AHEAD = 4
        x_idx, x_in, x_T, x_high, x_cut = (sem(n) for n in ("x_idx", "x_in", "x_T", "x_high", "x_cut"))
        w_high, w_cut, w_used = sem("w_high"), sem("w_cut"), sem("w_used")
        gu_low, gu_sum, gu_sig, gu_g, h_done, h_high, h_cut = (sem(n) for n in (
            "gu_low", "gu_sum", "gu_sig", "gu_g", "h_done", "h_high", "h_cut"))
        y_low, y_sum, y_ev, sc_idx, scat = (sem(n) for n in ("y_low", "y_sum", "y_ev", "sc_idx", "scat"))
        GU_PAIRS, Y_PAIRS = 2, 2
        H_LOW, H_HIGH, H_SAMPLE = slice(0, P), slice(P, 2 * P), slice(2 * P, 3 * P)

        def raw_part(q):
            unit = raw[:, q // 2 % 4, :, :]
            if q < FT:
                return unit[:, :, (q % 2) * P:(q % 2 + 1) * P]
            return unit[:, 8 * (q % 2):8 * (q % 2) + 8, :].rearrange("p a n -> p (a n)")

        def cut_part(w, q):
            part = w[:, q % AHEAD, :]
            return part.rearrange("p (a n) -> p a n", n=P) if q < FT else part

        with nc.Block() as block:
            @block.sync
            def _(sp):
                load_unit(sp, 0, 3)
                def late(e):
                    for j in range(4, 12):
                        sp.wait_ge(w_cut, e * SUBS + 2 * (j - 3))
                        sp.nop(nofuse=True)
                        load_unit(sp, e, j)
                with sp.Fori(0, E - 1) as e:
                    late(e)
                    for j in range(4):
                        sp.wait_ge(w_cut, e * SUBS + 2 * (j + 9))
                        sp.nop(nofuse=True)
                        load_unit(sp, e + 1, j)
                late(E - 1)

            @block.gpsimd
            def _(pool):
                def pick(dst, e, done, n):
                    for s in range(2):
                        pool.tensor_copy(dst[s][:, :], idx[s][:, bass.ds(e, 1)]).then_inc(done, 1)
                    pool.wait_ge(done, n)
                    pool.nop(nofuse=True)

                def gather(e, n):
                    pick(idx_in, e, x_idx, n)
                    for s in range(2):
                        pool.indirect_dma_start(xg[s][:, :], None, normed, bass.IndirectOffsetOnAxis(ap=idx_in[s][:, 0:1], axis=0)) \
                            .then_inc(x_in, 16)

                def scatter(e, n, before):
                    pool.wait_ge(y_ev, n * 2 + Y_PAIRS)
                    if before is not None:
                        pool.wait_ge(scat, before)
                    pick(idx_out, e, sc_idx, n * 2)
                    for s in range(2):
                        pool.indirect_dma_start(resid, bass.IndirectOffsetOnAxis(ap=idx_out[s][:, 0:1], axis=0), ytok[s][:, :], None,
                                                compute_op=ALU.add).then_inc(scat, 16)
                gather(0, 2)
                with pool.Fori(0, E - 1) as e:
                    pool.wait_ge(x_T, (e + 1) * 2)
                    gather(e + 1, (e + 2) * 2)
                    scatter(e, e + 1, e * 32)
                scatter(E - 1, E, (E - 1) * 32)
                pool.wait_ge(scat, E * 32)

            @block.tensor
            def _(pe):
                def turn_tokens(n):
                    pe.wait_ge(x_in, (n + 1) * 32)
                    pe.wait_ge(gu_sum, n * FT + GU_PAIRS)
                    for k in range(KT):
                        at_col = (k % 2) * CAP
                        pe.transpose(ps[:, k // 2, at_col:at_col + CAPS[0]], xg[0][:, k * P:(k + 1) * P], ident[:, :])
                        mm = pe.transpose(ps[:, k // 2, at_col + CAPS[0]:at_col + CAP], xg[1][:, k * P:(k + 1) * P],
                                          ident[0:CAPS[1], 0:CAPS[1]])
                        if k % 4 == 3:
                            mm.then_inc(x_T, 1)

                def gate_up(e):
                    pe.wait_ge(x_cut, (e + 1) * 2)
                    for q in range(FT):
                        pe.wait_ge(w_cut, e * SUBS + (q + 1))
                        pe.wait_ge(gu_sum, e * FT + (q + 1))
                        for part in range(2):
                            bank = 2 * (q % 2) + part
                            for k in range(KT):
                                tile = slice((8 * part + k) * P, (8 * part + k + 1) * P)
                                pe.matmul(ps[:, bank, 0:2 * CAP], wh[:, q % AHEAD, tile],
                                          xsplit[:, k, :, :].rearrange("p s t -> p (s t)"), start=k == 0, stop=False)
                                mm = pe.matmul(ps[:, bank, CAP:2 * CAP], wl[:, q % AHEAD, tile], xsplit[:, k, 0, :],
                                               start=False, stop=k == KT - 1)
                        mm.then_inc(w_used, 1)

                def down(e, last):
                    for i in range(8):
                        q, c = FT + i, i // 4
                        pe.wait_ge(w_cut, e * SUBS + (q + 1))
                        if i < 4:
                            pe.wait_ge(h_cut, e * 8 + 2 * (i + 1))
                        if i % 4 == 0:
                            pe.wait_ge(y_ev, e * 2 + (c + 1))
                        for kk in range(4):
                            k = 4 * (i % 4) + kk
                            cols = slice(kk * CH, (kk + 1) * CH)
                            first, end = k == 0, k == FT - 1
                            prompt, sample = ps[:, 4 + 2 * c, :], ps[:, 5 + 2 * c, :]
                            pe.matmul(prompt, hsplit[:, k, H_LOW], wh[:, q % AHEAD, cols], start=first, stop=False)
                            pe.matmul(prompt, hsplit[:, k, H_HIGH], wh[:, q % AHEAD, cols], start=False, stop=False)
                            pe.matmul(prompt, hsplit[:, k, H_HIGH], wl[:, q % AHEAD, cols], start=False, stop=end)
                            pe.matmul(sample, hsplit[:, k, H_SAMPLE], wh[:, q % AHEAD, cols], start=first, stop=False)
                            mm = pe.matmul(sample, hsplit[:, k, H_SAMPLE], wl[:, q % AHEAD, cols], start=False, stop=end)
                        mm.then_inc(w_used, 1)
                        if i == 1 and not last:
                            turn_tokens(e + 1)

                turn_tokens(0)
                with pe.Fori(0, E - 1) as e:
                    gate_up(e)
                    down(e, False)
                gate_up(E - 1)
                down(E - 1, True)

            @block.scalar
            def _(act):
                act.sem_inc(y_ev, Y_PAIRS)

                def high_weights(e, q):
                    if q % 2 == 0:
                        j = q // 2
                        act.wait_ge(raw_ld[j % 4], (e * 3 + (j // 4 + 1)) * 32)
                    act.activation(cut_part(wh, q), raw_part(q), ACT.Copy).then_inc(w_high, 1)

                def high_tokens(n):
                    for b in range(2):
                        act.wait_ge(x_T, n * 2 + (b + 1))
                        for i in range(2):
                            k = 4 * b + 2 * i
                            mm = act.activation(xsplit[:, k:k + 2, 0, :], ps[:, k // 2, 0:2 * CAP].rearrange("p (k t) -> p k t", k=2), ACT.Copy)
                        mm.then_inc(x_high, 1)

                def expert(e, last):
                    for q in range(SUBS):
                        act.wait_ge(w_used, e * SUBS + (q + 1))
                        if q < FT:
                            act.activation(low[:, q % 2, :, :], ps[:, 2 * (q % 2):2 * (q % 2) + 2, CAP:2 * CAP], ACT.Copy).then_inc(gu_low, 1)
                        if q + AHEAD < SUBS:
                            high_weights(e, q + AHEAD)
                        elif not last:
                            high_weights(e + 1, q + AHEAD - SUBS)
                        if q < FT:
                            act.wait_ge(gu_sum, e * FT + (q + 1 + GU_PAIRS))
                            act.activation(sg[:, q % 2, :], gu[:, q % 2, 0, :], ACT.Sigmoid).then_inc(gu_sig, 1)
                        if 2 <= q <= FT and q % 2 == 0:
                            act.wait_ge(h_done, e * FT + q)
                            act.activation(hsplit[:, q - 2:q, P:P + CAP], h[:, (q - 2) % 4:(q - 2) % 4 + 2, :], ACT.Copy).then_inc(h_high, 1)
                        if q == FT + 1 and not last:
                            high_tokens(e + 1)
                        if q in (FT + 3, FT + 7):
                            c = (q - FT) // 4
                            act.activation(ylow[:, c, :], ps[CAPS[1]:2 * CAPS[1], 5 + 2 * c, :], ACT.Copy).then_inc(y_low, 1)
                high_tokens(0)
                for q in range(AHEAD):
                    high_weights(0, q)
                with act.Fori(0, E - 1) as e:
                    expert(e, False)
                expert(E - 1, True)

            @block.vector
            def _(dve):
                dve.sem_inc(gu_sum, GU_PAIRS)

                def low_weights(e, q):
                    dve.wait_ge(w_high, e * SUBS + (q + 1))
                    dve.tensor_tensor(cut_part(wl, q), raw_part(q), cut_part(wh, q).bitcast(F32), ALU.subtract).then_inc(w_cut, 1)

                def low_tokens(n):
                    for b in range(2):
                        dve.wait_ge(x_high, n * 2 + (b + 1))
                        for i in range(2):
                            k = 4 * b + 2 * i
                            ins = dve.tensor_tensor(xsplit[:, k:k + 2, 1, :], ps[:, k // 2, 0:2 * CAP].rearrange("p (k t) -> p k t", k=2),
                                                    xsplit[:, k:k + 2, 0, :].bitcast(F32), ALU.subtract)
                        ins.then_inc(x_cut, 1)

                def expert(e, last):
                    for q in range(SUBS):
                        if q < FT:
                            pair = ps[:, 2 * (q % 2):2 * (q % 2) + 2, 0:CAP]
                            dve.wait_ge(gu_low, e * FT + (q + 1))
                            dve.tensor_tensor(gu[:, q % 2, :, :], pair, low[:, q % 2, :, :], ALU.add).then_inc(gu_sum, 1)
                        if q + AHEAD - 1 < SUBS:
                            low_weights(e, q + AHEAD - 1)
                        elif not last:
                            low_weights(e + 1, q + AHEAD - 1 - SUBS)
                        if q < FT:
                            dve.wait_ge(gu_sig, e * FT + (q + 1))
                            dve.tensor_tensor(sgg[:, q % 2, :], gu[:, q % 2, 0, :], sg[:, q % 2, :], ALU.mult).then_inc(gu_g, 1)
                            dve.wait_ge(gu_g, e * FT + (q + 1))
                            dve.tensor_tensor(h[:, q % 4, :], gu[:, q % 2, 1, :], sgg[:, q % 2, :], ALU.mult).then_inc(h_done, 1)
                        if 2 <= q <= FT and q % 2 == 0:
                            dve.wait_ge(h_high, e * 8 + q // 2)
                            two = (q - 2) % 4
                            for at_h, at_src, at_high, n in ((0, 0, P, CAPS[0]), (P + CAP, CAPS[0], 2 * P, CAPS[1])):
                                ins = dve.tensor_tensor(hsplit[:, q - 2:q, at_h:at_h + n], h[:, two:two + 2, at_src:at_src + n],
                                                        hsplit[:, q - 2:q, at_high:at_high + n].bitcast(F32), ALU.subtract)
                            ins.then_inc(h_cut, 1)
                        if q == FT + 1 and not last:
                            low_tokens(e + 1)
                        if q in (FT + 3, FT + 7):
                            c = (q - FT) // 4
                            cols = slice(c * CH, (c + 1) * CH)
                            dve.wait_ge(y_low, e * 2 + (c + 1))
                            if c == 0:
                                dve.wait_ge(scat, e * 32)
                            dve.tensor_tensor(ysum[:, c, :], ps[0:CAPS[1], 5 + 2 * c, :], ylow[:, c, :], ALU.add).then_inc(y_sum, 1)
                            dve.tensor_scalar(ytok[0][:, cols], ps[:, 4 + 2 * c, :], gate[0][:, bass.ds(e, 1)], None, ALU.mult)
                            dve.wait_ge(y_sum, e * 2 + (c + 1))
                            dve.tensor_scalar(ytok[1][:, cols], ysum[:, c, :], gate[1][:, bass.ds(e, 1)], None, ALU.mult).then_inc(y_ev, 1)
                low_tokens(0)
                for q in range(AHEAD - 1):
                    low_weights(0, q)
                with dve.Fori(0, E - 1) as e:
                    expert(e, False)
                expert(E - 1, True)

        l_g, l_ld, l_st = sem("l_g"), sems("l_ld", 4), sems("l_st", 4)
        l_ssq, l_var, l_std, l_rstd, l_y = (sem(n) for n in ("l_ssq", "l_var", "l_std", "l_rstd", "l_y"))
        LT = NT // 4

        with nc.Block() as block:
            @block.sync
            def _(sp):
                sp.dma_start(gF[:, :], final_g.rearrange("(o d) -> o d", o=1).partition_broadcast(P)).then_inc(l_g, 16)
                for s in range(4):
                    sp.dma_start(fin[:, s, :], resid[s * P:(s + 1) * P, :]).then_inc(l_ld[s], 16)
                with sp.Fori(1, LT) as i:
                    for s in range(4):
                        sp.wait_ge(l_y, i * 4 + (s - 3))
                        sp.dma_start(fin[:, s, :], resid[bass.ds(i * 4 * P + s * P, P), :]).then_inc(l_ld[s], 16)

            @block.scalar
            def _(act):
                def squares(i):
                    for s in range(4):
                        act.wait_ge(l_ld[s], (i + 1) * 16)
                        act.activation(fout[:, s, :], fin[:, s, :], ACT.Square, accum_out=stat[:, s:s + 1]).then_inc(l_ssq, 1)

                def roots(i):
                    for s in range(4):
                        act.wait_ge(l_var, i * 4 + (s + 1))
                        act.activation(stat[:, 8 + s:9 + s], stat[:, 4 + s:5 + s], ACT.Sqrt).then_inc(l_std, 1)

                def rows(i):
                    for s in range(4):
                        act.wait_ge(l_y, i * 4 + (s + 1))
                        act.dma_start(y[bass.ds(i * 4 * P + s * P, P), :], fout[:, s, :]).then_inc(l_st[s], 16)
                squares(0)
                roots(0)
                rows(0)
                with act.Fori(1, LT) as i:
                    for s in range(4):
                        act.wait_ge(l_st[s], i * 16)
                    squares(i)
                    roots(i)
                    rows(i)
                for s in range(4):
                    act.wait_ge(l_st[s], LT * 16)

            @block.vector
            def _(dve):
                dve.wait_ge(l_g, 16)
                with dve.Fori(0, LT) as i:
                    for s in range(4):
                        dve.wait_ge(l_ssq, i * 4 + (s + 1))
                        dve.tensor_scalar(stat[:, 4 + s:5 + s], stat[:, s:s + 1], 1.0 / D, EPS, ALU.mult, ALU.add).then_inc(l_var, 1)
                    for s in range(4):
                        dve.wait_ge(l_std, i * 4 + (s + 1))
                        dve.reciprocal(stat[:, 12 + s:13 + s], stat[:, 8 + s:9 + s]).then_inc(l_rstd, 1)
                        dve.wait_ge(l_rstd, i * 4 + (s + 1))
                        dve.scalar_tensor_tensor(out=fout[:, s, :], in0=fin[:, s, :], scalar=stat[:, 12 + s:13 + s], in1=gF[:, :],
                                                 op0=ALU.mult, op1=ALU.mult).then_inc(l_y, 1)


_INS = ['rel_bias', 'norm1_g', 'w_in', 'w_attn_br', 'w_four_br', 'w_gate', 'b_gate', 'w_out', 'norm2_g', 'w_router',
        'w_exp_gate', 'w_exp_up', 'w_exp_down', 'final_g']


def kernel(**inputs):
    import numpy as _np
    import concourse.bacc as _bacc
    from concourse import mybir as _mybir
    from concourse.bass_utils import run_bass_kernel_spmd as _run

    nc = _bacc.Bacc("TRN2", target_bir_lowering=False, num_devices=1)
    arrays, args = {}, []

    def add(name, a):
        a = _np.ascontiguousarray(a)
        arrays[name] = a
        args.append(nc.dram_tensor(name, a.shape, _mybir.dt.from_np(a.dtype), kind="ExternalInput").ap())

    xp, xs = _np.asarray(inputs["x_prompt"]), _np.asarray(inputs["x_sample"])
    add("in_x_dram", _np.concatenate([xp.reshape(-1, D), xs.reshape(-1, D)], 0))
    for name in _INS:
        a = _np.asarray(inputs[name])
        add(f"in_{name}_dram", a.reshape(-1, P).T if name == "b_gate" else a)
    add("c_identity_dram", _np.eye(P, dtype=_np.float32))
    add("c_one_hot_dram", bucket_one_hot())
    add("c_pos_prompt_dram", position_table(SEQS[0][1]))
    add("c_pos_sample_dram", position_table(SEQS[1][1]))
    add("c_chan_dram", channel_table())
    out = nc.dram_tensor("out_y_dram", (TOKENS, D), _mybir.dt.float32, kind="ExternalOutput").ap()
    encoder(nc, *args, out)
    r = _run(nc, [arrays], core_ids=[0])
    got = r.results[0]["out_y_dram"]
    n = SEQS[0][1]
    return got[:n].reshape(xp.shape), got[n:].reshape(xs.shape)
```

```python
from collections import namedtuple
from contextlib import ExitStack

import concourse.bass as bass
import numpy as np
from concourse import mybir

F32 = mybir.dt.float32
F32R = mybir.dt.float32r
U32 = mybir.dt.uint32
ALU = mybir.AluOpType
ACT = mybir.ActivationFunctionType
AX = mybir.AxisListType

P = 128
D = 1024
KT = D // P
SEQS = ((0, 1024), (1024, 512))
TOKENS = 1536
NT = TOKENS // P
CH = 512
NCH = TOKENS // CH
HD = 64
HEADS = 4
GROUPS = ((128, 1), (512, 4), (2048, 16))
NG = len(GROUPS)
HALF = 64
GW = HEADS * HD
ATT_W = NG * GW
F_GROUPS = 6
F_W = F_GROUPS * P
BUCKETS = 32
MAX_DISTANCE = 1024
E = 16
CAPS = tuple(2 * n // E for _, n in SEQS)
CAP = sum(CAPS)
FF = 2048
FT = FF // P
EPS = 1e-6
NEG = -1e30
WB = 256
AROW = GW + 2 * HEADS
TOEP = 384
KB = 1024


TABLES = ((0, 1), (1, 1)) + tuple((2, P * GROUPS[2][1] // n) for _, n in SEQS)



def bucket_of(rel):
    nb = BUCKETS // 2
    exact = nb // 2
    n = np.abs(rel)
    large = exact + (np.log(np.maximum(n, exact) / exact) / np.log(MAX_DISTANCE / exact) * (nb - exact)).astype(np.int32)
    return (rel > 0).astype(np.int32) * nb + np.where(n < exact, n, np.minimum(large, nb - 1))


def bucket_one_hot():
    table = np.zeros((BUCKETS + 1, len(TABLES), TOEP), np.float32)
    place = np.arange(TOEP) - 191
    for i, (g, classes) in enumerate(TABLES):
        dil = GROUPS[g][1]
        seen = (place % classes == 0) & (np.abs(place) <= HALF * classes)
        row = np.where(seen, bucket_of(dil // classes * place), BUCKETS)
        table[row, i, np.arange(TOEP)] = 1.0
    return table.reshape(BUCKETS + 1, len(TABLES) * TOEP)


def position_table(n):
    t = np.concatenate([np.arange(0, n, 2), np.arange(1, n, 2)])
    angle = 2 * np.pi * ((t[:, None] * np.arange(n // 2)[None, :]) % n) / n
    both = np.stack([np.cos(angle), np.sin(angle)], 1) / np.sqrt(n * P)
    return both.astype(np.float32)


def channel_table():
    c = np.arange(P)
    angle = 2 * np.pi * ((c[:, None] * c[None, :]) % P) / P
    return np.stack([np.cos(angle), -np.sin(angle)], 1).astype(np.float32)



QueryTile = namedtuple("QueryTile", "s r classes q0 k0 keys bias")


def attention_plan(g):
    dil = GROUPS[g][1]
    tiles, values = [], []
    for s, (base, n) in enumerate(SEQS):
        length = n // dil
        if length > P:
            cuts = [0] + list(range(HALF, length, P)) + [length]
            for r in range(dil):
                first = len(values)
                for a, b in zip(cuts, cuts[1:]):
                    values.append((s, r, 1, min(a, length - P)))
                for i in range(length // P):
                    keys = [(first + i + c, cuts[i + c + 1] - cuts[i + c], max(0, cuts[i + c] - (length - P))) for c in range(2)]
                    tiles.append(QueryTile(s=s, r=r, classes=1, q0=i * P, k0=cuts[i], keys=keys,
                                                 bias=cuts[i] - i * P + HALF))
        else:
            classes = P // length
            for r in range(dil // classes):
                values.append((s, r, classes, 0))
                tiles.append(QueryTile(s=s, r=r, classes=classes, q0=0, k0=0, keys=[(len(values) - 1, P, 0)], bias=HALF))
    return tiles, values


PLANS = [attention_plan(g) for g in range(NG)]
MAXV = max(len(v) for _, v in PLANS)


def of_class(view, s, g, r, classes, a, n):
    base, size = SEQS[s]
    return view[:, base:base + size].rearrange("p (n r) -> p r n", r=GROUPS[g][1] // classes)[:, r, a:a + n]


def encoder(nc, x, rel_bias, norm1_g, w_in, w_attn_br, w_four_br, w_gate, b_gate, w_out, norm2_g,
            w_router, w_eg, w_eu, w_ed, final_g, identity, one_hot, pos_prompt, pos_sample, chan, y):
    ctx = ExitStack()
    with ctx:
        ARENA = 17 * KB

        def at(name, kb, shape, dt=F32):
            return nc.alloc_sbuf_tensor_at(name, list(shape), dt, offset=int(ARENA + kb * KB))

        def sem(name):
            return ctx.enter_context(nc.semaphore(name))

        def sems(name, n):
            return [sem(f"{name}{i}") for i in range(n)]

        xnT = at("xnT", 0, [P, KT, TOKENS])
        attT = at("attT", 48, [P, GW // P, TOKENS])
        fourT = at("fourT", 60, [P, F_GROUPS, TOKENS])
        xlow = at("xlow", 0, [P, KT, TOKENS], F32R)
        xhigh = at("xhigh", 48, [P, KT, TOKENS], F32R)
        wraw = at("wraw", 96, [P, 2, KT, WB])
        wlow = at("wlow", 96, [P, 2, KT, WB], F32R)
        whigh = at("whigh", 112, [P, 2, KT, WB], F32R)
        xin = at("xin", 128, [P, 4, D])
        xs = at("xs", 144, [P, 2, D])
        g1 = at("g1", 152, [P, D])
        junk = at("junk", 156, [P, D])
        hot = at("hot", 160, [BUCKETS + 1, len(TABLES) * TOEP])
        hotr = at("hotr", 160, [BUCKETS + 1, len(TABLES) * TOEP], F32R)
        relhigh = at("relhigh", 167, [BUCKETS + 1, NG * HEADS], F32R)
        rellow = at("rellow", 168, [BUCKETS + 1, NG * HEADS], F32R)
        toep_sb = at("toep_sb", 176, [P, len(TABLES) * HEADS, TOEP])
        qT = at("qT", 128, [P, 2, TOKENS])
        kT = at("kT", 140, [P, 2, TOKENS])
        V = at("V", 152, [P, MAXV, GW])
        band = at("band", 168, [P, 2 * HEADS, 2 * P])
        same = at("same", 176, [P, 2, HEADS, P])
        sc = at("sc", 180, [P, 3, HEADS, 2 * P])
        pT = at("pT", 192, [P, 2, HEADS, 2, P])
        orow = at("orow", 200, [P, 3, AROW])
        rowstat = at("rowstat", 203.125, [P, 4, 2 * HEADS])
        u = at("u", 128, [P, NT, F_W])
        tabP = at("tabP", 96, [P, 8, 2, 512])
        tabS = at("tabS", 164, [P, 4, 2, 256])
        eo = at("eo", 172, [P, 4, 512])
        fe = at("fe", 180, [P, 2, 512])
        comb = at("comb", 184, [P, 2, NG, AROW])
        attk = at("attk", 190.25, [P, 2, GW])
        cw = at("cw", 192.25, [P, 64])
        chan_sb = at("chan_sb", 192.5, [P, 2, P])
        alow = at("alow", 48, [P, GW // P, TOKENS], F32R)
        flow = at("flow", 60, [P, F_GROUPS, TOKENS], F32R)
        graw = at("graw", 96, [P, 4, KT, P])
        glow = at("glow", 96, [P, 4, KT, P], F32R)
        ghigh = at("ghigh", 112, [P, 4, KT, P], F32R)
        mix0 = at("mix0", 128, [P, KT, CH])
        xh = at("xh", 144, [P, KT, CH], F32R)
        ah = at("ah", 160, [P, GW // P, CH], F32R)
        fh = at("fh", 164, [P, F_GROUPS, CH], F32R)
        sig = at("sig", 176, [P, 2, 2, CH])
        gated = at("gated", 184, [P, 2, 2, CH])
        xres = at("xres", 144, [P, 2, D])
        xn2 = at("xn2", 152, [P, 2, D])
        xn2T = at("xn2T", 160, [P, 2, KT, P])
        g2 = at("g2", 168, [P, D])
        junk2 = at("junk2", 172, [P, D])
        aff = [at("affP", 192, [E, 1024]), at("affS", 196, [E, 512])]
        vals = [at("valsP", 198, [E, CAPS[0]]), at("valsS", 198.5, [E, CAPS[1]])]
        idxr = [at("idxrP", 199, [E, CAPS[0]], U32), at("idxrS", 199.5, [E, CAPS[1]], U32)]
        idxf = [at("idxfP", 200, [E, CAPS[0]]), at("idxfS", 200.5, [E, CAPS[1]])]
        atok = at("atok", 201, [P, 2, E])
        wh = at("wh", 0, [P, 4, 16 * P], F32R)
        wl = at("wl", 32, [P, 4, 16 * P], F32R)
        hsplit = at("hsplit", 64, [P, FT, 2 * CAP], F32R)
        xg = [at("xgP", 88, [CAPS[0], D]), at("xgS", 92, [CAPS[1], D])]
        raw = [at(f"raw{i}", kb, [P, 16, WB]) for i, kb in enumerate((96, 112, 176, 128))]
        ytok = [at("ytokP", 144, [CAPS[0], D]), at("ytokS", 148, [CAPS[1], D])]
        xsplit = at("xsplit", 152, [P, KT, 2, CAP], F32R)
        low = at("low", 164, [P, 2, 2, CAP])
        gu = at("gu", 167, [P, 2, 2, CAP])
        sg = at("sg", 170, [P, 2, CAP])
        sgg = at("sgg", 171.5, [P, 2, CAP])
        h = at("h", 173, [P, 4, CAP])
        ylow = at("ylow", 192, [CAPS[1], 2, CH])
        ysum = at("ysum", 196, [CAPS[1], 2, CH])
        fin = at("fin", 0, [P, NT, D])
        fsquare = at("fsquare", 48, [P, 2, D])
        gF = at("gF", 56, [P, D])
        lstat = at("lstat", 60, [P, 4, NT])
        ident = at("ident", 203.25, [P, P])
        bg = at("bg", 203.75, [P, 2 * KT])
        relb = at("relb", 204, [BUCKETS + 1, NG * HEADS])
        wr = at("wr", 204.25, [P, KT, E])
        stat = at("stat", 204.75, [P, 64])
        negm = at("negm", 205, [P, 2, HEADS])
        gate = [at("gateP", 205.25, [CAPS[0], E]), at("gateS", 205.375, [CAPS[1], E])]
        idx = [at("idxP", 205.5, [CAPS[0], E], U32), at("idxS", 205.625, [CAPS[1], E], U32)]
        idx_in = [at("idx_inP", 205.75, [CAPS[0], 1], U32), at("idx_inS", 205.78125, [CAPS[1], 1], U32)]
        idx_out = [at("idx_outP", 205.8125, [CAPS[0], 1], U32), at("idx_outS", 205.84375, [CAPS[1], 1], U32)]

        ps = ctx.enter_context(nc.psum_tensor("ps", [P, 8, 512], F32))

        toep = nc.dram_tensor("toep", [P, len(TABLES) * HEADS, TOEP], F32, kind="Internal").ap()
        attrows = nc.dram_tensor("attrows", [NG, TOKENS, AROW], F32, kind="Internal").ap()
        resid = nc.dram_tensor("resid", [TOKENS, D], F32, kind="Internal").ap()
        normed = nc.dram_tensor("normed", [TOKENS, D], F32, kind="Internal").ap()

        w_loaded = sems("w_loaded", 2)
        b_high, b_cut = sem("b_high"), sem("b_cut")
        g_loaded = sems("g_loaded", 4)
        wo_loaded = sem("wo_loaded")

        def in_block(n):
            return (n % 3) * ATT_W + (n // 3) * WB if n < 9 else 3 * ATT_W + (n - 9) * WB

        def load_in_block(sp, n):
            c = in_block(n)
            sp.dma_start(wraw[:, n % 2, :, :], w_in[0, :, c:c + WB].rearrange("(k p) n -> p k n", p=P)) \
              .then_inc(w_loaded[n % 2], 16)

        def high_block(act, n):
            act.wait_ge(w_loaded[n % 2], 16 * (n // 2 + 1))
            act.activation(whigh[:, n % 2, :, :], wraw[:, n % 2, :, :], ACT.Copy).then_inc(b_high, 1)

        def low_block(dve, n):
            dve.wait_ge(b_high, n + 1)
            dve.tensor_tensor(wlow[:, n % 2, :, :], wraw[:, n % 2, :, :], whigh[:, n % 2, :, :].bitcast(F32),
                              ALU.subtract).then_inc(b_cut, 1)

        def load_piece(sp, i, d, b):
            slot = (3 * d + b) % 4
            for k, end, w, row, col in ((0, 4, w_gate, 0, b * D), (4, 8, w_gate, 4 * P, b * D)) if b < 2 else \
                                       ((0, 2, w_attn_br, 0, 0), (2, 8, w_four_br, 0, 0)):
                src = w[0, row:row + (end - k) * P, bass.ds(i * (4 * P) + (col + d * P), P)]
                sp.dma_start(graw[:, slot, k:end, :], src.rearrange("(k p) n -> p k n", p=P)).then_inc(g_loaded[slot], 16)

        def w_out_at(k):
            return fourT[:, k, 0:D] if k < F_GROUPS else attT[:, k - F_GROUPS, 0:D]

        h_loaded, c_loaded, x_in_ld = sem("h_loaded"), sem("c_loaded"), sems("x_in_ld", 4)
        n_ssq, n_var, n_std, n_rstd, n_xs = (sem(n) for n in ("n_ssq", "n_var", "n_std", "n_rstd", "n_xs"))
        n_T, n_high, n_cut = sem("n_T"), sem("n_high"), sem("n_cut")
        t_masked, t_mm, t_sb, t_sbD, t_out, t_tab, t_rel, t_hot = (sem(n) for n in ("t_masked", "t_mm", "t_sb", "t_sbD", "t_out", "t_tab", "t_rel", "t_hot"))
        ROWS_T = len(TABLES) * HEADS

        with nc.Block() as block:
            @block.sync
            def _(sp):
                sp.dma_start(relb[0:BUCKETS, :], rel_bias).then_inc(h_loaded, 16)
                sp.dma_start(hot[:, :], one_hot).then_inc(h_loaded, 16)
                for s in range(4):
                    sp.dma_start(xin[:, s, :], x[s * P:(s + 1) * P, :]).then_inc(x_in_ld[s], 16)
                    if s == 0:
                        sp.dma_start(g1[:, :], norm1_g.partition_broadcast(P)).then_inc(c_loaded, 16)
                        sp.dma_start(ident[:, :], identity).then_inc(c_loaded, 16)
                sp.dma_start(bg[:, :], b_gate).then_inc(c_loaded, 16)
                sp.dma_start(wr[:, :, :], w_router[0].rearrange("(k p) e -> p k e", p=P)).then_inc(c_loaded, 16)
                for n in range(2):
                    load_in_block(sp, n)
                with sp.Fori(1, NT // 4) as i:
                    for s in range(4):
                        sp.wait_ge(n_xs, i * 4 + (s - 3))
                        sp.dma_start(xin[:, s, :], x[bass.ds(i * 4 * P + s * P, P), :]).then_inc(x_in_ld[s], 16)
                sp.wait_ge(t_sb, ROWS_T // 2)
                sp.wait_ge(t_sbD, ROWS_T // 2)
                sp.dma_start(toep, toep_sb[:, :, :]).then_inc(t_out, 16)

            @block.gpsimd
            def _(pool):
                pool.memset(relb[BUCKETS:BUCKETS + 1, :], NEG).then_inc(t_masked, 1)

            @block.scalar
            def _(act):
                def square(i, s):
                    act.wait_ge(x_in_ld[s], (i + 1) * 16)
                    if s or not isinstance(i, int) or i:
                        act.wait_ge(n_ssq, i * 4 + s)
                    act.activation(junk[:, :], xin[:, s, :], ACT.Square, accum_out=stat[:, s:s + 1]).then_inc(n_ssq, 1)

                def root(i, s):
                    act.wait_ge(n_var, i * 4 + s + 1)
                    act.activation(stat[:, 8 + s:9 + s], stat[:, 4 + s:5 + s], ACT.Sqrt).then_inc(n_std, 1)

                def high(n, s):
                    act.wait_ge(n_T, n + 1)
                    act.activation(xhigh[:, :, bass.ds(n * P, P)],
                                   ps[:, 2 * (s % 2):2 * (s % 2) + 2, :].rearrange("p b (k t) -> p (b k) t", k=4), ACT.Copy).then_inc(n_high, 1)

                def rows(s):
                    for r in (4 * s, 4 * s + 2):
                        act.wait_ge(t_mm, r + 1)
                        act.activation(toep_sb[:, r, :], ps[:, 4 + r % 4, 0:TOEP], ACT.Copy).then_inc(t_sb, 1)

                def body(i):
                    for s in range(4):
                        square(i, s)
                        if isinstance(i, int):
                            rows(s)
                        root(i, s)
                        if s or not isinstance(i, int) or i:
                            high(i * 4 + (s - 1), s - 1)
                act.wait_ge(h_loaded, 32)
                act.activation(hotr[:, :], hot[:, :], ACT.Copy).then_inc(t_hot, 1)
                body(0)
                high_block(act, 0)
                high_block(act, 1)
                with act.Fori(1, NT // 4) as i:
                    body(i)
                high(NT - 1, NT - 1)

            @block.vector
            def _(dve):
                dve.wait_ge(t_masked, 1)
                dve.wait_ge(h_loaded, 32)
                dve.tensor_copy(relhigh[:, :], relb[:, :]).then_inc(t_rel, 1)
                dve.wait_ge(t_rel, 1)
                dve.tensor_tensor(rellow[:, :], relb[:, :], relhigh[:, :].bitcast(F32), ALU.subtract).then_inc(t_rel, 1)
                dve.wait_ge(c_loaded, 16 * 4)

                def rows(s):
                    for r in (4 * s + 1, 4 * s + 3):
                        dve.wait_ge(t_mm, r + 1)
                        dve.tensor_copy(toep_sb[:, r, :], ps[:, 4 + r % 4, 0:TOEP]).then_inc(t_sbD, 1)

                def low(n, s):
                    dve.wait_ge(n_high, n + 1)
                    dve.tensor_tensor(xlow[:, :, bass.ds(n * P, P)],
                                      ps[:, 2 * (s % 2):2 * (s % 2) + 2, :].rearrange("p b (k t) -> p (b k) t", k=4),
                                      xhigh[:, :, bass.ds(n * P, P)].bitcast(F32), ALU.subtract).then_inc(n_cut, 1)

                def body(i):
                    for s in range(4):
                        n = i * 4 + s
                        dve.wait_ge(n_ssq, n + 1)
                        dve.tensor_scalar(stat[:, 4 + s:5 + s], stat[:, s:s + 1], 1.0 / D, EPS, ALU.mult, ALU.add).then_inc(n_var, 1)
                        dve.wait_ge(n_std, n + 1)
                        dve.reciprocal(stat[:, 12 + s:13 + s], stat[:, 8 + s:9 + s]).then_inc(n_rstd, 1)
                        dve.wait_ge(n_rstd, n + 1)
                        if s >= 2 or not isinstance(i, int) or i:
                            dve.wait_ge(n_T, n - 1)
                        dve.scalar_tensor_tensor(out=xs[:, s % 2, :], in0=xin[:, s, :], scalar=stat[:, 12 + s:13 + s],
                                                 in1=g1[:, :], op0=ALU.mult, op1=ALU.mult).then_inc(n_xs, 1)
                        if isinstance(i, int):
                            rows(s)
                        if s or not isinstance(i, int) or i:
                            low(i * 4 + (s - 1), s - 1)
                body(0)
                low_block(dve, 0)
                low_block(dve, 1)
                with dve.Fori(1, NT // 4) as i:
                    body(i)
                low(NT - 1, NT - 1)

            @block.tensor
            def _(pe):
                def rows(i):
                    if i == 0:
                        pe.wait_ge(t_rel, 2)
                        pe.wait_ge(t_hot, 1)
                    for r in range(i * HEADS, (i + 1) * HEADS):
                        if r >= 4:
                            pe.wait_ge(t_sb if r % 2 == 0 else t_sbD, (r - 4) // 2 + 1)
                        col = TABLES[i][0] * HEADS + r % HEADS
                        for part in (relhigh, rellow):
                            mm = pe.matmul(ps[:, 4 + r % 4, 0:TOEP], part[:, col:col + 1].broadcast_to([BUCKETS + 1, P]),
                                           hotr[:, i * TOEP:(i + 1) * TOEP], start=part is relhigh, stop=part is rellow)
                        mm.then_inc(t_mm, 1)
                rows(0)
                pe.wait_ge(c_loaded, 16 * 4)

                def body(i):
                    for s in range(4):
                        n = i * 4 + s
                        pe.wait_ge(n_xs, n + 1)
                        if s >= 2 or not isinstance(i, int) or i:
                            pe.wait_ge(n_cut, n - 1)
                        for k in range(KT):
                            mm = pe.transpose(ps[:, 2 * (s % 2) + k // 4, (k % 4) * P:(k % 4 + 1) * P],
                                              xs[:, s % 2, k * P:(k + 1) * P], ident[:, :])
                        mm.then_inc(n_T, 1)
                        if isinstance(i, int) and s + 1 < len(TABLES):
                            rows(s + 1)
                body(0)
                with pe.Fori(1, NT // 4) as i:
                    body(i)

        p_mm, q_ev, kv_ev, u_ev = sem("p_mm"), sem("q_ev"), sem("kv_ev"), sem("u_ev")
        s_mm, s_max, s_neg, s_exp = sem("s_mm"), sem("s_max"), sem("s_neg"), sem("s_exp")
        pt_T, pt_evA, pt_evD, o_mm, o_ev = sem("pt_T"), sem("pt_evA"), sem("pt_evD"), sem("o_mm"), sem("o_ev")
        o_st = sems("o_st", 3)
        PB = [sum(12 + len(PLANS[h][1]) for h in range(g)) for g in range(NG + 1)]
        KVB = [sum(6 + len(PLANS[h][1]) for h in range(g)) for g in range(NG + 1)]
        units = [(g, i, t) for g in range(NG) for i, t in enumerate(PLANS[g][0])]
        BLOCK_END = [PB[n // 3] + (6, 12, 12 + len(PLANS[n // 3][1]))[n % 3] for n in range(9)] + \
                    [PB[NG] + NT * (m + 1) for m in range(3)]
        u_tiles = [(s, par, j) for s, (_, n) in enumerate(SEQS) for par in range(2) for j in range(n // 2 // P)]
        first_unit = [next(n for n, v in enumerate(units) if v[0] == g) for g in range(NG)] + [len(units)]
        NU = len(units)

        def bias_of(g, t, h):
            if t.classes > 1:
                return same[:, t.s, h, :]
            return band[:, g * HEADS + h, t.bias:t.bias + sum(w for _, w, _ in t.keys)]

        def bank_rows(bank, h, w):
            return ps[:, bank, (h // 2) * 256:(h // 2) * 256 + w]

        def copy_turned(copy, n, t, half, done):
            rows = [w + p0 for _, w, p0 in t.keys]
            src = ps[:, 4 + half, :].rearrange("p (h c q) -> p h c q", h=2, c=2)
            if len(rows) == 2 and rows[0] == rows[1]:
                ins = copy(pT[:, n % 2, 2 * half:2 * half + 2, :, :], src)
            else:
                for c, w in enumerate(rows):
                    ins = copy(pT[0:w, n % 2, 2 * half:2 * half + 2, c, :], src[0:w, :, c, :])
            ins.then_inc(done, 1)

        with nc.Block() as block:
            @block.sync
            def _(sp):
                sp.wait_ge(t_out, 16)
                rows = len(TABLES) * HEADS
                sp.dma_start(band[:, :, :], bass.AP(tensor=toep.tensor, offset=191 - HALF,
                                                    ap=[[rows * TOEP - 1, P], [TOEP, 2 * HEADS], [1, 2 * P]])).then_inc(t_tab, 16)
                for s in range(2):
                    sp.dma_start(same[:, s, :, :], bass.AP(tensor=toep.tensor, offset=(2 + s) * HEADS * TOEP + 191,
                                                           ap=[[rows * TOEP - 1, P], [TOEP, HEADS], [1, P]])).then_inc(t_tab, 16)

                def store(n):
                    g, i, t = units[n]
                    sp.wait_ge(o_ev, n + 1)
                    base, size = SEQS[t.s]
                    rows = attrows[g, base:base + size, :].rearrange("(n r) f -> r n f", r=GROUPS[g][1] // t.classes)
                    sp.dma_start(rows[t.r, t.q0:t.q0 + P, :], orow[:, n % 3, :]).then_inc(o_st[n % 3], 16)
                for g in range(NG):
                    for n in range(3 * g, 3 * g + 3):
                        sp.wait_ge(p_mm, BLOCK_END[n])
                        load_in_block(sp, n + 2)
                    for n in range(first_unit[g], first_unit[g + 1]):
                        store(n)
                sp.wait_ge(p_mm, BLOCK_END[9])
                load_in_block(sp, 11)
                for b in range(3):
                    sp.wait_ge(o_st[b], 16 * (NU // 3))

            @block.tensor
            def _(pe):
                def bank_free(g, p):
                    if p < 2:
                        if g:
                            pe.wait_ge(o_ev, first_unit[g])
                        return
                    if p - 2 < 6:
                        pe.wait_ge(q_ev, 6 * g + p - 1)
                    else:
                        pe.wait_ge(kv_ev, KVB[g] + p - 7)

                def tokens_first(p, n, toks):
                    bank, (high, low) = ps[:, 6 + p % 2, 0:WB], toks
                    for k in range(KT):
                        pe.matmul(bank, high[k], whigh[:, n % 2, k, :], start=k == 0, stop=False)
                        pe.matmul(bank, high[k], wlow[:, n % 2, k, :], start=False, stop=False)
                        mm = pe.matmul(bank, low[k], whigh[:, n % 2, k, :], start=False, stop=k == KT - 1)
                    mm.then_inc(p_mm, 1)

                def channels():
                    p = 0
                    for n in range(9, 12):
                        pe.wait_ge(b_cut, n + 1)
                        for s, par, j in u_tiles:
                            if p < 2:
                                pe.wait_ge(o_ev, NU)
                            else:
                                pe.wait_ge(u_ev, p - 1)
                            base, size = SEQS[s]
                            tokens_first(p, n, [[x[:, k, base:base + size].rearrange("p (n r) -> p r n", r=2)[:, par, j * P:(j + 1) * P]
                                                 for k in range(KT)] for x in (xhigh, xlow)])
                            p += 1

                def project(g):
                    p = 0
                    for b in range(2):
                        n = 3 * g + b
                        pe.wait_ge(b_cut, n + 1)
                        for hp in range(2):
                            for c in range(NCH):
                                bank_free(g, p)
                                bank, toks = ps[:, 6 + p % 2, :], slice(c * CH, (c + 1) * CH)
                                for k in range(KT):
                                    high, low = (w[:, n % 2, k, hp * P:(hp + 1) * P] for w in (whigh, wlow))
                                    pe.matmul(bank, high, xhigh[:, k, toks], start=k == 0, stop=False)
                                    pe.matmul(bank, high, xlow[:, k, toks], start=False, stop=False)
                                    mm = pe.matmul(bank, low, xhigh[:, k, toks], start=False, stop=k == KT - 1)
                                mm.then_inc(p_mm, 1)
                                p += 1
                    pe.wait_ge(b_cut, 3 * g + 3)
                    for s, r, classes, a in PLANS[g][1]:
                        bank_free(g, p)
                        tokens_first(p, 3 * g + 2, [[of_class(x[:, k, :], s, g, r, classes, a, P) for k in range(KT)]
                                                    for x in (xhigh, xlow)])
                        p += 1
                    pe.wait_ge(q_ev, 6 * (g + 1))
                    pe.wait_ge(kv_ev, KVB[g + 1])

                def scores(n):
                    g, i, t = units[n]
                    if n >= 2:
                        pe.wait_ge(s_max, 4 * (n - 1))
                    w = sum(w for _, w, _ in t.keys)
                    for h in range(HEADS):
                        rows = slice(64 * (h % 2), 64 * (h % 2) + 64)
                        mm = pe.matmul(bank_rows(2 * (n % 2) + h % 2, h, w),
                                       of_class(qT[rows, h // 2, :], t.s, g, t.r, t.classes, t.q0, P),
                                       of_class(kT[rows, h // 2, :], t.s, g, t.r, t.classes, t.k0, w),
                                       start=True, stop=True)
                        if h >= 2:
                            mm.then_inc(s_mm, 1)

                def turn(n):
                    g, i, t = units[n]
                    pe.wait_ge(s_exp, 4 * (n + 1))
                    if n:
                        pe.wait_ge(pt_evA, n)
                        pe.wait_ge(pt_evD, n)
                    for h in range(HEADS):
                        at_key = 0
                        for c, (_, w, p0) in enumerate(t.keys):
                            mm = pe.transpose(ps[0:w + p0, 4 + h // 2, ((h % 2) * 2 + c) * P:((h % 2) * 2 + c + 1) * P],
                                              sc[:, n % 3, h, at_key - p0:at_key + w], ident[:, :])
                            at_key += w
                        if h % 2:
                            mm.then_inc(pt_T, 1)

                def outputs(n):
                    g, i, t = units[n]
                    pe.wait_ge(pt_evA, n + 1)
                    pe.wait_ge(pt_evD, n + 1)
                    if n >= 2:
                        pe.wait_ge(o_ev, n - 1)
                    for h in range(HEADS):
                        for c, (v, w, p0) in enumerate(t.keys):
                            mm = pe.matmul(ps[:, 6 + n % 2, h * HD:(h + 1) * HD], pT[p0:p0 + w, n % 2, h, c, :],
                                           V[p0:p0 + w, v, h * HD:(h + 1) * HD], start=c == 0, stop=c == len(t.keys) - 1)
                    mm.then_inc(o_mm, 1)

                for g in range(NG):
                    project(g)
                    a, b = first_unit[g], first_unit[g + 1]
                    for n in range(a, b + 3):
                        if n < b:
                            scores(n)
                        if a <= n - 2 < b:
                            turn(n - 2)
                        if a <= n - 3:
                            outputs(n - 3)
                channels()

            @block.scalar
            def _(act):
                def exps(n):
                    g, i, t = units[n]
                    act.wait_ge(s_neg, n + 1)
                    w = sum(w for _, w, _ in t.keys)
                    for h in range(HEADS):
                        act.activation(sc[:, n % 3, h, 0:w], sc[:, n % 3, h, 0:w], ACT.Exp, bias=negm[:, n % 2, h:h + 1],
                                       accum_out=rowstat[:, n % 4, HEADS + h:HEADS + h + 1]).then_inc(s_exp, 1)

                def turned(n):
                    g, i, t = units[n]
                    act.wait_ge(pt_T, 2 * n + 1)
                    copy_turned(lambda o, x: act.activation(o, x, ACT.Copy), n, t, 0, pt_evA)

                for g in range(NG):
                    for hp in range(2):
                        for c in range(NCH):
                            p = hp * NCH + c
                            act.wait_ge(p_mm, PB[g] + p + 1)
                            act.activation(qT[:, hp, c * CH:(c + 1) * CH], ps[:, 6 + p % 2, :], ACT.Copy,
                                           scale=HD ** -0.5).then_inc(q_ev, 1)
                    high_block(act, 3 * g + 2)
                    high_block(act, 3 * g + 3)
                    a, b = first_unit[g], first_unit[g + 1]
                    for n in range(a, b + 2):
                        if n < b:
                            exps(n)
                        if n - 2 >= a:
                            turned(n - 2)
                        if n == a + 2:
                            high_block(act, 3 * g + 4)
                for p in range(3 * NT):
                    if p == NT:
                        high_block(act, 11)
                    act.wait_ge(p_mm, PB[NG] + p + 1)
                    act.activation(u[:, p % NT, p // NT * WB:(p // NT + 1) * WB], ps[:, 6 + p % 2, 0:WB], ACT.Copy).then_inc(u_ev, 1)

            @block.vector
            def _(dve):
                def biased(n):
                    g, i, t = units[n]
                    w = sum(w for _, w, _ in t.keys)
                    if n >= 3:
                        dve.wait_ge(pt_T, 2 * (n - 2))
                    if n >= 4:
                        dve.wait_ge(o_ev, n - 3)
                    for h in (0, 2, 1, 3):
                        dve.wait_ge(s_mm, 2 * n + 1 + h % 2)
                        dve.tensor_tensor_reduce(sc[:, n % 3, h, 0:w], bank_rows(2 * (n % 2) + h % 2, h, w), bias_of(g, t, h),
                                                 1.0, -3.0e38, ALU.add, ALU.max,
                                                 rowstat[:, n % 4, h:h + 1]).then_inc(s_max, 1)
                    dve.wait_ge(s_max, 4 * (n + 1))
                    if n >= 2:
                        dve.wait_ge(s_exp, 4 * (n - 1))
                    dve.tensor_scalar(negm[:, n % 2, :], rowstat[:, n % 4, 0:HEADS], -1.0, None, ALU.mult).then_inc(s_neg, 1)

                def turned(n):
                    g, i, t = units[n]
                    dve.wait_ge(pt_T, 2 * n + 2)
                    copy_turned(dve.tensor_copy, n, t, 1, pt_evD)

                def outputs(n):
                    if n >= 3:
                        dve.wait_ge(o_st[n % 3], 16 * (n // 3))
                    dve.wait_ge(s_exp, 4 * (n + 1))
                    dve.tensor_copy(orow[:, n % 3, GW:AROW], rowstat[:, n % 4, :])
                    dve.wait_ge(o_mm, n + 1)
                    dve.tensor_copy(orow[:, n % 3, 0:GW], ps[:, 6 + n % 2, 0:GW]).then_inc(o_ev, 1)

                for g in range(NG):
                    for hp in range(2):
                        for c in range(NCH):
                            p = 6 + hp * NCH + c
                            dve.wait_ge(p_mm, PB[g] + p + 1)
                            dve.tensor_copy(kT[:, hp, c * CH:(c + 1) * CH], ps[:, 6 + p % 2, :]).then_inc(kv_ev, 1)
                            if (hp, c) == (1, 0):
                                low_block(dve, 3 * g + 2)
                    for v in range(len(PLANS[g][1])):
                        p = 12 + v
                        dve.wait_ge(p_mm, PB[g] + p + 1)
                        dve.tensor_copy(V[:, v, :], ps[:, 6 + p % 2, 0:GW]).then_inc(kv_ev, 1)
                        if v == 4:
                            low_block(dve, 3 * g + 3)
                    a, b = first_unit[g], first_unit[g + 1]
                    if g == 0:
                        dve.wait_ge(t_tab, 16 * 3)
                    for n in range(a, b + 3):
                        if n < b:
                            biased(n)
                        if a <= n - 2 < b:
                            turned(n - 2)
                        if a <= n - 3:
                            outputs(n - 3)
                        if n == a + 2:
                            low_block(dve, 3 * g + 4)
                low_block(dve, 11)

        f_tabS, f_tabP, f_x, f_e, f_eev, f_f, f_fe, f_fo = (sem(n) for n in ("f_tabS", "f_tabP", "f_x", "f_e", "f_eev", "f_f", "f_fe", "f_fo"))
        a_ld = sems("a_ld", 2)
        a_max, a_w, a_exp, a_at, a_T, a_ev = (sem(n) for n in ("a_max", "a_w", "a_exp", "a_at", "a_T", "a_ev"))
        items = [(c, s) for s in (1, 0) for c in range(F_GROUPS)]
        tabs = (tabP, tabS)

        def load_comb(sp, t):
            sp.dma_start(comb[:, t % 2, :, :], attrows[:, t * P:(t + 1) * P, :].rearrange("g p f -> p g f")).then_inc(a_ld[t % 2], 16)

        with nc.Block() as block:
            @block.sync
            def _(sp):
                sp.dma_start(tabS[:, :, :, :], pos_sample.rearrange("(t p) c k -> p t c k", p=P)).then_inc(f_tabS, 16)
                sp.dma_start(chan_sb[:, :, :], chan).then_inc(f_tabS, 16)
                load_comb(sp, 0)
                load_comb(sp, 1)
                sp.dma_start(tabP[:, :, :, :], pos_prompt.rearrange("(t p) c k -> p t c k", p=P)).then_inc(f_tabP, 16)
                for t in range(2, NT):
                    sp.wait_ge(a_at, 3 * (t - 1))
                    load_comb(sp, t)
                sp.wait_ge(f_e, 4 * len(items) - 2)
                for m in range(4):
                    load_piece(sp, 0, m // 3, m % 3)

            @block.tensor
            def _(pe):
                def positions(i, par):
                    c, s = items[i]
                    half = SEQS[s][1] // 2
                    nt = half // P
                    first = (0 if s == 0 else 8) + par * nt
                    for part in range(2):
                        n = 4 * i + 2 * par + part
                        if n >= 2:
                            pe.wait_ge(f_eev, n - 1)
                        for j in range(nt):
                            mm = pe.matmul(ps[:, part, 0:half], u[:, first + j, c * P:(c + 1) * P],
                                           tabs[s][:, par * nt + j, part, :], start=j == 0, stop=j == nt - 1)
                        mm.then_inc(f_e, 1)

                def over_channels(i, par):
                    c, s = items[i]
                    half = SEQS[s][1] // 2
                    pe.wait_ge(f_eev, 4 * i + 2 * par + 2)
                    if i:
                        pe.wait_ge(f_fe if par == 0 else f_fo, i if par == 0 else 2 * i)
                    for part in range(2):
                        mm = pe.matmul(ps[:, 2 + par, 0:half], chan_sb[:, part, :], eo[:, 2 * par + part, 0:half],
                                       start=part == 0, stop=part == 1)
                    mm.then_inc(f_f, 1)

                def merged(t):
                    pe.wait_ge(a_at, 3 * (t + 1))
                    if t:
                        pe.wait_ge(a_ev, t)
                    for h in range(2):
                        mm = pe.transpose(ps[:, 6, h * P:(h + 1) * P], attk[:, t % 2, h * P:(h + 1) * P], ident[:, :])
                    mm.then_inc(a_T, 1)

                for i in range(len(items)):
                    if i in (0, F_GROUPS):
                        pe.wait_ge(*((f_tabP, 16) if i else (f_tabS, 32)))
                    positions(i, 0)
                    if i:
                        over_channels(i - 1, 1)
                    positions(i, 1)
                    over_channels(i, 0)
                    if i:
                        merged(i - 1)
                over_channels(len(items) - 1, 1)
                merged(NT - 1)

            @block.scalar
            def _(act):
                def sums(i, par):
                    half = SEQS[items[i][1]][1] // 2
                    for part in range(2):
                        n = 4 * i + 2 * par + part
                        act.wait_ge(f_e, n + 1)
                        act.activation(eo[:, 2 * par + part, 0:half], ps[:, part, 0:half], ACT.Copy).then_inc(f_eev, 1)

                def even_half(i):
                    half = SEQS[items[i][1]][1] // 2
                    act.wait_ge(f_f, 2 * i + 1)
                    if i >= 2:
                        act.wait_ge(f_fo, 2 * (i - 1))
                    act.activation(fe[:, i % 2, 0:half], ps[:, 2, 0:half], ACT.Copy).then_inc(f_fe, 1)

                def exps(t):
                    act.wait_ge(a_max, 2 * (t + 1))
                    act.activation(cw[:, 16:28], cw[:, 4:16], ACT.Exp).then_inc(a_exp, 1)

                def merged(t):
                    act.wait_ge(a_T, t + 1)
                    if t == 0:
                        act.wait_ge(f_x, KT)
                    act.activation(attT[:, :, t * P:(t + 1) * P], ps[:, 6, 0:2 * P].rearrange("p (h t) -> p h t", h=2),
                                   ACT.Copy).then_inc(a_ev, 1)

                for i in range(len(items)):
                    sums(i, 0)
                    sums(i, 1)
                    even_half(i)
                    exps(i)
                    if i:
                        merged(i - 1)
                merged(NT - 1)

            @block.vector
            def _(dve):
                def weights(t):
                    b = comb[:, t % 2, :, :]
                    m = lambda g: b[:, g, GW:GW + HEADS]
                    dve.wait_ge(a_ld[t % 2], 16 * (t // 2 + 1))
                    if t:
                        dve.wait_ge(a_exp, t)
                    dve.tensor_tensor(cw[:, 0:4], m(0), m(1), ALU.max).then_inc(a_w, 1)
                    dve.wait_ge(a_w, 6 * t + 1)
                    dve.tensor_tensor(cw[:, 0:4], cw[:, 0:4], m(2), ALU.max).then_inc(a_max, 1)
                    dve.wait_ge(a_max, 2 * t + 1)
                    dve.tensor_tensor(cw[:, 4:16].rearrange("p (g h) -> p g h", g=NG), b[:, :, GW:GW + HEADS],
                                      cw[:, 0:4].rearrange("p (o h) -> p o h", o=1).broadcast_to([P, NG, HEADS]),
                                      ALU.subtract).then_inc(a_max, 1)

                def merge(t):
                    b = comb[:, t % 2, :, :]
                    dve.wait_ge(a_exp, t + 1)
                    dve.tensor_tensor(cw[:, 28:40].rearrange("p (g h) -> p g h", g=NG), b[:, :, GW + HEADS:AROW],
                                      cw[:, 16:28].rearrange("p (g h) -> p g h", g=NG), ALU.mult).then_inc(a_w, 1)
                    dve.wait_ge(a_w, 6 * t + 2)
                    dve.tensor_tensor(cw[:, 40:44], cw[:, 28:32], cw[:, 32:36], ALU.add).then_inc(a_w, 1)
                    dve.wait_ge(a_w, 6 * t + 3)
                    dve.tensor_tensor(cw[:, 40:44], cw[:, 40:44], cw[:, 36:40], ALU.add).then_inc(a_w, 1)
                    dve.wait_ge(a_w, 6 * t + 4)
                    dve.reciprocal(cw[:, 44:48], cw[:, 40:44]).then_inc(a_w, 1)
                    dve.wait_ge(a_w, 6 * t + 5)
                    dve.tensor_tensor(cw[:, 48:60].rearrange("p (g h) -> p g h", g=NG), cw[:, 16:28].rearrange("p (g h) -> p g h", g=NG),
                                      cw[:, 44:48].rearrange("p (o h) -> p o h", o=1).broadcast_to([P, NG, HEADS]),
                                      ALU.mult).then_inc(a_w, 1)
                    dve.wait_ge(a_w, 6 * t + 6)
                    for g in range(NG):
                        o = b[:, g, 0:GW].rearrange("p (h e) -> p h e", h=HEADS)
                        ins = dve.tensor_tensor(o, o, cw[:, 48 + 4 * g:52 + 4 * g].rearrange("p (h o) -> p h o", o=1)
                                                .broadcast_to([P, HEADS, HD]), ALU.mult)
                    ins.then_inc(a_at, 1)
                    dve.wait_ge(a_at, 3 * t + 1)
                    dve.tensor_tensor(b[:, 0, 0:GW], b[:, 0, 0:GW], b[:, 1, 0:GW], ALU.add).then_inc(a_at, 1)
                    dve.wait_ge(a_at, 3 * t + 2)
                    if t >= 2:
                        dve.wait_ge(a_T, t - 1)
                    dve.tensor_tensor(attk[:, t % 2, :], b[:, 0, 0:GW], b[:, 2, 0:GW], ALU.add).then_inc(a_at, 1)

                def butterfly(i):
                    c, s = items[i]
                    base, size = SEQS[s]
                    half = size // 2
                    dve.wait_ge(f_fe, i + 1)
                    dve.wait_ge(f_f, 2 * i + 2)
                    dve.tensor_tensor(fourT[:, c, base:base + half], fe[:, i % 2, 0:half], ps[:, 3, 0:half], ALU.add).then_inc(f_fo, 1)
                    dve.tensor_tensor(fourT[:, c, base + half:base + size], fe[:, i % 2, 0:half], ps[:, 3, 0:half],
                                      ALU.subtract).then_inc(f_fo, 1)

                for k in range(KT):
                    dve.tensor_tensor(xnT[:, k, :], xlow[:, k, :].bitcast(F32), xhigh[:, k, :].bitcast(F32), ALU.add).then_inc(f_x, 1)
                for i in range(len(items)):
                    if i == 1:
                        dve.wait_ge(f_x, KT)
                    weights(i)
                    if i:
                        butterfly(i - 1)
                    merge(i)
                butterfly(len(items) - 1)

        m_mm, m_sig, m_gat, m_mix = (sem(n) for n in ("m_mm", "m_sig", "m_gat", "m_mix"))
        g_high, g_cut, t_high, t_cut = (sem(n) for n in ("g_high", "g_cut", "t_high", "t_cut"))
        QUAD = 4
        FREE = 2
        cuts = [(xnT, xh, xlow, k) for k in range(0, KT, 2)] + [(attT, ah, alow, 0)] + \
               [(fourT, fh, flow, k) for k in range(0, F_GROUPS, 2)]
        X_CUTS = KT // 2

        def mix_of(c):
            return mix0[:, :, :] if c == 0 else xnT[:, :, (c - 1) * CH:c * CH]

        with nc.Block() as block:
            @block.sync
            def _(sp):
                def pieces(c, i, d, before=None):
                    n = (c * 2 + i) * QUAD + d
                    for b in range(3):
                        if before is not None and 3 * before + b < 4:
                            continue
                        sp.wait_ge(m_mm, n * 4 - (4, 3, 2)[b])
                        sp.nop(nofuse=True)
                        load_piece(sp, i, d, b)
                for d in range(QUAD):
                    pieces(0, 0, d, d)
                for d in range(QUAD):
                    pieces(0, 1, d)
                with sp.Fori(0, 2) as i:
                    for d in range(QUAD):
                        pieces(1, i, d)
                for k in range(KT):
                    pieces(2, k // QUAD, k % QUAD)
                    if k == 1:
                        sp.wait_ge(m_mm, 2 * KT * 4)
                    for r in {0: (), KT - 1: (KT - 2, KT - 1)}.get(k, (k - 1,)):
                        sp.dma_start(w_out_at(r), w_out[0, r * P:(r + 1) * P, :]).then_inc(wo_loaded, 16)

            @block.tensor
            def _(pe):
                def step(c, i, d):
                    n = (c * 2 + i) * QUAD + d
                    cols = slice(c * CH, (c + 1) * CH)
                    pe.wait_ge(m_gat, n * 2 + (2 * FREE - 2))
                    for q, (b, first, tiles, high, low) in enumerate((
                            (0, 0, KT, xh, xlow), (1, 0, KT, xh, xlow), (2, 0, 2, ah, alow), (2, 2, F_GROUPS, fh, flow))):
                        slot = (3 * d + b) % 4
                        if q < 3:
                            pe.wait_ge(g_cut, n * 3 + (b + 1))
                        if q == 2:
                            pe.wait_ge(t_cut, (c + 1) * len(cuts))
                        for k in range(tiles):
                            if q == 0 and d == 0 and k % 2 == 0:
                                pe.wait_ge(t_cut, c * len(cuts) + k // 2 + 1)
                            bank = ps[:, 4 * (d % 2) + q, :]
                            wk = first + k
                            pe.matmul(bank, ghigh[:, slot, wk, :], high[:, k, :], start=k == 0, stop=False)
                            pe.matmul(bank, ghigh[:, slot, wk, :], low[:, k, cols], start=False, stop=False)
                            mm = pe.matmul(bank, glow[:, slot, wk, :], high[:, k, :], start=False, stop=k == tiles - 1)
                        mm.then_inc(m_mm, 1)
                for c in range(NCH):
                    with pe.Fori(0, 2) as i:
                        for d in range(QUAD):
                            step(c, i, d)

            @block.scalar
            def _(act):
                def high(turn, d, b):
                    slot = (3 * d + b) % 4
                    act.wait_ge(g_loaded[slot], (turn * 3 + (3 * d + b) // 4 + 1) * 32)
                    act.activation(ghigh[:, slot, :, :], graw[:, slot, :, :], ACT.Copy).then_inc(g_high, 1)

                def cut(c, which):
                    for src, dst, _, k in which:
                        act.activation(dst[:, k:k + 2, :], src[:, k:k + 2, c * CH:(c + 1) * CH], ACT.Copy).then_inc(t_high, 1)

                def quad(c, i, last=False):
                    for d in range(QUAD):
                        n = (c * 2 + i) * QUAD + d
                        for b in range(3):
                            if d + 1 < QUAD:
                                high(c * 2 + i, d + 1, b)
                            elif not last:
                                high(c * 2 + i + 1, 0, b)
                            if b < 2:
                                act.wait_ge(m_mm, n * 4 + (b + 1))
                                if b == 0:
                                    act.wait_ge(m_gat, n * 2 + (2 * FREE - 2))
                                act.nop(nofuse=True)
                                act.activation(sig[:, d % 2, b, :], ps[:, 4 * (d % 2) + b, :], ACT.Sigmoid,
                                               bias=bg[:, bass.ds(i * QUAD + (b * KT + d), 1)]).then_inc(m_sig, 1)
                high(0, 0, 0)
                cut(0, cuts[:X_CUTS])
                high(0, 0, 1)
                cut(0, cuts[X_CUTS:])
                high(0, 0, 2)
                for c in range(NCH - 1):
                    with act.Fori(0, 2) as i:
                        quad(c, i)
                    act.wait_ge(m_mm, ((c + 1) * 8 - 1) * 4 + 2)
                    cut(c + 1, cuts[:X_CUTS])
                    act.wait_ge(m_mm, (c + 1) * 8 * 4)
                    cut(c + 1, cuts[X_CUTS:])
                quad(NCH - 1, 0)
                quad(NCH - 1, 1, last=True)

            @block.vector
            def _(dve):
                dve.sem_inc(m_gat, 2 * FREE)
                dve.sem_inc(m_mix, FREE)

                def low(turn, d, b):
                    slot = (3 * d + b) % 4
                    dve.wait_ge(g_high, turn * 12 + (3 * d + b + 1))
                    dve.tensor_tensor(glow[:, slot, :, :], graw[:, slot, :, :], ghigh[:, slot, :, :].bitcast(F32),
                                      ALU.subtract).then_inc(g_cut, 1)

                def cut(c, first, end):
                    for m, (src, high, dst, k) in list(enumerate(cuts))[first:end]:
                        cols = slice(c * CH, (c + 1) * CH)
                        dve.wait_ge(t_high, c * len(cuts) + m + 1)
                        dve.tensor_tensor(dst[:, k:k + 2, cols], src[:, k:k + 2, cols], high[:, k:k + 2, :].bitcast(F32),
                                          ALU.subtract).then_inc(t_cut, 1)

                def quad(c, i, last=False):
                    for d in range(QUAD):
                        n = (c * 2 + i) * QUAD + d
                        for b in range(3):
                            if d + 1 < QUAD:
                                low(c * 2 + i, d + 1, b)
                            elif not last:
                                low(c * 2 + i + 1, 0, b)
                        for q in range(2):
                            dve.wait_ge(m_sig, n * 2 + (q + 1))
                            dve.wait_ge(m_mm, n * 4 + (q + 3))
                            if q == 0:
                                dve.wait_ge(m_mix, n + (FREE - 1))
                            dve.tensor_tensor(gated[:, d % 2, q, :], ps[:, 4 * (d % 2) + 2 + q, :], sig[:, d % 2, q, :],
                                              ALU.mult).then_inc(m_gat, 1)
                        dve.wait_ge(m_gat, n * 2 + (2 + 2 * FREE))
                        dve.tensor_tensor(mix_of(c)[:, bass.ds(i * QUAD + d, 1), :].rearrange("p o t -> p (o t)"),
                                          gated[:, d % 2, 0, :], gated[:, d % 2, 1, :], ALU.add).then_inc(m_mix, 1)
                low(0, 0, 0)
                cut(0, 0, X_CUTS)
                low(0, 0, 1)
                cut(0, X_CUTS, len(cuts))
                low(0, 0, 2)
                for c in range(NCH - 1):
                    with dve.Fori(0, 2) as i:
                        quad(c, i)
                    cut(c + 1, 0, len(cuts))
                quad(NCH - 1, 0)
                quad(NCH - 1, 1, last=True)

        raw_ld = sems("raw_ld", 4)
        r_g2, r_x, r_st = sem("r_g2"), sems("r_x", 2), sems("r_st", 2)
        r_y, r_x2, r_ssq, r_var, r_std, r_rstd, r_xn = (sem(n) for n in ("r_y", "r_x2", "r_ssq", "r_var", "r_std", "r_rstd", "r_xn"))
        r_T, r_TevA, r_TevD, r_lg, r_sm, r_exp, r_af, r_aT, r_aev = (sem(n) for n in (
            "r_T", "r_TevA", "r_TevD", "r_lg", "r_sm", "r_exp", "r_af", "r_aT", "r_aev"))
        r_top, r_idf, r_iT, r_fin = (sem(n) for n in ("r_top", "r_idf", "r_iT", "r_fin"))

        Row = namedtuple("Row", "out turn logits aff")
        PROMPT_TILES = SEQS[0][1] // P

        def tile_rows():
            rows, with_logits, with_aff = [], 0, 0
            for t in range(NT + 1):
                catch_up = t in (PROMPT_TILES, NT)
                to_logits, to_aff = (t, t) if catch_up else (max(with_logits, t - 1), max(with_aff, t - 2))
                rows.append(Row(out=[t] if t < NT else [], turn=[t - 1] if t else [],
                                logits=list(range(with_logits, to_logits)), aff=list(range(with_aff, to_aff))))
                with_logits, with_aff = to_logits, to_aff
            return rows
        ROWS = tile_rows()

        def load_unit(sp, e, j):
            for i in range(2):
                if j < 8:
                    dst = raw[j % 4][:, 8 * i:8 * i + 8, :]
                    src = (w_eg, w_eu)[i][0, bass.ds(e, 1), :, j * WB:(j + 1) * WB]
                else:
                    dst = raw[j % 4][:, 8 * i:8 * i + 8, :].rearrange("p a n -> p (a n)").rearrange("p (k n) -> p k n", k=4)
                    row, c = (j % 2) * D + i * CH, (j - 8) // 2 * CH
                    src = w_ed[0, bass.ds(e, 1), row:row + CH, c:c + CH]
                sp.dma_start(dst, src.rearrange("o (k p) n -> p (o k) n", p=P)).then_inc(raw_ld[j % 4], 16)

        with nc.Block() as block:
            @block.sync
            def _(sp):
                sp.dma_start(g2[:, :], norm2_g.partition_broadcast(P)).then_inc(r_g2, 16)
                for t in range(2):
                    sp.dma_start(xres[:, t, :], x[t * P:(t + 1) * P, :]).then_inc(r_x[t], 16)
                for j in range(3):
                    load_unit(sp, 0, j)
                for t in range(NT):
                    rows = slice(t * P, (t + 1) * P)
                    sp.wait_ge(r_xn, t + 1)
                    sp.dma_start(resid[rows, :], xres[:, t % 2, :]).then_inc(r_st[t % 2], 16)
                    sp.dma_start(normed[rows, :], xn2[:, t % 2, :]).then_inc(r_st[t % 2], 16)
                    if t + 2 < NT:
                        sp.wait_ge(r_st[t % 2], 32 * (t // 2 + 1))
                        sp.dma_start(xres[:, t % 2, :], x[(t + 2) * P:(t + 3) * P, :]).then_inc(r_x[t % 2], 16)
                for b in range(2):
                    sp.wait_ge(r_st[b], 32 * (NT // 2))

            @block.tensor
            def _(pe):
                def out(t):
                    if t == 0:
                        pe.wait_ge(wo_loaded, 16 * KT)
                    if t >= 2:
                        pe.wait_ge(r_x2, 2 * (t - 1))
                    for nb in range(2):
                        for k in range(KT):
                            mm = pe.matmul(ps[:, 6 * (t % 2) + nb, :], mix_of(t // 4)[:, k, (t % 4) * P:(t % 4 + 1) * P],
                                           w_out_at(k)[:, nb * CH:(nb + 1) * CH], start=k == 0, stop=k == KT - 1)
                        mm.then_inc(r_y, 1)

                def turn(t):
                    pe.wait_ge(r_xn, t + 1)
                    if t:
                        pe.wait_ge(r_TevA, t)
                        pe.wait_ge(r_TevD, t)
                    for k in range(KT):
                        mm = pe.transpose(ps[:, 2 + k // 4, (k % 4) * P:(k % 4 + 1) * P], xn2[:, t % 2, k * P:(k + 1) * P], ident[:, :])
                        if k % 4 == 3:
                            mm.then_inc(r_T, 1)

                def logits(t):
                    pe.wait_ge(r_TevA, t + 1)
                    pe.wait_ge(r_TevD, t + 1)
                    if t:
                        pe.wait_ge(r_exp, t)
                    for k in range(KT):
                        mm = pe.matmul(ps[:, 4, 0:E], xn2T[:, t % 2, k, :], wr[:, k, :], start=k == 0, stop=k == KT - 1)
                    mm.then_inc(r_lg, 1)

                def turn_aff(t):
                    pe.wait_ge(r_af, 2 * (t + 1))
                    if t:
                        pe.wait_ge(r_aev, t)
                    pe.transpose(ps[0:E, 5, 0:P], atok[:, t % 2, :], ident[:, :]).then_inc(r_aT, 1)

                for row in ROWS:
                    for t in row.out:
                        out(t)
                    for t in row.turn:
                        turn(t)
                    for t in row.logits:
                        logits(t)
                    for t in row.aff:
                        turn_aff(t)
                for s in range(2):
                    pe.wait_ge(r_idf, s + 1)
                    cap = CAPS[s]
                    pe.transpose(ps[0:cap, 6 + s, 0:E], vals[s][:, :], ident[0:E, 0:E])
                    pe.transpose(ps[0:cap, 6 + s, E:2 * E], idxf[s][:, :], ident[0:E, 0:E]).then_inc(r_iT, 1)

            @block.scalar
            def _(act):
                def norm(t):
                    act.wait_ge(r_x2, 2 * (t + 1))
                    if t:
                        act.wait_ge(r_ssq, t)
                    act.activation(junk2[:, :], xres[:, t % 2, :], ACT.Square, accum_out=stat[:, 0:1]).then_inc(r_ssq, 1)
                    act.wait_ge(r_var, t + 1)
                    act.activation(stat[:, 2:3], stat[:, 1:2], ACT.Sqrt).then_inc(r_std, 1)

                def turned(t):
                    act.wait_ge(r_T, 2 * t + 1)
                    if t >= 2:
                        act.wait_ge(r_lg, t - 1)
                    act.activation(xn2T[:, t % 2, 0:4, :], ps[:, 2, :].rearrange("p (k t) -> p k t", k=4), ACT.Copy).then_inc(r_TevA, 1)
                    if t >= PROMPT_TILES:
                        act.wait_ge(r_T, 2 * t + 2)
                        act.activation(xn2T[:, t % 2, 4:8, :], ps[:, 3, :].rearrange("p (k t) -> p k t", k=4), ACT.Copy).then_inc(r_TevD, 1)

                def softmax(t):
                    act.wait_ge(r_sm, t + 1)
                    act.activation(stat[:, 32 + 16 * (t % 2):48 + 16 * (t % 2)], ps[:, 4, 0:E], ACT.Exp, bias=stat[:, 5:6],
                                   accum_out=stat[:, 6:7]).then_inc(r_exp, 1)

                for row in ROWS:
                    for t in row.out:
                        norm(t)
                    for t in row.turn:
                        turned(t)
                    for t in row.logits:
                        softmax(t)

            @block.vector
            def _(dve):
                dve.wait_ge(r_g2, 16)

                def norm(t):
                    dve.wait_ge(r_x[t % 2], 16 * (t // 2 + 1))
                    for h in range(2):
                        dve.wait_ge(r_y, 2 * t + h + 1)
                        half = xres[:, t % 2, h * CH:(h + 1) * CH]
                        dve.tensor_tensor(half, half, ps[:, 6 * (t % 2) + h, :], ALU.add).then_inc(r_x2, 1)
                    if t > PROMPT_TILES:
                        top(0, next(rounds))
                    dve.wait_ge(r_ssq, t + 1)
                    dve.tensor_scalar(stat[:, 1:2], stat[:, 0:1], 1.0 / D, EPS, ALU.mult, ALU.add).then_inc(r_var, 1)
                    dve.wait_ge(r_std, t + 1)
                    dve.reciprocal(stat[:, 3:4], stat[:, 2:3]).then_inc(r_rstd, 1)
                    dve.wait_ge(r_rstd, t + 1)
                    if t >= 2:
                        dve.wait_ge(r_T, 2 * (t - 1))
                        dve.wait_ge(r_st[t % 2], 32 * (t // 2))
                    dve.scalar_tensor_tensor(out=xn2[:, t % 2, :], in0=xres[:, t % 2, :], scalar=stat[:, 3:4], in1=g2[:, :],
                                             op0=ALU.mult, op1=ALU.mult).then_inc(r_xn, 1)

                def turned(t):
                    dve.wait_ge(r_T, 2 * t + 2)
                    if t >= 2:
                        dve.wait_ge(r_lg, t - 1)
                    dve.tensor_copy(xn2T[:, t % 2, 4:8, :], ps[:, 3, :].rearrange("p (k t) -> p k t", k=4)).then_inc(r_TevD, 1)

                def softmax(t):
                    dve.wait_ge(r_lg, t + 1)
                    dve.tensor_reduce(stat[:, 5:6], ps[:, 4, 0:E], AX.X, ALU.max, negate=True).then_inc(r_sm, 1)
                    dve.wait_ge(r_exp, t + 1)
                    dve.reciprocal(stat[:, 7:8], stat[:, 6:7]).then_inc(r_af, 1)
                    dve.wait_ge(r_af, 2 * t + 1)
                    if t >= 2:
                        dve.wait_ge(r_aT, t - 1)
                    dve.tensor_scalar(atok[:, t % 2, :], stat[:, 32 + 16 * (t % 2):48 + 16 * (t % 2)], stat[:, 7:8], None,
                                      ALU.mult).then_inc(r_af, 1)

                def keep(t):
                    s, tile = (0, t) if t < PROMPT_TILES else (1, t - PROMPT_TILES)
                    dve.wait_ge(r_aT, t + 1)
                    dve.tensor_copy(aff[s][:, tile * P:(tile + 1) * P], ps[0:E, 5, 0:P]).then_inc(r_aev, 1)

                tops = [0]

                def top(s, r):
                    v = vals[s][:, 8 * r:8 * r + 8]
                    if tops[0]:
                        dve.wait_ge(r_top, tops[0])
                    dve.max(v, aff[s][:, :]).then_inc(r_top, 1)
                    dve.wait_ge(r_top, tops[0] + 1)
                    dve.max_index(idxr[s][:, 8 * r:8 * r + 8], v, aff[s][:, :]).then_inc(r_top, 1)
                    dve.wait_ge(r_top, tops[0] + 2)
                    dve.match_replace(aff[s][:, :], v, aff[s][:, :], -1.0).then_inc(r_top, 1)
                    tops[0] += 3

                def as_float(s):
                    dve.wait_ge(r_top, tops[0])
                    dve.tensor_scalar(idxf[s][:, :], idxr[s][:, :], float(SEQS[s][0]), None, ALU.add).then_inc(r_idf, 1)

                rounds = iter(range(CAPS[0] // 8))
                for row in ROWS:
                    for t in row.out:
                        norm(t)
                    for t in row.turn:
                        if t < PROMPT_TILES:
                            turned(t)
                    for t in row.logits:
                        if not row.out:
                            top(0, next(rounds))
                        softmax(t)
                    for t in row.aff:
                        keep(t)
                    if PROMPT_TILES - 1 in row.aff:
                        dve.wait_ge(r_aev, PROMPT_TILES)
                    if PROMPT_TILES in row.out:
                        for _ in range(4):
                            top(0, next(rounds))
                    elif row.out and row.out[0] > PROMPT_TILES:
                        for _ in range(2):
                            top(0, next(rounds))
                for r in rounds:
                    top(0, r)
                as_float(0)
                dve.wait_ge(r_aev, NT)
                for r in range(CAPS[1] // 8):
                    top(1, r)
                as_float(1)
                for s in range(2):
                    cap = CAPS[s]
                    dve.wait_ge(r_iT, s + 1)
                    dve.tensor_copy(gate[s][:, :], ps[0:cap, 6 + s, 0:E])
                    dve.tensor_copy(idx[s][:, :], ps[0:cap, 6 + s, E:2 * E]).then_inc(r_fin, 1)
                dve.wait_ge(r_fin, 2)

        SUBS = FT + 8
        AHEAD = 4
        x_idx, x_in, x_T, x_high, x_cut = (sem(n) for n in ("x_idx", "x_in", "x_T", "x_high", "x_cut"))
        w_high, w_cut, w_used = sem("w_high"), sem("w_cut"), sem("w_used")
        gu_low, gu_sum, gu_sig, gu_g, h_done, h_high, h_cut = (sem(n) for n in (
            "gu_low", "gu_sum", "gu_sig", "gu_g", "h_done", "h_high", "h_cut"))
        y_low, y_sum, y_ev, sc_idx, scat, sent = (sem(n) for n in ("y_low", "y_sum", "y_ev", "sc_idx", "scat", "sent"))
        GU_PAIRS, Y_PAIRS, SENT = 2, 2, 1
        H_LOW, H_HIGH, H_SAMPLE = slice(0, P), slice(P, 2 * P), slice(2 * P, 3 * P)

        def raw_part(q):
            unit = raw[q // 2 % 4][:, :, :]
            if q < FT:
                return unit[:, :, (q % 2) * P:(q % 2 + 1) * P]
            return unit[:, 8 * (q % 2):8 * (q % 2) + 8, :].rearrange("p a n -> p (a n)")

        def cut_part(w, q):
            part = w[:, q % AHEAD, :]
            return part.rearrange("p (a n) -> p a n", n=P) if q < FT else part

        with nc.Block() as block:
            @block.sync
            def _(sp):
                load_unit(sp, 0, 3)

                def late(e):
                    for j in range(4, 12):
                        sp.wait_ge(w_cut, e * SUBS + 2 * (j - 3))
                        sp.nop(nofuse=True)
                        load_unit(sp, e, j)
                with sp.Fori(0, E - 1) as e:
                    late(e)
                    for j in range(4):
                        sp.wait_ge(w_cut, e * SUBS + 2 * (j + 9))
                        sp.nop(nofuse=True)
                        load_unit(sp, e + 1, j)
                late(E - 1)

            @block.gpsimd
            def _(pool):
                def pick(dst, e, done, n):
                    for s in range(2):
                        pool.tensor_copy(dst[s][:, :], idx[s][:, bass.ds(e, 1)]).then_inc(done, 1)
                    pool.wait_ge(done, n)
                    pool.nop(nofuse=True)

                def gather(e, n):
                    pick(idx_in, e, x_idx, n)
                    for s in range(2):
                        pool.indirect_dma_start(xg[s][:, :], None, normed, bass.IndirectOffsetOnAxis(ap=idx_in[s][:, 0:1], axis=0)) \
                            .then_inc(x_in, 16)

                def scatter(e, n):
                    pool.wait_ge(y_ev, n * 2 + Y_PAIRS)
                    pick(idx_out, e, sc_idx, n * 2)
                    for s in range(2):
                        pool.indirect_dma_start(resid, bass.IndirectOffsetOnAxis(ap=idx_out[s][:, 0:1], axis=0), ytok[s][:, :], None,
                                                compute_op=ALU.add).then_inc(scat, 16)
                    pool.wait_ge(scat, n * 32)
                    pool.sem_inc(sent, 1)
                pool.sem_inc(sent, SENT)
                gather(0, 2)
                with pool.Fori(0, E - 1) as e:
                    pool.wait_ge(x_T, (e + 1) * 2)
                    gather(e + 1, (e + 2) * 2)
                    scatter(e, e + 1)
                scatter(E - 1, E)

            @block.tensor
            def _(pe):
                def turn_tokens(n):
                    pe.wait_ge(x_in, (n + 1) * 32)
                    pe.wait_ge(gu_sum, n * FT + GU_PAIRS)
                    for k in range(KT):
                        at_col = (k % 2) * CAP
                        pe.transpose(ps[:, k // 2, at_col:at_col + CAPS[0]], xg[0][:, k * P:(k + 1) * P], ident[:, :])
                        mm = pe.transpose(ps[:, k // 2, at_col + CAPS[0]:at_col + CAP], xg[1][:, k * P:(k + 1) * P],
                                          ident[0:CAPS[1], 0:CAPS[1]])
                        if k % 4 == 3:
                            mm.then_inc(x_T, 1)

                def gate_up(e):
                    pe.wait_ge(x_cut, (e + 1) * 2)
                    for q in range(FT):
                        pe.wait_ge(w_cut, e * SUBS + (q + 1))
                        pe.wait_ge(gu_sum, e * FT + (q + 1))
                        for part in range(2):
                            bank = 2 * (q % 2) + part
                            for k in range(KT):
                                tile = slice((8 * part + k) * P, (8 * part + k + 1) * P)
                                pe.matmul(ps[:, bank, 0:2 * CAP], wh[:, q % AHEAD, tile],
                                          xsplit[:, k, :, :].rearrange("p s t -> p (s t)"), start=k == 0, stop=False)
                                mm = pe.matmul(ps[:, bank, CAP:2 * CAP], wl[:, q % AHEAD, tile], xsplit[:, k, 0, :],
                                               start=False, stop=k == KT - 1)
                        mm.then_inc(w_used, 1)

                def down(e, last):
                    for i in range(8):
                        q, c = FT + i, i // 4
                        pe.wait_ge(w_cut, e * SUBS + (q + 1))
                        if i < 4:
                            pe.wait_ge(h_cut, e * 8 + 2 * (i + 1))
                        if i % 4 == 0:
                            pe.wait_ge(y_ev, e * 2 + (c + 1))
                        for kk in range(4):
                            k = 4 * (i % 4) + kk
                            cols = slice(kk * CH, (kk + 1) * CH)
                            first, end = k == 0, k == FT - 1
                            prompt, sample = ps[:, 4 + 2 * c, :], ps[:, 5 + 2 * c, :]
                            pe.matmul(prompt, hsplit[:, k, H_LOW], wh[:, q % AHEAD, cols], start=first, stop=False)
                            pe.matmul(prompt, hsplit[:, k, H_HIGH], wh[:, q % AHEAD, cols], start=False, stop=False)
                            pe.matmul(prompt, hsplit[:, k, H_HIGH], wl[:, q % AHEAD, cols], start=False, stop=end)
                            pe.matmul(sample, hsplit[:, k, H_SAMPLE], wh[:, q % AHEAD, cols], start=first, stop=False)
                            mm = pe.matmul(sample, hsplit[:, k, H_SAMPLE], wl[:, q % AHEAD, cols], start=False, stop=end)
                        mm.then_inc(w_used, 1)
                        if i == 1 and not last:
                            turn_tokens(e + 1)

                turn_tokens(0)
                with pe.Fori(0, E - 1) as e:
                    gate_up(e)
                    down(e, False)
                gate_up(E - 1)
                down(E - 1, True)

            @block.scalar
            def _(act):
                act.sem_inc(y_ev, Y_PAIRS)

                def high_weights(e, q):
                    if q % 2 == 0:
                        j = q // 2
                        act.wait_ge(raw_ld[j % 4], (e * 3 + (j // 4 + 1)) * 32)
                    act.activation(cut_part(wh, q), raw_part(q), ACT.Copy).then_inc(w_high, 1)

                def high_tokens(n):
                    for b in range(2):
                        act.wait_ge(x_T, n * 2 + (b + 1))
                        for i in range(2):
                            k = 4 * b + 2 * i
                            ins = act.activation(xsplit[:, k:k + 2, 0, :], ps[:, k // 2, 0:2 * CAP].rearrange("p (k t) -> p k t", k=2), ACT.Copy)
                        ins.then_inc(x_high, 1)

                def expert(e, last):
                    for q in range(SUBS):
                        act.wait_ge(w_used, e * SUBS + (q + 1))
                        if q < FT:
                            act.activation(low[:, q % 2, :, :], ps[:, 2 * (q % 2):2 * (q % 2) + 2, CAP:2 * CAP], ACT.Copy).then_inc(gu_low, 1)
                        if q + AHEAD < SUBS:
                            high_weights(e, q + AHEAD)
                        elif not last:
                            high_weights(e + 1, q + AHEAD - SUBS)
                        if q < FT:
                            act.wait_ge(gu_sum, e * FT + (q + 1 + GU_PAIRS))
                            act.activation(sg[:, q % 2, :], gu[:, q % 2, 0, :], ACT.Sigmoid).then_inc(gu_sig, 1)
                        if 2 <= q <= FT and q % 2 == 0:
                            act.wait_ge(h_done, e * FT + q)
                            act.activation(hsplit[:, q - 2:q, P:P + CAP], h[:, (q - 2) % 4:(q - 2) % 4 + 2, :], ACT.Copy).then_inc(h_high, 1)
                        if q == FT + 1 and not last:
                            high_tokens(e + 1)
                        if q in (FT + 3, FT + 7):
                            c = (q - FT) // 4
                            act.activation(ylow[:, c, :], ps[CAPS[1]:2 * CAPS[1], 5 + 2 * c, :], ACT.Copy).then_inc(y_low, 1)
                for q in range(AHEAD):
                    high_weights(0, q)
                high_tokens(0)
                with act.Fori(0, E - 1) as e:
                    expert(e, False)
                expert(E - 1, True)

            @block.vector
            def _(dve):
                dve.sem_inc(gu_sum, GU_PAIRS)

                def low_weights(e, q):
                    dve.wait_ge(w_high, e * SUBS + (q + 1))
                    dve.tensor_tensor(cut_part(wl, q), raw_part(q), cut_part(wh, q).bitcast(F32), ALU.subtract).then_inc(w_cut, 1)

                def low_tokens(n):
                    for b in range(2):
                        dve.wait_ge(x_high, n * 2 + (b + 1))
                        for i in range(2):
                            k = 4 * b + 2 * i
                            ins = dve.tensor_tensor(xsplit[:, k:k + 2, 1, :], ps[:, k // 2, 0:2 * CAP].rearrange("p (k t) -> p k t", k=2),
                                                    xsplit[:, k:k + 2, 0, :].bitcast(F32), ALU.subtract)
                        ins.then_inc(x_cut, 1)

                def expert(e, last):
                    for q in range(SUBS):
                        if q < FT:
                            pair = ps[:, 2 * (q % 2):2 * (q % 2) + 2, 0:CAP]
                            dve.wait_ge(gu_low, e * FT + (q + 1))
                            dve.tensor_tensor(gu[:, q % 2, :, :], pair, low[:, q % 2, :, :], ALU.add).then_inc(gu_sum, 1)
                        if q + AHEAD - 1 < SUBS:
                            low_weights(e, q + AHEAD - 1)
                        elif not last:
                            low_weights(e + 1, q + AHEAD - 1 - SUBS)
                        if q < FT:
                            dve.wait_ge(gu_sig, e * FT + (q + 1))
                            dve.tensor_tensor(sgg[:, q % 2, :], gu[:, q % 2, 0, :], sg[:, q % 2, :], ALU.mult).then_inc(gu_g, 1)
                            dve.wait_ge(gu_g, e * FT + (q + 1))
                            dve.tensor_tensor(h[:, q % 4, :], gu[:, q % 2, 1, :], sgg[:, q % 2, :], ALU.mult).then_inc(h_done, 1)
                        if 2 <= q <= FT and q % 2 == 0:
                            dve.wait_ge(h_high, e * 8 + q // 2)
                            two = (q - 2) % 4
                            for at_h, at_src, at_high, n in ((0, 0, P, CAPS[0]), (P + CAP, CAPS[0], 2 * P, CAPS[1])):
                                ins = dve.tensor_tensor(hsplit[:, q - 2:q, at_h:at_h + n], h[:, two:two + 2, at_src:at_src + n],
                                                        hsplit[:, q - 2:q, at_high:at_high + n].bitcast(F32), ALU.subtract)
                            ins.then_inc(h_cut, 1)
                        if q == FT + 1 and not last:
                            low_tokens(e + 1)
                        if q in (FT + 3, FT + 7):
                            c = (q - FT) // 4
                            cols = slice(c * CH, (c + 1) * CH)
                            dve.wait_ge(y_low, e * 2 + (c + 1))
                            if c == 0:
                                dve.wait_ge(sent, e + SENT)
                            dve.tensor_tensor(ysum[:, c, :], ps[0:CAPS[1], 5 + 2 * c, :], ylow[:, c, :], ALU.add).then_inc(y_sum, 1)
                            dve.tensor_scalar(ytok[0][:, cols], ps[:, 4 + 2 * c, :], gate[0][:, bass.ds(e, 1)], None, ALU.mult)
                            dve.wait_ge(y_sum, e * 2 + (c + 1))
                            dve.tensor_scalar(ytok[1][:, cols], ysum[:, c, :], gate[1][:, bass.ds(e, 1)], None, ALU.mult).then_inc(y_ev, 1)
                for q in range(AHEAD - 1):
                    low_weights(0, q)
                low_tokens(0)
                with dve.Fori(0, E - 1) as e:
                    expert(e, False)
                expert(E - 1, True)

        l_g, l_ld, l_st = sem("l_g"), sems("l_ld", NT), sem("l_st")
        l_ssq, l_var, l_std, l_rstd, l_y = (sem(n) for n in ("l_ssq", "l_var", "l_std", "l_rstd", "l_y"))

        with nc.Block() as block:
            @block.sync
            def _(sp):
                sp.dma_start(gF[:, :], final_g.rearrange("(o d) -> o d", o=1).partition_broadcast(P)).then_inc(l_g, 16)
                for t in range(NT):
                    sp.dma_start(fin[:, t, :], resid[t * P:(t + 1) * P, :]).then_inc(l_ld[t], 16)
                for t in range(NT):
                    sp.wait_ge(l_y, t + 1)
                    sp.dma_start(y[t * P:(t + 1) * P, :], fin[:, t, :]).then_inc(l_st, 16)
                sp.wait_ge(l_st, NT * 16)

            @block.scalar
            def _(act):
                def root(t):
                    act.wait_ge(l_var, t + 1)
                    act.activation(lstat[:, 2, t:t + 1], lstat[:, 1, t:t + 1], ACT.Sqrt).then_inc(l_std, 1)
                for t in range(NT):
                    act.wait_ge(l_ld[t], 16)
                    act.activation(fsquare[:, t % 2, :], fin[:, t, :], ACT.Square, accum_out=lstat[:, 0, t:t + 1]).then_inc(l_ssq, 1)
                    if t:
                        root(t - 1)
                root(NT - 1)

            @block.vector
            def _(dve):
                def rows(t):
                    dve.wait_ge(l_std, t + 1)
                    dve.reciprocal(lstat[:, 3, t:t + 1], lstat[:, 2, t:t + 1]).then_inc(l_rstd, 1)
                    dve.wait_ge(l_rstd, t + 1)
                    dve.scalar_tensor_tensor(out=fin[:, t, :], in0=fin[:, t, :], scalar=lstat[:, 3, t:t + 1], in1=gF[:, :],
                                             op0=ALU.mult, op1=ALU.mult).then_inc(l_y, 1)
                dve.wait_ge(l_g, 16)
                for t in range(NT):
                    dve.wait_ge(l_ssq, t + 1)
                    dve.tensor_scalar(lstat[:, 1, t:t + 1], lstat[:, 0, t:t + 1], 1.0 / D, EPS, ALU.mult, ALU.add).then_inc(l_var, 1)
                    if t:
                        rows(t - 1)
                rows(NT - 1)


_INS = ['rel_bias', 'norm1_g', 'w_in', 'w_attn_br', 'w_four_br', 'w_gate', 'b_gate', 'w_out', 'norm2_g', 'w_router',
        'w_exp_gate', 'w_exp_up', 'w_exp_down', 'final_g']


def kernel(**inputs):
    import numpy as _np
    import concourse.bacc as _bacc
    from concourse import mybir as _mybir
    from concourse.bass_utils import run_bass_kernel_spmd as _run

    nc = _bacc.Bacc("TRN2", target_bir_lowering=False, num_devices=1)
    arrays, args = {}, []

    def add(name, a):
        a = _np.ascontiguousarray(a)
        arrays[name] = a
        args.append(nc.dram_tensor(name, a.shape, _mybir.dt.from_np(a.dtype), kind="ExternalInput").ap())

    xp, xs = _np.asarray(inputs["x_prompt"]), _np.asarray(inputs["x_sample"])
    add("in_x_dram", _np.concatenate([xp.reshape(-1, D), xs.reshape(-1, D)], 0))
    for name in _INS:
        a = _np.asarray(inputs[name])
        add(f"in_{name}_dram", a.reshape(-1, P).T if name == "b_gate" else a)
    add("c_identity_dram", _np.eye(P, dtype=_np.float32))
    add("c_one_hot_dram", bucket_one_hot())
    add("c_pos_prompt_dram", position_table(SEQS[0][1]))
    add("c_pos_sample_dram", position_table(SEQS[1][1]))
    add("c_chan_dram", channel_table())
    out = nc.dram_tensor("out_y_dram", (TOKENS, D), _mybir.dt.float32, kind="ExternalOutput").ap()
    encoder(nc, *args, out)
    r = _run(nc, [arrays], core_ids=[0])
    got = r.results[0]["out_y_dram"]
    n = SEQS[0][1]
    return got[:n].reshape(xp.shape), got[n:].reshape(xs.shape)
```
